# Optimizing a Trainium2 kernel written in Bass

```python
import jax, jax.numpy as jnp
from jax import lax
import numpy as np

D_MODEL = 1024
BATCH = 1
SEQ = 1024
DEPTH = 2

CHUNK = 64
Q_BLOCK = 128
N_MIXERS = 3
EXPAND = 2
D_INNER = EXPAND * D_MODEL
N_HEADS = 16
HEAD_DIM = D_INNER // N_HEADS
MLA_Q_RANK = 256
MLA_KV_RANK = 128
MLA_NOPE_DIM = 128
MLA_ROPE_DIM = 64
MLA_V_DIM = D_INNER // N_HEADS
ROPE_BASE = 10000.0
FORGET_BIAS = 3.0
EPS = 1e-6
NEG = -1e30

kernel_name = 'hybrid_stickbreak_mla_forgetting_trunk'

def rmsnorm(x, g):
    x32 = x.astype(jnp.float32)
    y = x32 * lax.rsqrt(jnp.mean(x32 * x32, axis=-1, keepdims=True) + EPS)
    return (y * g.astype(jnp.float32)).astype(x.dtype)

def split_heads(t, n_heads):
    b, s, _ = t.shape
    return t.reshape(b, s, n_heads, -1).transpose(0, 2, 1, 3)

def merge_heads(t):
    b, h, s, d = t.shape
    return t.transpose(0, 2, 1, 3).reshape(b, s, h * d)

def sweep_query_blocks(block_fn, seq):
    outs = [block_fn(start, start + Q_BLOCK) for start in range(0, seq, Q_BLOCK)]
    return jnp.concatenate(outs, axis=2)

def rope(x, positions):
    r = x.shape[-1]
    inv_freq = ROPE_BASE ** (-jnp.arange(0, r, 2, dtype=jnp.float32) / r)
    ang = positions.astype(jnp.float32)[:, :, None, None] * inv_freq
    cos, sin = jnp.cos(ang), jnp.sin(ang)
    x32 = x.astype(jnp.float32)
    x1, x2 = x32[..., : r // 2], x32[..., r // 2:]
    return jnp.concatenate([x1 * cos - x2 * sin, x1 * sin + x2 * cos], axis=-1).astype(x.dtype)

def stick_breaking_mixer(h, w_in, w_out):
    b, s, _ = h.shape
    q, k, v, gate = jnp.split(h @ w_in, 4, axis=-1)
    q, k, v = split_heads(q, N_HEADS), split_heads(k, N_HEADS), split_heads(v, N_HEADS)
    scale = HEAD_DIM ** -0.5

    def block(start, end):
        z = jnp.einsum('bhqd,bhkd->bhqk', q[:, :, start:end], k[:, :, :end],
                       preferred_element_type=jnp.float32) * scale
        strict = jnp.arange(end)[None, :] < jnp.arange(start, end)[:, None]
        log_skip = jnp.where(strict, jax.nn.log_sigmoid(-z), 0.0)
        later = lax.cumsum(log_skip, axis=3, reverse=True) - log_skip
        w = jnp.where(strict, jnp.exp(jax.nn.log_sigmoid(z) + later), 0.0)
        return jnp.einsum('bhqk,bhkd->bhqd', w.astype(v.dtype), v[:, :, :end])

    o = merge_heads(sweep_query_blocks(block, s))
    return (o * jax.nn.silu(gate)) @ w_out

def mla_mixer(h, positions, w_in, q_norm, w_qb, kv_norm, w_kvb, w_out):
    b, s, _ = h.shape
    i1 = MLA_Q_RANK
    i2 = i1 + MLA_KV_RANK
    i3 = i2 + MLA_ROPE_DIM
    proj = h @ w_in
    q_lat, kv_lat, k_rope, gate = proj[..., :i1], proj[..., i1:i2], proj[..., i2:i3], proj[..., i3:]
    q = (rmsnorm(q_lat, q_norm) @ w_qb).reshape(b, s, N_HEADS, MLA_NOPE_DIM + MLA_ROPE_DIM)
    q_nope = q[..., :MLA_NOPE_DIM].transpose(0, 2, 1, 3)
    q_rope = rope(q[..., MLA_NOPE_DIM:], positions).transpose(0, 2, 1, 3)
    kv = (rmsnorm(kv_lat, kv_norm) @ w_kvb).reshape(b, s, N_HEADS, MLA_NOPE_DIM + MLA_V_DIM)
    k_nope = kv[..., :MLA_NOPE_DIM].transpose(0, 2, 1, 3)
    v = kv[..., MLA_NOPE_DIM:].transpose(0, 2, 1, 3)
    k_rope = rope(k_rope[:, :, None, :], positions)[:, :, 0, :]
    scale = (MLA_NOPE_DIM + MLA_ROPE_DIM) ** -0.5

    def block(start, end):
        z = (jnp.einsum('bhqd,bhkd->bhqk', q_nope[:, :, start:end], k_nope[:, :, :end],
                        preferred_element_type=jnp.float32)
             + jnp.einsum('bhqr,bkr->bhqk', q_rope[:, :, start:end], k_rope[:, :end],
                          preferred_element_type=jnp.float32)) * scale
        allowed = (jnp.arange(end)[None, :] // CHUNK) <= (jnp.arange(start, end)[:, None] // CHUNK)
        p = jax.nn.softmax(jnp.where(allowed, z, NEG), axis=-1)
        return jnp.einsum('bhqk,bhkd->bhqd', p.astype(v.dtype), v[:, :, :end])

    o = merge_heads(sweep_query_blocks(block, s))
    return (o * jax.nn.silu(gate)) @ w_out

def forgetting_mixer(h, w_in, b_f, w_out):
    b, s, _ = h.shape
    proj = h @ w_in
    q = split_heads(proj[..., :D_INNER], N_HEADS)
    k = split_heads(proj[..., D_INNER:2 * D_INNER], N_HEADS)
    v = split_heads(proj[..., 2 * D_INNER:3 * D_INNER], N_HEADS)
    gate = proj[..., 3 * D_INNER:4 * D_INNER]
    f_logit = proj[..., 4 * D_INNER:].astype(jnp.float32) + b_f.astype(jnp.float32)
    cum_log_f = lax.cumsum(jax.nn.log_sigmoid(f_logit), axis=1).transpose(0, 2, 1)
    scale = HEAD_DIM ** -0.5

    def block(start, end):
        z = jnp.einsum('bhqd,bhkd->bhqk', q[:, :, start:end], k[:, :, :end],
                       preferred_element_type=jnp.float32) * scale
        z = z + cum_log_f[:, :, start:end, None] - cum_log_f[:, :, None, :end]
        causal = jnp.arange(end)[None, :] <= jnp.arange(start, end)[:, None]
        p = jax.nn.softmax(jnp.where(causal, z, NEG), axis=-1)
        return jnp.einsum('bhqk,bhkd->bhqd', p.astype(v.dtype), v[:, :, :end])

    o = merge_heads(sweep_query_blocks(block, s))
    return (o * jax.nn.silu(gate)) @ w_out

def setup_inputs(seed: int = 0) -> dict:
    key = jax.random.key(seed)
    ks = iter(jax.random.split(key, 32))

    def w(shape):
        return jax.random.normal(next(ks), shape, jnp.float32) * shape[0] ** -0.5

    def gain(n):
        return 1.0 + 0.02 * jax.random.normal(next(ks), (n,), jnp.float32)

    x = jax.random.normal(next(ks), (BATCH, SEQ, D_MODEL), jnp.float32)
    offsets = jax.random.randint(next(ks), (BATCH,), 0, 64) * CHUNK
    positions = (offsets[:, None] + jnp.arange(SEQ)[None, :]).astype(jnp.int32)
    mla_in = MLA_Q_RANK + MLA_KV_RANK + MLA_ROPE_DIM + D_INNER
    return {
        'x': x,
        'positions': positions,
        'ln0': gain(D_MODEL),
        'w_in0': w((D_MODEL, 4 * D_INNER)),
        'w_out0': w((D_INNER, D_MODEL)),
        'ln1': gain(D_MODEL),
        'w_in1': w((D_MODEL, mla_in)),
        'q_norm1': gain(MLA_Q_RANK),
        'w_qb1': w((MLA_Q_RANK, N_HEADS * (MLA_NOPE_DIM + MLA_ROPE_DIM))),
        'kv_norm1': gain(MLA_KV_RANK),
        'w_kvb1': w((MLA_KV_RANK, N_HEADS * (MLA_NOPE_DIM + MLA_V_DIM))),
        'w_out1': w((D_INNER, D_MODEL)),
        'ln2': gain(D_MODEL),
        'w_in2': w((D_MODEL, 4 * D_INNER + N_HEADS)),
        'b_f2': FORGET_BIAS + 0.1 * jax.random.normal(next(ks), (N_HEADS,), jnp.float32),
        'w_out2': w((D_INNER, D_MODEL)),
        'ln3': gain(D_MODEL),
        'w_in3': w((D_MODEL, 4 * D_INNER)),
        'w_out3': w((D_INNER, D_MODEL)),
        'final_norm': gain(D_MODEL),
    }

def reference(x, positions, ln0, w_in0, w_out0, ln1, w_in1, q_norm1, w_qb1, kv_norm1, w_kvb1,
              w_out1, ln2, w_in2, b_f2, w_out2, ln3, w_in3, w_out3, final_norm):
    layer_params = [
        (ln0, (w_in0, w_out0)),
        (ln1, (w_in1, q_norm1, w_qb1, kv_norm1, w_kvb1, w_out1)),
        (ln2, (w_in2, b_f2, w_out2)),
        (ln3, (w_in3, w_out3)),
    ]
    for i in range(DEPTH):
        ln, p = layer_params[i]
        h = rmsnorm(x, ln)
        kind = i % N_MIXERS
        if kind == 0:
            y = stick_breaking_mixer(h, *p)
        elif kind == 1:
            y = mla_mixer(h, positions, *p)
        else:
            y = forgetting_mixer(h, *p)
        x = x + y
    return rmsnorm(x, final_norm)


_drawn_inputs = setup_inputs


def setup_inputs(seed=0):
    import zlib

    import numpy as np

    out = dict(_drawn_inputs(seed))
    spreads = {}
    factors = {'ln0': 4.897, 'ln1': 8.0, 'q_norm1': 8.0, 'kv_norm1': 8.0, 'final_norm': 2.836}
    for name, (base, spread) in spreads.items():
        noise = np.random.default_rng([zlib.crc32(name.encode()), seed]).standard_normal(out[name].shape)
        drawn = base * np.exp(spread * noise) if base else spread * noise
        out[name] = __import__('jax').numpy.asarray(drawn.astype(out[name].dtype))
    for name, factor in factors.items():
        out[name] = (out[name] * factor).astype(out[name].dtype)
    return out
```

```python
from contextlib import ExitStack

import concourse.bass as bass
from concourse import mybir

F32 = mybir.dt.float32
F32R = mybir.dt.float32r
I32 = mybir.dt.int32
ALU = mybir.AluOpType
ACT = mybir.ActivationFunctionType
AX_X = mybir.AxisListType.X

P = 128
BANK = 512
D = 1024
TOK = 1024
KT = D // P
TT = TOK // P
HEADS = 16
HD = 128
D_INNER = HEADS * HD
HALVES = TOK // BANK
QG = BANK // P
CHUNK = 64
Q_RANK, KV_RANK, ROPE = 256, 128, 64
QKT = Q_RANK // P
HALF_ROPE = ROPE // 2
LAT = Q_RANK + KV_RANK + ROPE
NOPE = 128
EPS = 1e-6
NEG = -1e30
STICK_SCALE = HD ** -0.5
MLA_SCALE = (NOPE + ROPE) ** -0.5


def at_least(eng, sem, value):
    if isinstance(value, int) and value <= 0:
        return
    eng.wait_ge(sem, value)


def settled(eng, value):
    return value if isinstance(value, int) else eng.snap(value)


def products(w_hi, w_lo, x_hi, x_lo):
    return ((w_lo, x_hi), (w_hi, x_lo), (w_hi, x_hi))


class Chip:

    def __init__(self, nc, ctx, tag):
        self.nc, self.ctx, self.tag = nc, ctx, tag

    def sb(self, name, shape, dt=F32):
        return self.ctx.enter_context(self.nc.sbuf_tensor(f"{self.tag}_{name}", shape, dt))

    def psum(self, name, shape):
        return self.ctx.enter_context(self.nc.psum_tensor(f"{self.tag}_{name}", shape, F32))

    def sem(self, name):
        return self.ctx.enter_context(self.nc.semaphore(f"{self.tag}_{name}"))


def build_constants(nc, c, outer):
    ident = outer.sb("ident", [P, P])
    ident_r = outer.sb("ident_r", [P, P], F32R)
    strict_r = outer.sb("strict_r", [P, P], F32R)
    chunk_r = outer.sb("chunk_r", [P, P], F32R)
    strict = c.sb("strict", [P, P])
    chunk = c.sb("chunk", [P, P])
    cleared, made, cast = c.sem("cleared"), c.sem("made"), c.sem("cast")
    with nc.Block() as block:

        @block.gpsimd
        def _(pool):
            pool.memset(ident[:], 0.0).then_inc(cleared, 1)
            pool.memset(strict[:], 0.0).then_inc(cleared, 1)
            pool.memset(chunk[:], 0.0).then_inc(cleared, 1)
            pool.wait_ge(cleared, 3)
            pool.affine_select(out=ident[:], in_=ident[:], compare_op=ALU.not_equal, fill=1.0,
                               base=0, pattern=[[-1, P]], channel_multiplier=1).then_inc(made, 1)
            pool.affine_select(out=strict[:], in_=strict[:], compare_op=ALU.is_gt, fill=NEG,
                               base=0, pattern=[[-1, P]], channel_multiplier=1).then_inc(made, 1)
            pool.memset(chunk[0:CHUNK, CHUNK:P], NEG).then_inc(made, 1)

        @block.vector
        def _(dve):
            dve.wait_ge(made, 3)
            dve.tensor_copy(ident_r[:], ident[:]).then_inc(cast, 1)
            dve.tensor_copy(strict_r[:], strict[:]).then_inc(cast, 1)
            dve.tensor_copy(chunk_r[:], chunk[:]).then_inc(cast, 1)
            dve.wait_ge(cast, 3)
    return ident, ident_r, strict_r, chunk_r


def rstd_steps(dve, chain, sq_sum, width, var, rstd, tmp, var_done, root_done, root_value):
    dve.tensor_scalar(var, sq_sum, 1.0 / width, EPS, ALU.mult, ALU.add).then_inc(var_done, 1)
    dve.wait_ge(root_done, root_value)
    chain(dve.reciprocal(rstd, rstd))
    chain(dve.tensor_tensor(tmp, rstd, rstd, ALU.mult))
    chain(dve.tensor_tensor(tmp, tmp, var, ALU.mult))
    chain(dve.tensor_scalar(tmp, tmp, -0.5, 1.5, ALU.mult, ALU.add))
    chain(dve.tensor_tensor(rstd, rstd, tmp, ALU.mult))


def build_norm(nc, c, x_sb, x_dram, gain_dram, ident, hT_hi, hT_lo):
    gain = c.sb("gain", [P, KT])
    junk = c.sb("junk", [P, D])
    sq_sum, var, rstd, tmp = (c.sb(n, [P, TT]) for n in ("sq_sum", "var", "rstd", "tmp"))
    banks = c.psum("banks", [P, 4, BANK])
    x_in = [c.sem(f"x_in{t}") for t in range(TT)]
    gain_in, squared, var_done, root_done, linked, scaled, turned, hi_done, lo_done = (
        c.sem(n) for n in ("gain_in", "squared", "var_done", "root_done", "linked", "scaled",
                           "turned", "hi_done", "lo_done"))
    groups = [(half, kt) for half in range(HALVES) for kt in range(KT)]
    with nc.Block() as block:

        @block.sync
        def _(sp):
            if x_dram is not None:
                for t in range(TT):
                    sp.dma_start(x_sb[:, t, :], x_dram[t * P:(t + 1) * P, :]).then_inc(x_in[t], 16)
            sp.dma_start(gain[:], gain_dram.rearrange("(k p) -> p k", p=P),
                         allow_slow_non_contiguous=True).then_inc(gain_in, 16)

        @block.scalar
        def _(act):
            for half in range(HALVES):
                for t in range(half * QG, (half + 1) * QG):
                    if x_dram is not None:
                        act.wait_ge(x_in[t], 16)
                    if t:
                        act.wait_ge(squared, t)
                    act.activation(junk[:], x_sb[:, t, :], ACT.Square,
                                   accum_out=sq_sum[:, t:t + 1]).then_inc(squared, 1)
                act.wait_ge(var_done, half + 1)
                act.activation(rstd[:, half * QG:(half + 1) * QG], var[:, half * QG:(half + 1) * QG],
                               ACT.Sqrt).then_inc(root_done, 1)
            act.wait_ge(gain_in, 16)
            for n, (half, kt) in enumerate(groups):
                act.wait_ge(turned, n + 1)
                act.activation(hT_hi[:, kt, half * BANK:(half + 1) * BANK], banks[:, n % 4, :],
                               ACT.Copy, scale=gain[:, kt:kt + 1]).then_inc(hi_done, 1)

        @block.vector
        def _(dve):
            count = [0]

            def chain(ins):
                count[0] += 1
                ins.then_inc(linked, 1)
                dve.wait_ge(linked, count[0])

            for half in range(HALVES):
                cols = slice(half * QG, (half + 1) * QG)
                dve.wait_ge(squared, (half + 1) * QG)
                rstd_steps(dve, chain, sq_sum[:, cols], D, var[:, cols], rstd[:, cols],
                           tmp[:, cols], var_done, root_done, half + 1)
                for t in range(half * QG, (half + 1) * QG):
                    dve.tensor_scalar(x_sb[:, t, :], x_sb[:, t, :], rstd[:, t:t + 1], None,
                                      ALU.mult).then_inc(scaled, 1)
            dve.wait_ge(gain_in, 16)
            for n, (half, kt) in enumerate(groups):
                dve.wait_ge(hi_done, n + 1)
                cols = slice(half * BANK, (half + 1) * BANK)
                dve.scalar_tensor_tensor(hT_lo[:, kt, cols], banks[:, n % 4, :], gain[:, kt:kt + 1],
                                         hT_hi[:, kt, cols].bitcast(F32), ALU.mult,
                                         ALU.subtract).then_inc(lo_done, 1)
            dve.wait_ge(lo_done, len(groups))

        @block.tensor
        def _(pe):
            for n, (half, kt) in enumerate(groups):
                if kt == 0:
                    pe.wait_ge(scaled, (half + 1) * QG)
                at_least(pe, lo_done, n - 3)
                for q in range(QG):
                    mm = pe.transpose(banks[:, n % 4, q * P:(q + 1) * P],
                                      x_sb[:, half * QG + q, kt * P:(kt + 1) * P], ident[:])
                mm.then_inc(turned, 1)


def build_stick_heads(nc, c, w_in, ident, ident_r, strict_r, hT_hi, hT_lo, og_dram):
    GATE, VAL, KEY, QRY = range(4)
    FIRST_COL = {GATE: 3 * D_INNER, VAL: 2 * D_INNER, KEY: D_INNER, QRY: 0}
    UNITS = 4
    PROJ = UNITS * HALVES
    HI_EVACS = 6

    w_raw = c.sb("w_raw", [P, 2, KT, P])
    w_hi = c.sb("w_hi", [P, 2, KT, P], F32R)
    w_lo = c.sb("w_lo", [P, 2, KT, P], F32R)
    q_hi, q_lo = c.sb("q_hi", [P, TOK], F32R), c.sb("q_lo", [P, TOK], F32R)
    k_hi, k_lo = c.sb("k_hi", [P, 2 * TOK], F32R), c.sb("k_lo", [P, 2 * TOK], F32R)
    v_cols = c.sb("v_cols", [P, TOK])
    v_hi, v_lo = c.sb("v_hi", [P, TT, HD], F32R), c.sb("v_lo", [P, TT, HD], F32R)
    gate = c.sb("gate", [P, 2 * TOK])
    skip = c.sb("skip", [P, 2, TOK])
    take = c.sb("take", [P, 2, TOK])
    wT_hi = c.sb("wT_hi", [P, TT, BANK], F32R)
    wT_lo = c.sb("wT_lo", [P, TT, BANK], F32R)
    og = c.sb("og", [P, HALVES, BANK])
    zero = c.sb("zero", [P, 1])

    pj = c.psum("pj", [P, 2, BANK])
    z = c.psum("z", [P, TOK])
    wT = c.psum("wT", [P, TT, P])
    vT = c.psum("vT", [P, QG, P])
    pv = c.psum("pv", [P, BANK])

    w_in_s = [c.sem(f"w_in{s}") for s in range(2)]
    og_out = [c.sem(f"og_out{s}") for s in range(HALVES)]
    (w_split, proj_done, proj_hi, proj_free, z_done, skip_done, take_done, scan_done, w_done,
     wT_done, wT_hi_done, wT_lo_done, vT_done, vT_hi_done, vT_lo_done, pv_done, og_done,
     zeroed) = (c.sem(n) for n in (
         "w_split", "proj_done", "proj_hi", "proj_free", "z_done", "skip_done", "take_done",
         "scan_done", "w_done", "wT_done", "wT_hi_done", "wT_lo_done", "vT_done", "vT_hi_done",
         "vT_lo_done", "pv_done", "og_done", "zeroed"))

    w_units = w_in.rearrange("(k p) (u h n) -> h u p k n", p=P, u=UNITS, n=HD)

    def half_cols(half):
        return slice(half * BANK, (half + 1) * BANK)

    def iterations(eng, step):
        step(-1, False, True)
        step(0, True, True)
        with eng.Fori(1, HEADS - 1) as i:
            step(i, True, True)
        step(HEADS - 1, True, False)

    with nc.Block() as block:

        @block.sync
        def _(sp):
            def load(j):
                for u in range(UNITS):
                    n = UNITS * j + u
                    if u != QRY:
                        at_least(sp, w_split, 2 * (n - 1 + (u == KEY)))
                    src = w_units[bass.ds(j, 1), FIRST_COL[u] // D_INNER, :, :, :]
                    sp.dma_start(w_raw[:, u % 2, :, :], src.rearrange("h p k n -> (h p) k n"))\
                        .then_inc(w_in_s[u % 2], 16)

            def store(i, group):
                i = settled(sp, i)
                sp.wait_ge(og_done, HALVES * i + group + 1)
                dst = og_dram[bass.ds(i, 1), :, half_cols(group)].rearrange("h p n -> (h p) n")
                sp.dma_start(dst, og[:, group, :]).then_inc(og_out[group], 16)

            load(0)
            load(1)
            store(0, 0)
            with sp.Fori(2, HEADS) as j:
                load(j)
                store(j - 2, 1)
                store(j - 1, 0)
            store(HEADS - 2, 1)
            store(HEADS - 1, 0)
            store(HEADS - 1, 1)
            for group in range(HALVES):
                sp.wait_ge(og_out[group], 16 * HEADS)

        @block.gpsimd
        def _(pool):
            def split(j):
                for u in range(UNITS):
                    n = UNITS * j + u
                    pool.wait_ge(w_in_s[u % 2], 16 * (2 * j + u // 2 + 1))
                    at_least(pool, proj_done, HALVES * (n - 1))
                    raw = w_raw[:, u % 2, :, :]
                    pool.tensor_tensor(w_hi[:, u % 2, :, :], raw,
                                       zero[:].unsqueeze(2).broadcast_to([P, KT, P]),
                                       ALU.add).then_inc(w_split, 1)
                    pool.wait_ge(w_split, 2 * n + 1)
                    pool.tensor_tensor(w_lo[:, u % 2, :, :], w_raw[:, u % 2, :, :],
                                       w_hi[:, u % 2, :, :].bitcast(F32),
                                       ALU.subtract).then_inc(w_split, 1)

            pool.wait_ge(zeroed, 1)
            split(0)
            with pool.Fori(1, HEADS) as j:
                split(j)

        @block.tensor
        def _(pe):
            def project(j, v):
                m = PROJ * j + v
                u, half = v // HALVES, v % HALVES
                at_least(pe, w_split, 2 * (UNITS * j + u + 1))
                at_least(pe, proj_free, m - 1)
                for kt in range(KT):
                    for n, (w, h) in enumerate(products(w_hi, w_lo, hT_hi, hT_lo)):
                        mm = pe.matmul(pj[:, v % 2, :], w[:, u % 2, kt, :],
                                       h[:, kt, half_cols(half)], start=(kt == 0 and n == 0),
                                       stop=(kt == KT - 1 and n == 2))
                mm.then_inc(proj_done, 1)

            def scores(i, s):
                at_least(pe, proj_free, PROJ * (i + 1) if s >= QG else PROJ * (i + 1) - 1)
                at_least(pe, take_done, TT * i + s)
                n_keys = (s + 1) * P
                queries = slice(s * P, (s + 1) * P)
                for c0 in range(0, n_keys, BANK):
                    width = min(BANK, n_keys - c0)
                    last = c0 + width == n_keys
                    for n, (q, k) in enumerate(products(q_hi, q_lo, k_hi, k_lo)):
                        mm = pe.matmul(z[:, c0:c0 + width], q[:, queries],
                                       k[:, bass.ds((i % 2) * TOK + c0, width)],
                                       start=(n == 0), stop=(n == 2 and not last))
                    if last:
                        mm = pe.matmul(z[:, s * P:(s + 1) * P], ident_r[:], strict_r[:],
                                       start=False, stop=True)
                mm.then_inc(z_done, 1)

            def turn_weights(i, s):
                pe.wait_ge(w_done, TT * i + s + 1)
                at_least(pe, wT_lo_done, TT * i + s)
                for kb in range(s + 1):
                    mm = pe.transpose(wT[:, kb, :], take[:, s % 2, kb * P:(kb + 1) * P], ident[:])
                mm.then_inc(wT_done, 1)

            def turn_values(i, half):
                pe.wait_ge(proj_free, PROJ * i + HALVES * VAL + half + 1)
                at_least(pe, vT_lo_done, HALVES * i + half)
                for b in range(QG):
                    t = half * QG + b
                    mm = pe.transpose(vT[:, b, :], v_cols[:, t * P:(t + 1) * P], ident[:])
                mm.then_inc(vT_done, 1)

            def mix(i, group):
                pe.wait_ge(wT_lo_done, TT * i + QG * (group + 1))
                pe.wait_ge(vT_lo_done, HALVES * i + group + 1)
                at_least(pe, og_done, HALVES * i + group)
                blocks = QG * (group + 1)
                for kb in range(blocks):
                    q0 = max(kb - QG * group, 0) * P
                    for n, (v, w) in enumerate(products(v_hi, v_lo, wT_hi, wT_lo)):
                        mm = pe.matmul(pv[:, q0:BANK], v[:, kb, :], w[:, kb, q0:BANK],
                                       start=(kb == 0 and n == 0),
                                       stop=(kb == blocks - 1 and n == 2))
                mm.then_inc(pv_done, 1)

            def step(i, attend, proj):
                if attend:
                    scores(i, 0)
                for s in range(TT):
                    if proj:
                        project(i + 1, s)
                    if not attend:
                        continue
                    if s == 0 and not (isinstance(i, int) and i == 0):
                        mix(i - 1, 1)
                    if s == QG:
                        mix(i, 0)
                    if s < HALVES:
                        turn_values(i, s)
                    turn_weights(i, s)
                    if s + 1 < TT:
                        scores(i, s + 1)

            iterations(pe, step)
            mix(HEADS - 1, 1)

        @block.scalar
        def _(act):
            def project_hi(j, v):
                u, half = v // HALVES, v % HALVES
                if u == VAL:
                    return
                act.wait_ge(proj_done, PROJ * j + v + 1)
                bank = pj[:, v % 2, :]
                if u == GATE:
                    at_least(act, og_done, HALVES * (j - 2) + half + 1)
                    act.activation(gate[:, bass.ds((j % 2) * TOK + half * BANK, BANK)], bank,
                                   ACT.Sigmoid).then_inc(proj_hi, 1)
                elif u == KEY:
                    act.activation(k_hi[:, bass.ds((j % 2) * TOK + half * BANK, BANK)], bank,
                                   ACT.Copy).then_inc(proj_hi, 1)
                else:
                    act.activation(q_hi[:, half_cols(half)], bank, ACT.Copy,
                                   scale=STICK_SCALE).then_inc(proj_hi, 1)

            def sigmoids(i, s):
                n_keys = (s + 1) * P
                act.wait_ge(z_done, TT * i + s + 1)
                at_least(act, wT_done, TT * i + s - 1)
                act.activation(skip[:, s % 2, 0:n_keys], z[:, 0:n_keys], ACT.Sigmoid,
                               scale=-1.0).then_inc(skip_done, 1)
                act.activation(take[:, s % 2, 0:n_keys], z[:, 0:n_keys],
                               ACT.Sigmoid).then_inc(take_done, 1)

            def values_hi(i, half):
                act.wait_ge(vT_done, HALVES * i + half + 1)
                act.activation(v_hi[:, half * QG:(half + 1) * QG, :], vT[:],
                               ACT.Copy).then_inc(vT_hi_done, 1)

            def weights_hi(i, s):
                act.wait_ge(wT_done, TT * i + s + 1)
                q0 = (s % QG) * P
                act.activation(wT_hi[:, 0:s + 1, q0:q0 + P], wT[:, 0:s + 1, :],
                               ACT.Copy).then_inc(wT_hi_done, 1)

            def step(i, attend, proj):
                if attend:
                    sigmoids(i, 0)
                for s in range(TT):
                    if proj:
                        project_hi(i + 1, s)
                    if not attend:
                        continue
                    if s < HALVES:
                        values_hi(i, s)
                    weights_hi(i, s)
                    if s + 1 < TT:
                        sigmoids(i, s + 1)

            iterations(act, step)

        @block.vector
        def _(dve):
            def project_lo(j, v):
                u, half = v // HALVES, v % HALVES
                bank = pj[:, v % 2, :]
                if u == VAL:
                    dve.wait_ge(proj_done, PROJ * j + v + 1)
                    dve.tensor_copy(v_cols[:, half_cols(half)], bank).then_inc(proj_free, 1)
                    return
                order = v if u == GATE else v - HALVES
                dve.wait_ge(proj_hi, HI_EVACS * j + order + 1)
                if u == GATE:
                    cols = bass.ds((j % 2) * TOK + half * BANK, BANK)
                    dve.tensor_tensor(gate[:, cols], bank, gate[:, cols],
                                      ALU.mult).then_inc(proj_free, 1)
                elif u == KEY:
                    cols = bass.ds((j % 2) * TOK + half * BANK, BANK)
                    dve.tensor_tensor(k_lo[:, cols], bank, k_hi[:, cols].bitcast(F32),
                                      ALU.subtract).then_inc(proj_free, 1)
                else:
                    cols = half_cols(half)
                    dve.scalar_tensor_tensor(q_lo[:, cols], bank, STICK_SCALE,
                                             q_hi[:, cols].bitcast(F32), ALU.mult,
                                             ALU.subtract).then_inc(proj_free, 1)

            def weights(i, s):
                n_keys = (s + 1) * P
                dve.wait_ge(skip_done, TT * i + s + 1)
                from_last = skip[:, s % 2, 0:n_keys][:, ::-1]
                dve.tensor_tensor_scan(from_last, from_last, zero[:].broadcast_to([P, n_keys]),
                                       1.0, ALU.mult, ALU.add).then_inc(scan_done, 1)
                dve.wait_ge(scan_done, TT * i + s + 1)
                dve.wait_ge(take_done, TT * i + s + 1)
                dve.tensor_tensor(take[:, s % 2, 0:n_keys - 1], take[:, s % 2, 0:n_keys - 1],
                                  skip[:, s % 2, 1:n_keys], ALU.mult).then_inc(w_done, 1)

            def values_lo(i, half):
                tiles = slice(half * QG, (half + 1) * QG)
                dve.wait_ge(vT_hi_done, HALVES * i + half + 1)
                dve.tensor_tensor(v_lo[:, tiles, :], vT[:], v_hi[:, tiles, :].bitcast(F32),
                                  ALU.subtract).then_inc(vT_lo_done, 1)

            def weights_lo(i, s):
                q0 = (s % QG) * P
                dve.wait_ge(wT_hi_done, TT * i + s + 1)
                dve.tensor_tensor(wT_lo[:, 0:s + 1, q0:q0 + P], wT[:, 0:s + 1, :],
                                  wT_hi[:, 0:s + 1, q0:q0 + P].bitcast(F32),
                                  ALU.subtract).then_inc(wT_lo_done, 1)

            def gated(i, group):
                dve.wait_ge(pv_done, HALVES * i + group + 1)
                at_least(dve, og_out[group], 16 * i)
                dve.tensor_tensor(og[:, group, :], pv[:],
                                  gate[:, bass.ds((i % 2) * TOK + group * BANK, BANK)],
                                  ALU.mult).then_inc(og_done, 1)

            def step(i, attend, proj):
                if attend:
                    weights(i, 0)
                for s in range(TT):
                    if proj:
                        project_lo(i + 1, s)
                    if not attend:
                        continue
                    if s == 0 and not (isinstance(i, int) and i == 0):
                        gated(i - 1, 1)
                    if s == QG:
                        gated(i, 0)
                    if s < HALVES:
                        values_lo(i, s)
                    weights_lo(i, s)
                    if s + 1 < TT:
                        weights(i, s + 1)

            dve.memset(zero[:], 0.0).then_inc(zeroed, 1)
            dve.wait_ge(zeroed, 1)
            iterations(dve, step)
            gated(HEADS - 1, 1)


def build_out(nc, c, w_out, og_dram, x_dram, x_sb, x_save, final_gain, out_dram):
    w_raw = c.sb("w_raw", [P, 2, D])
    w_hi, w_lo = c.sb("w_hi", [P, 2, D], F32R), c.sb("w_lo", [P, 2, D], F32R)
    og_raw = c.sb("og_raw", [P, 2, BANK])
    og_hi, og_lo = c.sb("og_hi", [P, 2, BANK], F32R), c.sb("og_lo", [P, 2, BANK], F32R)
    y = c.psum("y", [P, QG, 2, BANK])
    raw_in = [c.sem(f"raw_in{s}") for s in range(2)]
    x_in, hi_done, og_lo_done, w_lo_done, mm_done, added, saved = (
        c.sem(n) for n in ("x_in", "hi_done", "og_lo_done", "w_lo_done", "mm_done", "added",
                           "saved"))
    final = final_gain is not None
    if final:
        gain = c.sb("gain", [P, D])
        junk = c.sb("junk", [P, D])
        sq_sum, var, rstd, tmp = (c.sb(n, [P, TT]) for n in ("sq_sum", "var", "rstd", "tmp"))
        gain_in, squared, var_done, root_done, linked = (
            c.sem(n) for n in ("gain_in", "squared", "var_done", "root_done", "linked"))
    normed = c.sem("normed")

    def pairs(eng, half, work):
        for k in range(2):
            work(half * HEADS + k, k, k == 0, False)
        with eng.Fori(1, HEADS // 2 - 1) as pair:
            for k in range(2):
                work(pair * 2 + (half * HEADS + k), k, False, False)
        for k in range(2):
            work(half * HEADS + HEADS - 2 + k, k, False, k == 1)

    with nc.Block() as block:

        @block.sync
        def _(sp):
            def load(half):
                def work(n, slot, first, last):
                    h = settled(sp, n - half * HEADS)
                    at_least(sp, og_lo_done, n - 1)
                    at_least(sp, w_lo_done, n - 1)
                    sp.dma_start(og_raw[:, slot, :],
                                 og_dram[bass.ds(h, 1), :, half * BANK:(half + 1) * BANK]
                                 .rearrange("h p n -> (h p) n")).then_inc(raw_in[slot], 16)
                    sp.dma_start(w_raw[:, slot, :],
                                 w_out[bass.ds(h * HD, HD), :]).then_inc(raw_in[slot], 16)
                return work

            for half in range(HALVES):
                pairs(sp, half, load(half))

        @block.gpsimd
        def _(pool):
            def work(n, slot, first, last):
                pool.wait_ge(hi_done, 2 * n + 2)
                at_least(pool, mm_done, n - 1)
                pool.tensor_tensor(w_lo[:, slot, :], w_raw[:, slot, :],
                                   w_hi[:, slot, :].bitcast(F32), ALU.subtract).then_inc(w_lo_done, 1)

            for t in range(TT):
                pool.dma_start(x_sb[:, t, :], x_dram[t * P:(t + 1) * P, :]).then_inc(x_in, 16)
            if final:
                pool.dma_start(gain[:], final_gain.rearrange("(a n) -> a n", a=1)
                               .broadcast_to([P, D])).then_inc(gain_in, 16)
            for half in range(HALVES):
                pairs(pool, half, work)

        @block.scalar
        def _(act):
            def work(n, slot, first, last):
                act.wait_ge(raw_in[slot], n * 16 + (32 - slot * 16))
                at_least(act, mm_done, n - 1)
                act.activation(og_hi[:, slot, :], og_raw[:, slot, :], ACT.Copy).then_inc(hi_done, 1)
                act.activation(w_hi[:, slot, :], w_raw[:, slot, :], ACT.Copy).then_inc(hi_done, 1)

            for half in range(HALVES):
                pairs(act, half, work)
            if final:
                for half in range(HALVES):
                    for t in range(half * QG, (half + 1) * QG):
                        act.wait_ge(added, 2 * t + 2)
                        if t:
                            act.wait_ge(squared, t)
                        act.activation(junk[:], x_sb[:, t, :], ACT.Square,
                                       accum_out=sq_sum[:, t:t + 1]).then_inc(squared, 1)
                    act.wait_ge(var_done, half + 1)
                    act.activation(rstd[:, half * QG:(half + 1) * QG],
                                   var[:, half * QG:(half + 1) * QG],
                                   ACT.Sqrt).then_inc(root_done, 1)
            else:
                for t in range(TT):
                    act.wait_ge(added, 2 * t + 2)
                    act.dma_start(x_save[t * P:(t + 1) * P, :], x_sb[:, t, :]).then_inc(saved, 16)
                act.wait_ge(saved, 16 * TT)

        @block.vector
        def _(dve):
            count = [0]

            def chain(ins):
                count[0] += 1
                ins.then_inc(linked, 1)
                dve.wait_ge(linked, count[0])

            def work(n, slot, first, last):
                dve.wait_ge(hi_done, 2 * n + 1)
                at_least(dve, mm_done, n - 1)
                dve.tensor_tensor(og_lo[:, slot, :], og_raw[:, slot, :],
                                  og_hi[:, slot, :].bitcast(F32), ALU.subtract).then_inc(og_lo_done, 1)

            for half in range(HALVES):
                pairs(dve, half, work)
                dve.wait_ge(mm_done, HEADS * (half + 1))
                if half == 0:
                    dve.wait_ge(x_in, 16 * TT)
                for b in range(QG):
                    for n in range(2):
                        cols = slice(n * BANK, (n + 1) * BANK)
                        t = half * QG + b
                        dve.tensor_tensor(x_sb[:, t, cols], y[:, b, n, :], x_sb[:, t, cols],
                                          ALU.add).then_inc(added, 1)
            if final:
                dve.wait_ge(gain_in, 16)
                for half in range(HALVES):
                    cols = slice(half * QG, (half + 1) * QG)
                    dve.wait_ge(squared, (half + 1) * QG)
                    rstd_steps(dve, chain, sq_sum[:, cols], D, var[:, cols], rstd[:, cols],
                               tmp[:, cols], var_done, root_done, half + 1)
                    for t in range(half * QG, (half + 1) * QG):
                        dve.scalar_tensor_tensor(x_sb[:, t, :], x_sb[:, t, :], rstd[:, t:t + 1],
                                                 gain[:], ALU.mult, ALU.mult).then_inc(normed, 1)
                for t in range(TT):
                    dve.wait_ge(normed, t + 1)

        @block.tensor
        def _(pe):
            def work(n, slot, first, last):
                pe.wait_ge(og_lo_done, n + 1)
                pe.wait_ge(w_lo_done, n + 1)
                for b in range(QG):
                    for col in range(2):
                        if first and not (isinstance(n, int) and n == 0):
                            pe.wait_ge(added, 2 * b + col + 1)
                        for k, (o, w) in enumerate(products(og_hi, og_lo, w_hi, w_lo)):
                            mm = pe.matmul(y[:, b, col, :], o[:, slot, b * P:(b + 1) * P],
                                           w[:, slot, col * BANK:(col + 1) * BANK],
                                           start=(first and k == 0), stop=(last and k == 2))
                mm.then_inc(mm_done, 1)

            for half in range(HALVES):
                pairs(pe, half, work)

    if final:
        stored = c.sem("stored")
        with nc.Block() as block:

            @block.sync
            def _(sp):
                for t in range(TT):
                    sp.dma_start(out_dram[t * P:(t + 1) * P, :], x_sb[:, t, :]).then_inc(stored, 16)
                sp.wait_ge(stored, 16 * TT)


def build_latents(nc, c, w_in, positions, inv_freq, q_norm, kv_norm, w_qb, ident, hT_hi, hT_lo,
                  qn_hi, qn_lo, kvn_hi, kvn_lo, kr_hi, kr_lo, qr_dram):
    GROUPS = 2
    GH = HEADS // GROUPS
    LAT_T = QKT + 1

    wl_raw = c.sb("wl_raw", [P, KT, LAT])
    wl_hi, wl_lo = c.sb("wl_hi", [P, KT, LAT], F32R), c.sb("wl_lo", [P, KT, LAT], F32R)
    wr_raw = c.sb("wr_raw", [P, QKT, HEADS, ROPE])
    wr_hi = c.sb("wr_hi", [P, QKT, HEADS, ROPE], F32R)
    wr_lo = c.sb("wr_lo", [P, QKT, HEADS, ROPE], F32R)
    lat = c.sb("lat", [P, TT, LAT])
    junk = c.sb("junk", [P, Q_RANK])
    sq_sum, var, rstd, tmp = (c.sb(n, [P, 2 * TT]) for n in ("sq_sum", "var", "rstd", "tmp"))
    gain = c.sb("gain", [P, LAT_T])
    pos_i = c.sb("pos_i", [P, TT], I32)
    pos = c.sb("pos", [P, TT])
    freq = c.sb("freq", [P, HALF_ROPE])
    ang, turns, part = (c.sb(n, [P, TT, HALF_ROPE]) for n in ("ang", "turns", "part"))
    t_hi, t_lo = (c.sb(n, [P, TT, HALF_ROPE], F32R) for n in ("t_hi", "t_lo"))
    cos2, sin2 = (c.sb(n, [P, TT, 2, HALF_ROPE]) for n in ("cos2", "sin2"))
    qx = c.sb("qx", [P, 2, GH, 2, HALF_ROPE])
    qc, qs = (c.sb(n, [P, 2, GH, 2, HALF_ROPE]) for n in ("qc", "qs"))
    qr = c.sb("qr", [P, 2, GH, 2, HALF_ROPE])
    kc, ks = qc[:, 0, :, :, :], qs[:, 0, :, :, :]
    kr = qr[:].rearrange("p s h a r -> p (s h a r)").rearrange("p (t a r) -> p t a r", t=TT, a=2)
    assert GH == TT
    banks = c.psum("banks", [P, 8, BANK])

    (in_w, in_wr, in_small, in_gain, wl_hi_done, wl_lo_done, wr_done, mm_done, lat_done, squared,
     var_done, root_done, linked, scaled, angles, trig, turned, hi_done, lo_done, rotated_k,
     q_mm, q_x, q_mul, q_rot, q_out0, q_out1, pooled) = (c.sem(n) for n in (
         "in_w", "in_wr", "in_small", "in_gain", "wl_hi_done", "wl_lo_done", "wr_done", "mm_done",
         "lat_done", "squared", "var_done", "root_done", "linked", "scaled", "angles", "trig",
         "turned", "hi_done", "lo_done", "rotated_k", "q_mm", "q_x", "q_mul", "q_rot", "q_out0",
         "q_out1", "pooled"))
    q_out = [q_out0, q_out1]

    import math
    two_pi = 2.0 * math.pi
    c1 = math.floor(two_pi * 2 ** 9) / 2 ** 9
    c2 = math.floor((two_pi - c1) * 2 ** 21) / 2 ** 21
    c3 = two_pi - c1 - c2
    ROUND = 1.5 * 2 ** 23

    turns_of = [(u, half) for u in range(LAT_T + 1) for half in range(HALVES)]
    units = [(t, g) for t in range(TT) for g in range(GROUPS)]
    KEY_BANKS = 4

    with nc.Block() as block:

        @block.sync
        def _(sp):
            sp.dma_start(wl_raw[:], w_in.rearrange("(k p) n -> p k n", p=P)[:, :, 0:LAT])\
                .then_inc(in_w, 16)
            sp.dma_start(pos_i[:], positions.rearrange("b (t p) -> p (b t)", p=P),
                         allow_slow_non_contiguous=True)\
                .then_inc(in_small, 16)
            sp.dma_start(freq[:], inv_freq.broadcast_to([P, HALF_ROPE])).then_inc(in_small, 16)
            sp.dma_start(gain[:, 0:QKT], q_norm.rearrange("(k p) -> p k", p=P),
                         allow_slow_non_contiguous=True).then_inc(in_gain, 16)
            sp.dma_start(gain[:, QKT:LAT_T], kv_norm.rearrange("(k p) -> p k", p=P),
                         allow_slow_non_contiguous=True)\
                .then_inc(in_gain, 16)
            for k in range(QKT):
                src = w_qb[k * P:(k + 1) * P, :].rearrange("p (h n) -> p h n", h=HEADS)
                sp.dma_start(wr_raw[:, k, :, :], src[:, :, NOPE:NOPE + ROPE]).then_inc(in_wr, 16)
            for n, (t, g) in enumerate(units):
                sp.wait_ge(q_rot, 2 * (n + 1))
                sp.dma_start(qr_dram[t * P:(t + 1) * P, g * GH * ROPE:(g + 1) * GH * ROPE],
                             qr[:, n % 2, :, :, :].rearrange("p h a r -> p (h a r)"))\
                    .then_inc(q_out[n % 2], 16)
            for s in range(2):
                sp.wait_ge(q_out[s], 16 * len(units) // 2)

        @block.gpsimd
        def _(pool):
            for kt in range(KT):
                pool.wait_ge(wl_hi_done, kt + 1)
                pool.tensor_tensor(wl_lo[:, kt, :], wl_raw[:, kt, :], wl_hi[:, kt, :].bitcast(F32),
                                   ALU.subtract).then_inc(wl_lo_done, 1)
            for k in range(QKT):
                pool.wait_ge(wr_done, k + 1)
                pool.tensor_tensor(wr_lo[:, k, :, :], wr_raw[:, k, :, :],
                                   wr_hi[:, k, :, :].bitcast(F32), ALU.subtract).then_inc(pooled, 1)
            for n in range(len(units)):
                pool.wait_ge(q_mul, 2 * (n + 1))
                if n >= 2:
                    pool.wait_ge(q_out[n % 2], 16 * (n // 2))
                s = n % 2
                pool.tensor_tensor(qr[:, s, :, 0, :], qc[:, s, :, 0, :], qs[:, s, :, 1, :],
                                   ALU.subtract).then_inc(q_rot, 1)
                pool.tensor_tensor(qr[:, s, :, 1, :], qs[:, s, :, 0, :], qc[:, s, :, 1, :],
                                   ALU.add).then_inc(q_rot, 1)

        @block.tensor
        def _(pe):
            for t in range(TT):
                at_least(pe, squared, 2 * (t - KEY_BANKS + 1))
                for kt in range(KT):
                    if t == 0:
                        pe.wait_ge(wl_lo_done, kt + 1)
                    for n, (h, w) in enumerate(products(hT_hi, hT_lo, wl_hi, wl_lo)):
                        mm = pe.matmul(banks[:, t % KEY_BANKS, 0:LAT], h[:, kt, t * P:(t + 1) * P],
                                       w[:, kt, :], start=(kt == 0 and n == 0),
                                       stop=(kt == KT - 1 and n == 2))
                mm.then_inc(mm_done, 1)
            pe.wait_ge(squared, 2 * TT)
            for n, (u, half) in enumerate(turns_of):
                if u == 0 and half == 0:
                    pe.wait_ge(scaled, 2 * TT)
                if u == LAT_T and half == 0:
                    pe.wait_ge(rotated_k, 4)
                at_least(pe, lo_done, n - KEY_BANKS + 1)
                for b in range(QG):
                    t = half * QG + b
                    src = lat[:, t, u * P:(u + 1) * P] if u < LAT_T else \
                        kr[:, t, :, :].rearrange("p a r -> p (a r)")
                    mm = pe.transpose(banks[:, n % KEY_BANKS, b * P:(b + 1) * P], src, ident[:])
                mm.then_inc(turned, 1)
            pe.wait_ge(lo_done, QKT * HALVES)
            pe.wait_ge(pooled, QKT)
            for n, (t, g) in enumerate(units):
                at_least(pe, q_x, n - 3)
                for k in range(QKT):
                    for m, (h, w) in enumerate(products(qn_hi, qn_lo, wr_hi, wr_lo)):
                        mm = pe.matmul(banks[:, KEY_BANKS + n % 4, :], h[:, k, t * P:(t + 1) * P],
                                       w[:, k, g * GH:(g + 1) * GH, :]
                                       .rearrange("p h r -> p (h r)"),
                                       start=(k == 0 and m == 0), stop=(k == QKT - 1 and m == 2))
                mm.then_inc(q_mm, 1)

        @block.scalar
        def _(act):
            for t in range(TT):
                act.wait_ge(mm_done, t + 1)
                bank = banks[:, t % KEY_BANKS, :]
                act.activation(lat[:, t, :], bank[:, 0:LAT], ACT.Copy).then_inc(lat_done, 1)
                if t:
                    act.wait_ge(squared, 2 * t)
                act.activation(junk[:], bank[:, 0:Q_RANK], ACT.Square,
                               accum_out=sq_sum[:, t:t + 1]).then_inc(squared, 1)
                act.wait_ge(squared, 2 * t + 1)
                act.activation(junk[:, 0:KV_RANK], bank[:, Q_RANK:Q_RANK + KV_RANK], ACT.Square,
                               accum_out=sq_sum[:, TT + t:TT + t + 1]).then_inc(squared, 1)
            act.wait_ge(var_done, 2)
            act.activation(rstd[:], var[:], ACT.Sqrt).then_inc(root_done, 1)
            act.wait_ge(angles, 2)
            for a in range(2):
                act.activation(sin2[:, :, a, :], ang[:], ACT.Sin).then_inc(trig, 1)
                act.activation(cos2[:, :, a, :], part[:], ACT.Sin).then_inc(trig, 1)
            act.wait_ge(in_gain, 32)
            for n, (u, half) in enumerate(turns_of):
                act.wait_ge(turned, n + 1)
                cols = slice(half * BANK, (half + 1) * BANK)
                bank = banks[:, n % KEY_BANKS, :]
                if u < QKT:
                    ins = act.activation(qn_hi[:, u, cols], bank, ACT.Copy, scale=gain[:, u:u + 1])
                elif u < LAT_T:
                    ins = act.activation(kvn_hi[:, cols], bank, ACT.Copy, scale=gain[:, u:u + 1])
                else:
                    ins = act.activation(kr_hi[:, cols], bank, ACT.Copy)
                ins.then_inc(hi_done, 1)
            for n in range(len(units)):
                act.wait_ge(q_mm, n + 1)
                at_least(act, q_mul, 2 * (n - 1))
                act.activation(qx[:, n % 2, :, :, :].rearrange("p h a r -> p (h a r)"),
                               banks[:, KEY_BANKS + n % 4, :], ACT.Copy).then_inc(q_x, 1)

        @block.vector
        def _(dve):
            count = [0]

            def chain(ins):
                count[0] += 1
                ins.then_inc(linked, 1)
                dve.wait_ge(linked, count[0])

            def reduce_angle():
                chain(dve.tensor_scalar(turns[:], ang[:], 1.0 / two_pi, ROUND, ALU.mult, ALU.add))
                chain(dve.tensor_scalar(turns[:], turns[:], -ROUND, None, ALU.add))
                chain(dve.tensor_copy(t_hi[:], turns[:]))
                chain(dve.tensor_tensor(t_lo[:], turns[:], t_hi[:].bitcast(F32), ALU.subtract))
                for const in (c1, c2, c3):
                    for t in (t_hi, t_lo):
                        chain(dve.scalar_tensor_tensor(ang[:], t[:].bitcast(F32), -const, ang[:],
                                                       ALU.mult, ALU.add))

            dve.wait_ge(in_w, 16)
            for kt in range(KT):
                dve.tensor_copy(wl_hi[:, kt, :], wl_raw[:, kt, :]).then_inc(wl_hi_done, 1)
            dve.wait_ge(in_wr, 16 * QKT)
            for k in range(QKT):
                dve.tensor_copy(wr_hi[:, k, :, :], wr_raw[:, k, :, :]).then_inc(wr_done, 1)
            dve.wait_ge(in_small, 32)
            chain(dve.tensor_copy(pos[:], pos_i[:]))
            chain(dve.tensor_tensor(ang[:], pos[:].unsqueeze(2).broadcast_to([P, TT, HALF_ROPE]),
                                    freq[:].unsqueeze(1).broadcast_to([P, TT, HALF_ROPE]),
                                    ALU.mult))
            reduce_angle()
            reduce_angle()
            chain(dve.tensor_scalar(part[:], ang[:], math.pi / 2, None, ALU.add))
            chain(dve.tensor_scalar(turns[:], part[:], math.pi, -two_pi, ALU.is_gt, ALU.mult))
            chain(dve.tensor_tensor(part[:], part[:], turns[:], ALU.add))
            PI_BELOW = 3.1415925
            dve.tensor_scalar(part[:], part[:], PI_BELOW, -PI_BELOW, ALU.min, ALU.max)\
                .then_inc(angles, 1)
            dve.tensor_scalar(ang[:], ang[:], PI_BELOW, -PI_BELOW, ALU.min, ALU.max)\
                .then_inc(angles, 1)

            dve.wait_ge(squared, 2 * TT)
            dve.tensor_scalar(var[:, 0:TT], sq_sum[:, 0:TT], 1.0 / Q_RANK, EPS, ALU.mult,
                              ALU.add).then_inc(var_done, 1)
            dve.tensor_scalar(var[:, TT:], sq_sum[:, TT:], 1.0 / KV_RANK, EPS, ALU.mult,
                              ALU.add).then_inc(var_done, 1)
            dve.wait_ge(root_done, 1)
            chain(dve.reciprocal(rstd[:], rstd[:]))
            chain(dve.tensor_tensor(tmp[:], rstd[:], rstd[:], ALU.mult))
            chain(dve.tensor_tensor(tmp[:], tmp[:], var[:], ALU.mult))
            chain(dve.tensor_scalar(tmp[:], tmp[:], -0.5, 1.5, ALU.mult, ALU.add))
            chain(dve.tensor_tensor(rstd[:], rstd[:], tmp[:], ALU.mult))
            dve.wait_ge(lat_done, TT)
            for t in range(TT):
                q, kv = lat[:, t, 0:Q_RANK], lat[:, t, Q_RANK:Q_RANK + KV_RANK]
                dve.tensor_scalar(q, q, rstd[:, t:t + 1], None, ALU.mult).then_inc(scaled, 1)
                dve.tensor_scalar(kv, kv, rstd[:, TT + t:TT + t + 1], None,
                                  ALU.mult).then_inc(scaled, 1)

            dve.wait_ge(trig, 4)
            k_x = lat[:, :, Q_RANK + KV_RANK:LAT].rearrange("p t (a r) -> p t a r", a=2)
            chain(dve.tensor_tensor(kc, k_x, cos2[:], ALU.mult))
            chain(dve.tensor_tensor(ks, k_x, sin2[:], ALU.mult))
            for a in range(2):
                dve.tensor_tensor(kr[:, :, a, 0:HALF_ROPE], kc[:, :, 0, :], ks[:, :, 1, :],
                                  ALU.subtract).then_inc(rotated_k, 1)
                dve.tensor_tensor(kr[:, :, a, HALF_ROPE:ROPE], ks[:, :, 0, :], kc[:, :, 1, :],
                                  ALU.add).then_inc(rotated_k, 1)

            dve.wait_ge(in_gain, 32)
            for n, (u, half) in enumerate(turns_of):
                dve.wait_ge(hi_done, n + 1)
                cols = slice(half * BANK, (half + 1) * BANK)
                bank = banks[:, n % KEY_BANKS, :]
                if u < QKT:
                    ins = dve.scalar_tensor_tensor(qn_lo[:, u, cols], bank, gain[:, u:u + 1],
                                                   qn_hi[:, u, cols].bitcast(F32), ALU.mult,
                                                   ALU.subtract)
                elif u < LAT_T:
                    ins = dve.scalar_tensor_tensor(kvn_lo[:, cols], bank, gain[:, u:u + 1],
                                                   kvn_hi[:, cols].bitcast(F32), ALU.mult,
                                                   ALU.subtract)
                else:
                    ins = dve.tensor_tensor(kr_lo[:, cols], bank, kr_hi[:, cols].bitcast(F32),
                                            ALU.subtract)
                ins.then_inc(lo_done, 1)
            dve.wait_ge(rotated_k, 4)
            for n, (t, g) in enumerate(units):
                s = n % 2
                dve.wait_ge(q_x, n + 1)
                at_least(dve, q_rot, 2 * (n - 1))
                x = qx[:, s, :, :, :].rearrange("p h a r -> p h (a r)")
                for out, trig2 in ((qc, cos2), (qs, sin2)):
                    angle = trig2[:, t, :, :].rearrange("p a r -> p (a r)").unsqueeze(1)
                    dve.tensor_tensor(out[:, s, :, :, :].rearrange("p h a r -> p h (a r)"), x,
                                      angle.broadcast_to([P, GH, ROPE]), ALU.mult)\
                       .then_inc(q_mul, 1)
            dve.wait_ge(lo_done, len(turns_of))


def build_mla_heads(nc, c, w_in, w_qb, w_kvb, ident, ident_r, chunk_r, hT_hi, hT_lo, qn_hi, qn_lo,
                    kvn_hi, kvn_lo, kr_hi, kr_lo, qr_dram, og_dram):
    CHUNKS = ((0, 3), (3, 3), (6, 2))
    G_STEP = TT - 2 * len(CHUNKS)
    Q_STEPS = (5, 7)
    PER_HEAD = 8
    ROPE_STACK = 2 * ROPE
    assert ROPE_STACK == P

    wg_raw = c.sb("wg_raw", [P, 3, P])
    wg_hi, wg_lo = c.sb("wg_hi", [P, KT, P], F32R), c.sb("wg_lo", [P, KT, P], F32R)
    ws_raw = c.sb("ws_raw", [P, QKT + 1, P])
    ws_hi, ws_lo = c.sb("ws_hi", [P, QKT + 1, P], F32R), c.sb("ws_lo", [P, QKT + 1, P], F32R)
    wv_raw = c.sb("wv_raw", [P, HD])
    wv_hi, wv_lo = c.sb("wv_hi", [P, HD], F32R), c.sb("wv_lo", [P, HD], F32R)
    qr_in = c.sb("qr_in", [P, TT, 2, ROPE])
    qr = c.sb("qr", [P, TOK], F32R)
    q_hi, q_lo = c.sb("q_hi", [P, TOK], F32R), c.sb("q_lo", [P, TOK], F32R)
    k_hi, k_lo = c.sb("k_hi", [P, 2 * TOK], F32R), c.sb("k_lo", [P, 2 * TOK], F32R)
    v_hi, v_lo = c.sb("v_hi", [P, TT, HD], F32R), c.sb("v_lo", [P, TT, HD], F32R)
    gate = c.sb("gate", [P, 2 * TOK])
    prob = c.sb("prob", [P, 2, TOK])
    pT_hi, pT_lo = c.sb("pT_hi", [P, TT, BANK], F32R), c.sb("pT_lo", [P, TT, BANK], F32R)
    og = c.sb("og", [P, HALVES, BANK])
    top, neg_top, total, inverse = (c.sb(n, [P, TT]) for n in ("top", "neg_top", "total",
                                                               "inverse"))
    zero = c.sb("zero", [P, 1])

    g = c.psum("g", [P, HALVES, BANK])
    z = c.psum("z", [P, TOK])
    pT = c.psum("pT", [P, TT, P])
    pv = c.psum("pv", [P, BANK])
    small = c.psum("small", [P, BANK])

    (wg_in, ws_in, wv_in, qr_loaded, w_split, ws_split, wv_split, g_mm, g_sig, g_done, small_mm,
     small_hi, small_free, z_done, top_done, neg_done, exp_done, inv_done, p_done, pT_done,
     pT_hi_done, pT_lo_done, pv_done, og_done, og_out0, og_out1, zeroed) = (c.sem(n) for n in (
         "wg_in", "ws_in", "wv_in", "qr_loaded", "w_split", "ws_split", "wv_split", "g_mm",
         "g_sig", "g_done", "small_mm", "small_hi", "small_free", "z_done", "top_done",
         "neg_done", "exp_done", "inv_done", "p_done", "pT_done", "pT_hi_done", "pT_lo_done",
         "pv_done", "og_done", "og_out0", "og_out1", "zeroed"))
    og_out = [og_out0, og_out1]

    w_cols = w_in.rearrange("(k p) n -> p k n", p=P)
    qb_cols = w_qb.rearrange("(k p) n -> p k n", p=P)
    qr_rows = qr_dram.rearrange("(t p) n -> p t n", p=P)

    K0, V0, K1, V1, Q0, R0, Q1, R1 = range(PER_HEAD)

    def use(i, n):
        if isinstance(i, int) and i == -1:
            return {K0: 1, K1: 2, Q0: 3, R0: 4, Q1: 5, R1: 6}[n]
        if isinstance(i, int) and i == HEADS - 1:
            return 6 + PER_HEAD * i + {V0: 1, V1: 2}[n]
        return i * PER_HEAD + (6 + n + 1)

    def half_cols(half):
        return slice(half * BANK, (half + 1) * BANK)

    def iterations(eng, step):
        step(-1, False, True)
        step(0, True, True)
        with eng.Fori(1, HEADS - 1) as i:
            step(i, True, True)
        step(HEADS - 1, True, False)

    with nc.Block() as block:

        @block.sync
        def _(sp):
            def load_small(j):
                at_least(sp, ws_split, 2 * j)
                sp.dma_start(ws_raw[:, 0:QKT, :],
                             qb_cols[:, :, bass.ds(j * (NOPE + ROPE), NOPE)]).then_inc(ws_in, 16)
                sp.dma_start(ws_raw[:, QKT, :],
                             w_kvb[:, bass.ds(j * (NOPE + HD), NOPE)]).then_inc(ws_in, 16)

            def load_gate(j):
                for n, (k0, count) in enumerate(CHUNKS):
                    at_least(sp, w_split, 2 * (len(CHUNKS) * j + n))
                    sp.dma_start(wg_raw[:, 0:count, :],
                                 w_cols[:, k0:k0 + count, bass.ds(j * HD + LAT, HD)])\
                        .then_inc(wg_in, 16)

            def load_values(j):
                at_least(sp, wv_split, 2 * j)
                sp.dma_start(wv_raw[:], w_kvb[:, bass.ds(j * (NOPE + HD) + NOPE, HD)])\
                    .then_inc(wv_in, 16)

            def load_rotated(j):
                if isinstance(j, int):
                    at_least(sp, small_mm, use(j - 2, R1) if j else 0)
                else:
                    sp.wait_ge(small_mm, use(j - 2, R1))
                src = qr_rows[:, :, bass.ds(j * ROPE, ROPE)]
                for a in range(2):
                    sp.dma_start(qr_in[:, :, a, :], src).then_inc(qr_loaded, 16)

            def store(i, group):
                i = settled(sp, i)
                sp.wait_ge(og_done, HALVES * i + group + 1)
                dst = og_dram[bass.ds(i, 1), :, half_cols(group)].rearrange("h p n -> (h p) n")
                sp.dma_start(dst, og[:, group, :]).then_inc(og_out[group], 16)

            def load(j):
                load_small(j)
                load_gate(j)
                load_values(j)
                load_rotated(j)

            load(0)
            load(1)
            store(0, 0)
            with sp.Fori(2, HEADS) as j:
                load(j)
                store(j - 2, 1)
                store(j - 1, 0)
            store(HEADS - 2, 1)
            store(HEADS - 1, 0)
            store(HEADS - 1, 1)
            for group in range(HALVES):
                sp.wait_ge(og_out[group], 16 * HEADS)

        @block.gpsimd
        def _(pool):
            def split(raw, hi, lo, done, before):
                zeros = zero[:].broadcast_to([P, HD]) if len(raw.shape) == 2 else \
                    zero[:].unsqueeze(2).broadcast_to([P, raw.shape[1], P])
                pool.tensor_tensor(hi, raw, zeros, ALU.add).then_inc(done, 1)
                pool.wait_ge(done, before * 2 + 1)
                pool.tensor_tensor(lo, raw, hi.bitcast(F32), ALU.subtract).then_inc(done, 1)

            def splits(j):
                pool.wait_ge(ws_in, 32 * j + 32)
                if isinstance(j, int):
                    at_least(pool, small_mm, use(j - 2, Q1) if j else 0)
                else:
                    pool.wait_ge(small_mm, use(j - 2, Q1))
                split(ws_raw[:], ws_hi[:], ws_lo[:], ws_split, j)
                for n, (k0, count) in enumerate(CHUNKS):
                    m = len(CHUNKS) * j + n
                    pool.wait_ge(wg_in, 16 * m + 16)
                    at_least(pool, g_mm, 2 * len(CHUNKS) * (j - 1) + len(CHUNKS) + n + 1)
                    split(wg_raw[:, 0:count, :], wg_hi[:, k0:k0 + count, :],
                          wg_lo[:, k0:k0 + count, :], w_split, m)
                pool.wait_ge(wv_in, 16 * j + 16)
                if isinstance(j, int):
                    at_least(pool, small_mm, use(j - 1, V1) if j else 0)
                else:
                    pool.wait_ge(small_mm, use(j - 1, V1))
                split(wv_raw[:], wv_hi[:], wv_lo[:], wv_split, j)

            pool.wait_ge(zeroed, 1)
            splits(0)
            with pool.Fori(1, HEADS) as j:
                splits(j)

        @block.tensor
        def _(pe):
            def small_use(i, n):
                at_least(pe, small_free, use(i, n) - 1)

            def keys(i, half):
                n = (K0, K1)[half]
                pe.wait_ge(ws_split, 2 * i + 4)
                small_use(i, n)
                for m, (w, x) in enumerate(products(ws_hi, ws_lo, kvn_hi, kvn_lo)):
                    mm = pe.matmul(small[:], w[:, QKT, :], x[:, half_cols(half)],
                                   start=(m == 0), stop=(m == 2))
                mm.then_inc(small_mm, 1)

            def queries(i, half):
                small_use(i, (Q0, Q1)[half])
                for k in range(QKT):
                    for m, (w, x) in enumerate(products(ws_hi, ws_lo, qn_hi, qn_lo)):
                        mm = pe.matmul(small[:], w[:, k, :], x[:, k, half_cols(half)],
                                       start=(k == 0 and m == 0), stop=(k == QKT - 1 and m == 2))
                mm.then_inc(small_mm, 1)

            def rotated(i, half):
                pe.wait_ge(qr_loaded, 32 * i + 64)
                small_use(i, (R0, R1)[half])
                for b in range(QG):
                    mm = pe.transpose(small[:, b * P:(b + 1) * P],
                                      qr_in[:, half * QG + b, :, :].rearrange("p a r -> p (a r)"),
                                      ident[:])
                mm.then_inc(small_mm, 1)

            def values(i, half):
                pe.wait_ge(wv_split, 2 * i + 2)
                small_use(i, (V0, V1)[half])
                for b in range(QG):
                    rows = slice((half * QG + b) * P, (half * QG + b + 1) * P)
                    for m, (x, w) in enumerate(products(kvn_hi, kvn_lo, wv_hi, wv_lo)):
                        mm = pe.matmul(small[:, b * P:(b + 1) * P], x[:, rows], w[:],
                                       start=(m == 0), stop=(m == 2))
                mm.then_inc(small_mm, 1)

            def gates(i, s):
                half, n = divmod(s - G_STEP, len(CHUNKS))
                k0, count = CHUNKS[n]
                pe.wait_ge(w_split, 2 * (len(CHUNKS) * (i + 1) + n + 1))
                at_least(pe, g_done, HALVES * i + HALVES)
                for kt in range(k0, k0 + count):
                    for m, (w, h) in enumerate(products(wg_hi, wg_lo, hT_hi, hT_lo)):
                        mm = pe.matmul(g[:, half, :], w[:, kt, :], h[:, kt, half_cols(half)],
                                       start=(kt == 0 and m == 0), stop=(kt == KT - 1 and m == 2))
                mm.then_inc(g_mm, 1)

            def scores(i, s):
                if isinstance(i, int):
                    pe.wait_ge(small_free, use(i - 1, (R0, R1)[s // QG]))
                else:
                    pe.wait_ge(small_free, use(i - 1, (R0, R1)[s // QG]))
                at_least(pe, exp_done, TT * i + s)
                n_keys = (s + 1) * P
                rows = slice(s * P, (s + 1) * P)
                for c0 in range(0, n_keys, BANK):
                    width = min(BANK, n_keys - c0)
                    last = c0 + width == n_keys
                    out = z[:, c0:c0 + width]
                    pe.matmul(out, qr[:, rows], kr_lo[:, c0:c0 + width], start=True, stop=False)
                    for q, k in products(q_hi, q_lo, k_hi, k_lo):
                        pe.matmul(out, q[:, rows], k[:, bass.ds((i % 2) * TOK + c0, width)],
                                  start=False, stop=False)
                    mm = pe.matmul(out, qr[:, rows], kr_hi[:, c0:c0 + width], start=False,
                                   stop=not last)
                    if last:
                        mm = pe.matmul(z[:, rows], ident_r[:], chunk_r[:], start=False, stop=True)
                mm.then_inc(z_done, 1)

            def turn_probs(i, s):
                pe.wait_ge(p_done, TT * i + s + 1)
                at_least(pe, pT_lo_done, TT * i + s)
                for kb in range(s + 1):
                    mm = pe.transpose(pT[:, kb, :], prob[:, s % 2, kb * P:(kb + 1) * P], ident[:])
                mm.then_inc(pT_done, 1)

            def mix(i, group):
                pe.wait_ge(pT_lo_done, TT * i + QG * (group + 1))
                pe.wait_ge(small_free, use(i, (V0, V1)[group]))
                at_least(pe, og_done, HALVES * i + group)
                blocks = QG * (group + 1)
                for kb in range(blocks):
                    q0 = max(kb - QG * group, 0) * P
                    for n, (v, w) in enumerate(products(v_hi, v_lo, pT_hi, pT_lo)):
                        mm = pe.matmul(pv[:, q0:BANK], v[:, kb, :], w[:, kb, q0:BANK],
                                       start=(kb == 0 and n == 0),
                                       stop=(kb == blocks - 1 and n == 2))
                mm.then_inc(pv_done, 1)

            def step(i, attend, proj):
                if attend:
                    scores(i, 0)
                for s in range(TT):
                    if proj and s < HALVES:
                        keys(i, s)
                    if proj and s in Q_STEPS:
                        queries(i, Q_STEPS.index(s))
                    if attend:
                        if s == 0 and not (isinstance(i, int) and i == 0):
                            mix(i - 1, 1)
                        if s == QG:
                            mix(i, 0)
                        if s == 0:
                            values(i, 0)
                        turn_probs(i, s)
                        if s + 1 < TT:
                            scores(i, s + 1)
                        if s == 1:
                            values(i, 1)
                    if proj and s in Q_STEPS:
                        rotated(i, Q_STEPS.index(s))
                    if proj and s >= G_STEP:
                        gates(i, s)

            iterations(pe, step)
            mix(HEADS - 1, 1)

        @block.scalar
        def _(act):
            def evacuate(i, n):
                act.wait_ge(small_mm, use(i, n))
                half = {K0: 0, K1: 1, V0: 0, V1: 1, Q0: 0, Q1: 1, R0: 0, R1: 1}[n]
                if n in (K0, K1):
                    out = k_hi[:, bass.ds(((i + 1) % 2) * TOK + half * BANK, BANK)]
                elif n in (V0, V1):
                    out = v_hi[:, half * QG:(half + 1) * QG, :].rearrange("p t d -> p (t d)")
                elif n in (Q0, Q1):
                    out = q_hi[:, half_cols(half)]
                else:
                    out = qr[:, half_cols(half)]
                act.activation(out, small[:], ACT.Copy).then_inc(small_hi, 1)

            def exps(i, s):
                n_keys = (s + 1) * P
                act.wait_ge(neg_done, TT * i + s + 1)
                at_least(act, pT_done, TT * i + s - 1)
                act.activation(prob[:, s % 2, 0:n_keys], z[:, 0:n_keys], ACT.Exp,
                               bias=neg_top[:, s:s + 1], scale=MLA_SCALE,
                               accum_out=total[:, s:s + 1]).then_inc(exp_done, 1)

            def probs_hi(i, s):
                act.wait_ge(pT_done, TT * i + s + 1)
                q0 = (s % QG) * P
                act.activation(pT_hi[:, 0:s + 1, q0:q0 + P], pT[:, 0:s + 1, :],
                               ACT.Copy).then_inc(pT_hi_done, 1)

            def gate_sigmoid(j):
                act.wait_ge(g_mm, 2 * len(CHUNKS) * (j + 1))
                at_least(act, og_done, HALVES * (j - 1))
                act.activation(gate[:, bass.ds((j % 2) * TOK, TOK)],
                               g[:].rearrange("p a n -> p (a n)"), ACT.Sigmoid).then_inc(g_sig, 1)

            def step(i, attend, proj):
                if attend:
                    exps(i, 0)
                for s in range(TT):
                    if proj and s < HALVES:
                        evacuate(i, (K0, K1)[s])
                    if proj and s in Q_STEPS:
                        evacuate(i, (Q0, Q1)[Q_STEPS.index(s)])
                    if attend:
                        if s == 0:
                            evacuate(i, V0)
                        probs_hi(i, s)
                        if s + 1 < TT:
                            exps(i, s + 1)
                        if s == 1:
                            evacuate(i, V1)
                            gate_sigmoid(i)
                    if proj and s in Q_STEPS:
                        evacuate(i, (R0, R1)[Q_STEPS.index(s)])

            iterations(act, step)

        @block.vector
        def _(dve):
            def evacuate(i, n):
                dve.wait_ge(small_hi, use(i, n))
                half = {K0: 0, K1: 1, V0: 0, V1: 1, Q0: 0, Q1: 1, R0: 0, R1: 1}[n]
                src = small[:]
                if n in (K0, K1):
                    cols = bass.ds(((i + 1) % 2) * TOK + half * BANK, BANK)
                    hi, lo = k_hi[:, cols], k_lo[:, cols]
                elif n in (V0, V1):
                    tiles = slice(half * QG, (half + 1) * QG)
                    hi = v_hi[:, tiles, :].rearrange("p t d -> p (t d)")
                    lo = v_lo[:, tiles, :].rearrange("p t d -> p (t d)")
                elif n in (Q0, Q1):
                    hi, lo = q_hi[:, half_cols(half)], q_lo[:, half_cols(half)]
                else:
                    hi = lo = qr[ROPE:P, half_cols(half)]
                    src = small[ROPE:P, :]
                dve.tensor_tensor(lo, src, hi.bitcast(F32), ALU.subtract).then_inc(small_free, 1)

            def maxima(i, s):
                n_keys = (s + 1) * P
                dve.wait_ge(z_done, TT * i + s + 1)
                dve.tensor_reduce(top[:, s:s + 1], z[:, 0:n_keys], axis=AX_X,
                                  op=ALU.max).then_inc(top_done, 1)
                dve.wait_ge(top_done, TT * i + s + 1)
                dve.tensor_scalar(neg_top[:, s:s + 1], top[:, s:s + 1], -MLA_SCALE, None,
                                  ALU.mult).then_inc(neg_done, 1)

            def normalise(i, s):
                n_keys = (s + 1) * P
                dve.wait_ge(exp_done, TT * i + s + 1)
                dve.reciprocal(inverse[:, s:s + 1], total[:, s:s + 1]).then_inc(inv_done, 1)
                dve.wait_ge(inv_done, TT * i + s + 1)
                dve.tensor_scalar(prob[:, s % 2, 0:n_keys], prob[:, s % 2, 0:n_keys],
                                  inverse[:, s:s + 1], None, ALU.mult).then_inc(p_done, 1)

            def probs_lo(i, s):
                q0 = (s % QG) * P
                dve.wait_ge(pT_hi_done, TT * i + s + 1)
                dve.tensor_tensor(pT_lo[:, 0:s + 1, q0:q0 + P], pT[:, 0:s + 1, :],
                                  pT_hi[:, 0:s + 1, q0:q0 + P].bitcast(F32),
                                  ALU.subtract).then_inc(pT_lo_done, 1)

            def gate_mult(j):
                dve.wait_ge(g_sig, j + 1)
                for half in range(HALVES):
                    cols = bass.ds((j % 2) * TOK + half * BANK, BANK)
                    dve.tensor_tensor(gate[:, cols], g[:, half, :], gate[:, cols],
                                      ALU.mult).then_inc(g_done, 1)

            def gated(i, group):
                dve.wait_ge(pv_done, HALVES * i + group + 1)
                at_least(dve, og_out[group], 16 * i)
                at_least(dve, g_done, HALVES * (i + 1))
                dve.tensor_tensor(og[:, group, :], pv[:],
                                  gate[:, bass.ds((i % 2) * TOK + group * BANK, BANK)],
                                  ALU.mult).then_inc(og_done, 1)

            def step(i, attend, proj):
                if attend:
                    maxima(i, 0)
                    normalise(i, 0)
                for s in range(TT):
                    if proj and s < HALVES:
                        evacuate(i, (K0, K1)[s])
                    if proj and s in Q_STEPS:
                        evacuate(i, (Q0, Q1)[Q_STEPS.index(s)])
                    if attend:
                        if s == 0 and not (isinstance(i, int) and i == 0):
                            gated(i - 1, 1)
                        if s == QG:
                            gated(i, 0)
                        if s == 0:
                            evacuate(i, V0)
                        probs_lo(i, s)
                        if s + 1 < TT:
                            maxima(i, s + 1)
                            normalise(i, s + 1)
                        if s == 1:
                            evacuate(i, V1)
                            gate_mult(i)
                    if proj and s in Q_STEPS:
                        evacuate(i, (R0, R1)[Q_STEPS.index(s)])

            dve.memset(zero[:], 0.0).then_inc(zeroed, 1)
            iterations(dve, step)
            gated(HEADS - 1, 1)


def build(nc, x, positions, ln0, w_in0, w_out0, ln1, w_in1, q_norm1, w_qb1, kv_norm1, w_kvb1,
          w_out1, final_norm, inv_freq, out):
    og_dram = nc.dram_tensor("og_scratch", [HEADS, HD, TOK], F32, kind="Internal").ap()
    x1_dram = nc.dram_tensor("x1_scratch", [TOK, D], F32, kind="Internal").ap()
    qr_dram = nc.dram_tensor("qr_scratch", [TOK, HEADS * ROPE], F32, kind="Internal").ap()
    x_rows = x.rearrange("b t d -> (b t) d")
    out_rows = out.rearrange("b t d -> (b t) d")

    with ExitStack() as whole:
        shared = Chip(nc, whole, "all")
        with ExitStack() as ctx:
            ident, ident_r, strict_r, chunk_r = build_constants(nc, Chip(nc, ctx, "const"), shared)

        with ExitStack() as layer:
            h = Chip(nc, layer, "h0")
            hT_hi, hT_lo = h.sb("hT_hi", [P, KT, TOK], F32R), h.sb("hT_lo", [P, KT, TOK], F32R)
            with ExitStack() as ctx:
                c = Chip(nc, ctx, "norm0")
                build_norm(nc, c, c.sb("x", [P, TT, D]), x_rows, ln0, ident, hT_hi, hT_lo)
            with ExitStack() as ctx:
                build_stick_heads(nc, Chip(nc, ctx, "stick"), w_in0, ident, ident_r, strict_r,
                                  hT_hi, hT_lo, og_dram)

        with ExitStack() as layer:
            h = Chip(nc, layer, "h1")
            hT_hi, hT_lo = h.sb("hT_hi", [P, KT, TOK], F32R), h.sb("hT_lo", [P, KT, TOK], F32R)
            with ExitStack() as ctx:
                x_sb = Chip(nc, ctx, "x1").sb("x", [P, TT, D])
                with ExitStack() as inner:
                    build_out(nc, Chip(nc, inner, "out0"), w_out0, og_dram, x_rows, x_sb, x1_dram,
                              None, None)
                with ExitStack() as inner:
                    build_norm(nc, Chip(nc, inner, "norm1"), x_sb, None, ln1, ident, hT_hi, hT_lo)
            qn_hi, qn_lo = (h.sb(n, [P, QKT, TOK], F32R) for n in ("qn_hi", "qn_lo"))
            kvn_hi, kvn_lo = (h.sb(n, [P, TOK], F32R) for n in ("kvn_hi", "kvn_lo"))
            kr_hi, kr_lo = (h.sb(n, [P, TOK], F32R) for n in ("kr_hi", "kr_lo"))
            with ExitStack() as ctx:
                build_latents(nc, Chip(nc, ctx, "lat"), w_in1, positions, inv_freq, q_norm1,
                              kv_norm1, w_qb1, ident, hT_hi, hT_lo, qn_hi, qn_lo, kvn_hi, kvn_lo,
                              kr_hi, kr_lo, qr_dram)
            with ExitStack() as ctx:
                build_mla_heads(nc, Chip(nc, ctx, "mla"), w_in1, w_qb1, w_kvb1, ident, ident_r,
                                chunk_r, hT_hi, hT_lo, qn_hi, qn_lo, kvn_hi, kvn_lo, kr_hi, kr_lo,
                                qr_dram, og_dram)

        with ExitStack() as ctx:
            c = Chip(nc, ctx, "out1")
            build_out(nc, c, w_out1, og_dram, x1_dram, c.sb("x", [P, TT, D]), None, final_norm,
                      out_rows)


_INS = ["x", "positions", "ln0", "w_in0", "w_out0", "ln1", "w_in1", "q_norm1", "w_qb1",
        "kv_norm1", "w_kvb1", "w_out1", "final_norm"]


def kernel(**inputs):
    import numpy as _np
    import concourse.bacc as _bacc
    from concourse import mybir as _mybir
    from concourse.bass_utils import run_bass_kernel_spmd as _run

    nc = _bacc.Bacc("TRN2", target_bir_lowering=False, num_devices=1)
    arrays = {f"in_{n}_dram": _np.ascontiguousarray(inputs[n]) for n in _INS}
    freq = 10000.0 ** (-_np.arange(0, ROPE, 2, dtype=_np.float64) / ROPE)
    arrays["in_inv_freq_dram"] = freq.astype(_np.float32).reshape(1, HALF_ROPE)
    args = [nc.dram_tensor(n, a.shape, _mybir.dt.from_np(a.dtype), kind="ExternalInput").ap()
            for n, a in arrays.items()]
    out = nc.dram_tensor("out_0_dram", (1, TOK, D), F32, kind="ExternalOutput").ap()
    build(nc, *args, out)
    r = _run(nc, [arrays], core_ids=[0])
    return r.results[0]["out_0_dram"]
```

```python
from contextlib import ExitStack

import concourse.bass as bass
from concourse import mybir

F32 = mybir.dt.float32
F32R = mybir.dt.float32r
I32 = mybir.dt.int32
ALU = mybir.AluOpType
ACT = mybir.ActivationFunctionType
AX_X = mybir.AxisListType.X

P = 128
BANK = 512
D = 1024
TOK = 1024
KT = D // P
TT = TOK // P
HEADS = 16
HD = 128
D_INNER = HEADS * HD
HALVES = TOK // BANK
QG = BANK // P
CHUNK = 64
Q_RANK, KV_RANK, ROPE = 256, 128, 64
QKT = Q_RANK // P
HALF_ROPE = ROPE // 2
LAT = Q_RANK + KV_RANK + ROPE
NOPE = 128
EPS = 1e-6
NEG = -1e30
STICK_SCALE = HD ** -0.5
MLA_SCALE = (NOPE + ROPE) ** -0.5


def at_least(eng, sem, value):
    if isinstance(value, int) and value <= 0:
        return
    eng.wait_ge(sem, value)


def settled(eng, value):
    return value if isinstance(value, int) else eng.snap(value)


def products(w_hi, w_lo, x_hi, x_lo):
    return ((w_lo, x_hi), (w_hi, x_lo), (w_hi, x_hi))


class Chip:

    def __init__(self, nc, ctx, tag):
        self.nc, self.ctx, self.tag = nc, ctx, tag

    def sb(self, name, shape, dt=F32):
        return self.ctx.enter_context(self.nc.sbuf_tensor(f"{self.tag}_{name}", shape, dt))

    def psum(self, name, shape):
        return self.ctx.enter_context(self.nc.psum_tensor(f"{self.tag}_{name}", shape, F32))

    def sem(self, name):
        return self.ctx.enter_context(self.nc.semaphore(f"{self.tag}_{name}"))


def build_constants(nc, c, outer):
    ident = outer.sb("ident", [P, P])
    ident_r = outer.sb("ident_r", [P, P], F32R)
    strict_r = outer.sb("strict_r", [P, P], F32R)
    chunk_r = outer.sb("chunk_r", [P, P], F32R)
    strict = c.sb("strict", [P, P])
    chunk = c.sb("chunk", [P, P])
    cleared, made, cast = c.sem("cleared"), c.sem("made"), c.sem("cast")
    with nc.Block() as block:

        @block.gpsimd
        def _(pool):
            pool.memset(ident[:], 0.0).then_inc(cleared, 1)
            pool.memset(strict[:], 0.0).then_inc(cleared, 1)
            pool.memset(chunk[:], 0.0).then_inc(cleared, 1)
            pool.wait_ge(cleared, 3)
            pool.affine_select(out=ident[:], in_=ident[:], compare_op=ALU.not_equal, fill=1.0,
                               base=0, pattern=[[-1, P]], channel_multiplier=1).then_inc(made, 1)
            pool.affine_select(out=strict[:], in_=strict[:], compare_op=ALU.is_gt, fill=NEG,
                               base=0, pattern=[[-1, P]], channel_multiplier=1).then_inc(made, 1)
            pool.memset(chunk[0:CHUNK, CHUNK:P], NEG).then_inc(made, 1)

        @block.vector
        def _(dve):
            dve.wait_ge(made, 3)
            dve.tensor_copy(ident_r[:], ident[:]).then_inc(cast, 1)
            dve.tensor_copy(strict_r[:], strict[:]).then_inc(cast, 1)
            dve.tensor_copy(chunk_r[:], chunk[:]).then_inc(cast, 1)
            dve.wait_ge(cast, 3)
    return ident, ident_r, strict_r, chunk_r


def rstd_steps(dve, chain, sq_sum, width, var, rstd, tmp, var_done, root_done, root_value):
    dve.tensor_scalar(var, sq_sum, 1.0 / width, EPS, ALU.mult, ALU.add).then_inc(var_done, 1)
    dve.wait_ge(root_done, root_value)
    chain(dve.reciprocal(rstd, rstd))
    chain(dve.tensor_tensor(tmp, rstd, rstd, ALU.mult))
    chain(dve.tensor_tensor(tmp, tmp, var, ALU.mult))
    chain(dve.tensor_scalar(tmp, tmp, -0.5, 1.5, ALU.mult, ALU.add))
    chain(dve.tensor_tensor(rstd, rstd, tmp, ALU.mult))


def build_norm(nc, c, x_sb, x_dram, gain_dram, ident, hT_hi, hT_lo):
    gain = c.sb("gain", [P, KT])
    junk = c.sb("junk", [P, D])
    sq_sum, var, rstd, tmp = (c.sb(n, [P, TT]) for n in ("sq_sum", "var", "rstd", "tmp"))
    banks = c.psum("banks", [P, 4, BANK])
    x_in = [c.sem(f"x_in{t}") for t in range(TT)]
    gain_in, squared, var_done, root_done, linked, scaled, turned, hi_done, lo_done = (
        c.sem(n) for n in ("gain_in", "squared", "var_done", "root_done", "linked", "scaled",
                           "turned", "hi_done", "lo_done"))
    groups = [(half, kt) for half in range(HALVES) for kt in range(KT)]
    with nc.Block() as block:

        @block.sync
        def _(sp):
            if x_dram is not None:
                for t in range(TT):
                    sp.dma_start(x_sb[:, t, :], x_dram[t * P:(t + 1) * P, :]).then_inc(x_in[t], 16)
            sp.dma_start(gain[:], gain_dram.rearrange("(k p) -> p k", p=P),
                         allow_slow_non_contiguous=True).then_inc(gain_in, 16)

        @block.scalar
        def _(act):
            for half in range(HALVES):
                for t in range(half * QG, (half + 1) * QG):
                    if x_dram is not None:
                        act.wait_ge(x_in[t], 16)
                    if t:
                        act.wait_ge(squared, t)
                    act.activation(junk[:], x_sb[:, t, :], ACT.Square,
                                   accum_out=sq_sum[:, t:t + 1]).then_inc(squared, 1)
                act.wait_ge(var_done, half + 1)
                act.activation(rstd[:, half * QG:(half + 1) * QG], var[:, half * QG:(half + 1) * QG],
                               ACT.Sqrt).then_inc(root_done, 1)
            act.wait_ge(gain_in, 16)
            for n, (half, kt) in enumerate(groups):
                act.wait_ge(turned, n + 1)
                act.activation(hT_hi[:, kt, half * BANK:(half + 1) * BANK], banks[:, n % 4, :],
                               ACT.Copy, scale=gain[:, kt:kt + 1]).then_inc(hi_done, 1)

        @block.vector
        def _(dve):
            count = [0]

            def chain(ins):
                count[0] += 1
                ins.then_inc(linked, 1)
                dve.wait_ge(linked, count[0])

            for half in range(HALVES):
                cols = slice(half * QG, (half + 1) * QG)
                dve.wait_ge(squared, (half + 1) * QG)
                rstd_steps(dve, chain, sq_sum[:, cols], D, var[:, cols], rstd[:, cols],
                           tmp[:, cols], var_done, root_done, half + 1)
                for t in range(half * QG, (half + 1) * QG):
                    dve.tensor_scalar(x_sb[:, t, :], x_sb[:, t, :], rstd[:, t:t + 1], None,
                                      ALU.mult).then_inc(scaled, 1)
            dve.wait_ge(gain_in, 16)
            for n, (half, kt) in enumerate(groups):
                dve.wait_ge(hi_done, n + 1)
                cols = slice(half * BANK, (half + 1) * BANK)
                dve.scalar_tensor_tensor(hT_lo[:, kt, cols], banks[:, n % 4, :], gain[:, kt:kt + 1],
                                         hT_hi[:, kt, cols].bitcast(F32), ALU.mult,
                                         ALU.subtract).then_inc(lo_done, 1)
            dve.wait_ge(lo_done, len(groups))

        @block.tensor
        def _(pe):
            for n, (half, kt) in enumerate(groups):
                if kt == 0:
                    pe.wait_ge(scaled, (half + 1) * QG)
                at_least(pe, lo_done, n - 3)
                for q in range(QG):
                    mm = pe.transpose(banks[:, n % 4, q * P:(q + 1) * P],
                                      x_sb[:, half * QG + q, kt * P:(kt + 1) * P], ident[:])
                mm.then_inc(turned, 1)


def build_stick_heads(nc, c, w_in, ident, ident_r, strict_r, hT_hi, hT_lo, og_dram):
    KEY, VAL, QRY, GATE = range(4)
    PART = {QRY: 0, KEY: 1, VAL: 2, GATE: 3}
    SLOT = {KEY: 0, VAL: 1, QRY: 2, GATE: 1}
    UNITS = 4
    PLAN = ((KEY, 0), (KEY, 1), (VAL, 0), (VAL, 1), (QRY, 0), (GATE, 0), (QRY, 1), (GATE, 1))
    STEP_OF = {what: v for v, what in enumerate(PLAN)}
    AHEAD = 2
    PROJ = UNITS * HALVES
    HI_EVACS = 6

    w_raw = c.sb("w_raw", [P, 2, KT, P])
    w_hi = c.sb("w_hi", [P, 3, KT, P], F32R)
    w_lo = c.sb("w_lo", [P, 3, KT, P], F32R)
    q_hi, q_lo = c.sb("q_hi", [P, TOK], F32R), c.sb("q_lo", [P, TOK], F32R)
    k_hi, k_lo = c.sb("k_hi", [P, 2 * TOK], F32R), c.sb("k_lo", [P, 2 * TOK], F32R)
    v_cols = c.sb("v_cols", [P, TOK])
    v_hi, v_lo = c.sb("v_hi", [P, TT, HD], F32R), c.sb("v_lo", [P, TT, HD], F32R)
    gate = c.sb("gate", [P, 2 * TOK])
    skip = c.sb("skip", [P, 2, TOK])
    take = c.sb("take", [P, 2, TOK])
    wT_hi = c.sb("wT_hi", [P, TT, BANK], F32R)
    wT_lo = c.sb("wT_lo", [P, TT, BANK], F32R)
    og = c.sb("og", [P, HALVES, BANK])
    zero = c.sb("zero", [P, 1])

    pj = c.psum("pj", [P, 2, BANK])
    z = c.psum("z", [P, TOK])
    wT = c.psum("wT", [P, TT, P])
    vT = c.psum("vT", [P, QG, P])
    pv = c.psum("pv", [P, BANK])

    w_in_s = [c.sem(f"w_in{s}") for s in range(2)]
    og_out = [c.sem(f"og_out{s}") for s in range(HALVES)]
    (w_split, proj_done, proj_hi, proj_free, z_done, skip_done, take_done, scan_done, w_done,
     wT_done, wT_hi_done, wT_lo_done, vT_done, vT_hi_done, vT_lo_done, pv_done, og_done,
     zeroed) = (c.sem(n) for n in (
         "w_split", "proj_done", "proj_hi", "proj_free", "z_done", "skip_done", "take_done",
         "scan_done", "w_done", "wT_done", "wT_hi_done", "wT_lo_done", "vT_done", "vT_hi_done",
         "vT_lo_done", "pv_done", "og_done", "zeroed"))

    w_units = w_in.rearrange("(k p) (u h n) -> h u p k n", p=P, u=UNITS, n=HD)

    def half_cols(half):
        return slice(half * BANK, (half + 1) * BANK)

    def ahead(i, s, attend, proj):
        if s + AHEAD < TT:
            return [(i, s + AHEAD)] if attend else []
        return [(i + 1, s + AHEAD - TT)] if proj else []

    def iterations(eng, step):
        step(-1, False, True)
        step(0, True, True)
        with eng.Fori(1, HEADS - 1) as i:
            step(i, True, True)
        step(HEADS - 1, True, False)

    with nc.Block() as block:

        @block.sync
        def _(sp):
            def load(j):
                for u in range(UNITS):
                    n = UNITS * j + u
                    if u != QRY:
                        at_least(sp, w_split, 2 * (n - 1 + (u == VAL)))
                    src = w_units[bass.ds(j, 1), PART[u], :, :, :]
                    sp.dma_start(w_raw[:, u % 2, :, :], src.rearrange("h p k n -> (h p) k n"))\
                        .then_inc(w_in_s[u % 2], 16)

            def store(i, group):
                i = settled(sp, i)
                sp.wait_ge(og_done, HALVES * i + group + 1)
                dst = og_dram[bass.ds(i, 1), :, half_cols(group)].rearrange("h p n -> (h p) n")
                sp.dma_start(dst, og[:, group, :]).then_inc(og_out[group], 16)

            load(0)
            load(1)
            store(0, 0)
            with sp.Fori(2, HEADS) as j:
                load(j)
                store(j - 2, 1)
                store(j - 1, 0)
            store(HEADS - 2, 1)
            store(HEADS - 1, 0)
            store(HEADS - 1, 1)
            for group in range(HALVES):
                sp.wait_ge(og_out[group], 16 * HEADS)

        @block.gpsimd
        def _(pool):
            def split(j):
                for u in range(UNITS):
                    n = UNITS * j + u
                    pool.wait_ge(w_in_s[u % 2], 16 * (2 * j + u // 2 + 1))
                    before, j0 = {GATE: (VAL, j), VAL: (GATE, j - 1)}.get(u, (u, j - 1))
                    at_least(pool, proj_done, PROJ * j0 + (STEP_OF[before, 1] + 1))
                    raw = w_raw[:, u % 2, :, :]
                    pool.tensor_tensor(w_hi[:, SLOT[u], :, :], raw,
                                       zero[:].unsqueeze(2).broadcast_to([P, KT, P]),
                                       ALU.add).then_inc(w_split, 1)
                    pool.wait_ge(w_split, 2 * n + 1)
                    pool.tensor_tensor(w_lo[:, SLOT[u], :, :], w_raw[:, u % 2, :, :],
                                       w_hi[:, SLOT[u], :, :].bitcast(F32),
                                       ALU.subtract).then_inc(w_split, 1)

            pool.wait_ge(zeroed, 1)
            split(0)
            with pool.Fori(1, HEADS) as j:
                split(j)

        @block.tensor
        def _(pe):
            def project(j, v):
                m = PROJ * j + v
                u, half = PLAN[v]
                at_least(pe, w_split, 2 * (UNITS * j + u + 1))
                at_least(pe, proj_free, m - 1)
                for kt in range(KT):
                    for n, (w, h) in enumerate(products(w_hi, w_lo, hT_hi, hT_lo)):
                        mm = pe.matmul(pj[:, v % 2, :], w[:, SLOT[u], kt, :],
                                       h[:, kt, half_cols(half)], start=(kt == 0 and n == 0),
                                       stop=(kt == KT - 1 and n == 2))
                mm.then_inc(proj_done, 1)

            def scores(i, s):
                need = STEP_OF[QRY, s // QG] + 1
                at_least(pe, proj_free, PROJ * i + need)
                at_least(pe, take_done, TT * i + s)
                n_keys = (s + 1) * P
                queries = slice(s * P, (s + 1) * P)
                for c0 in range(0, n_keys, BANK):
                    width = min(BANK, n_keys - c0)
                    last = c0 + width == n_keys
                    for n, (q, k) in enumerate(products(q_hi, q_lo, k_hi, k_lo)):
                        mm = pe.matmul(z[:, c0:c0 + width], q[:, queries],
                                       k[:, bass.ds((i % 2) * TOK + c0, width)],
                                       start=(n == 0), stop=(n == 2 and not last))
                    if last:
                        mm = pe.matmul(z[:, s * P:(s + 1) * P], ident_r[:], strict_r[:],
                                       start=False, stop=True)
                mm.then_inc(z_done, 1)

            def turn_weights(i, s):
                pe.wait_ge(w_done, TT * i + s + 1)
                at_least(pe, wT_lo_done, TT * i + s)
                for kb in range(s + 1):
                    mm = pe.transpose(wT[:, kb, :], take[:, s % 2, kb * P:(kb + 1) * P], ident[:])
                mm.then_inc(wT_done, 1)

            def turn_values(i, half):
                pe.wait_ge(proj_free, PROJ * i + (STEP_OF[VAL, half] + 1))
                at_least(pe, vT_lo_done, HALVES * i + half)
                for b in range(QG):
                    t = half * QG + b
                    mm = pe.transpose(vT[:, b, :], v_cols[:, t * P:(t + 1) * P], ident[:])
                mm.then_inc(vT_done, 1)

            def mix(i, group):
                pe.wait_ge(wT_lo_done, TT * i + QG * (group + 1))
                pe.wait_ge(vT_lo_done, HALVES * i + group + 1)
                at_least(pe, og_done, HALVES * i + group)
                blocks = QG * (group + 1)
                for kb in range(blocks):
                    q0 = max(kb - QG * group, 0) * P
                    for n, (v, w) in enumerate(products(v_hi, v_lo, wT_hi, wT_lo)):
                        mm = pe.matmul(pv[:, q0:BANK], v[:, kb, :], w[:, kb, q0:BANK],
                                       start=(kb == 0 and n == 0),
                                       stop=(kb == blocks - 1 and n == 2))
                mm.then_inc(pv_done, 1)

            def step(i, attend, proj):
                for s in range(TT):
                    if attend:
                        if s == 0 and not (isinstance(i, int) and i == 0):
                            mix(i - 1, 1)
                        if s == QG:
                            mix(i, 0)
                        turn_weights(i, s)
                    for head, block_ in ahead(i, s, attend, proj):
                        scores(head, block_)
                    if proj:
                        project(i + 1, s)
                    if attend and s < HALVES:
                        turn_values(i, s)

            iterations(pe, step)
            mix(HEADS - 1, 1)

        @block.scalar
        def _(act):
            def project_hi(j, v):
                u, half = PLAN[v]
                if u == VAL:
                    return
                act.wait_ge(proj_done, PROJ * j + v + 1)
                bank = pj[:, v % 2, :]
                if u == GATE:
                    at_least(act, og_done, HALVES * (j - 2) + half + 1)
                    act.activation(gate[:, bass.ds((j % 2) * TOK + half * BANK, BANK)], bank,
                                   ACT.Sigmoid).then_inc(proj_hi, 1)
                elif u == KEY:
                    act.activation(k_hi[:, bass.ds((j % 2) * TOK + half * BANK, BANK)], bank,
                                   ACT.Copy).then_inc(proj_hi, 1)
                else:
                    act.activation(q_hi[:, half_cols(half)], bank, ACT.Copy,
                                   scale=STICK_SCALE).then_inc(proj_hi, 1)

            def sigmoids(i, s):
                n_keys = (s + 1) * P
                act.wait_ge(z_done, TT * i + s + 1)
                at_least(act, wT_done, TT * i + s - 1)
                act.activation(skip[:, s % 2, 0:n_keys], z[:, 0:n_keys], ACT.Sigmoid,
                               scale=-1.0).then_inc(skip_done, 1)
                act.activation(take[:, s % 2, 0:n_keys], z[:, 0:n_keys],
                               ACT.Sigmoid).then_inc(take_done, 1)

            def values_hi(i, half):
                act.wait_ge(vT_done, HALVES * i + half + 1)
                act.activation(v_hi[:, half * QG:(half + 1) * QG, :], vT[:],
                               ACT.Copy).then_inc(vT_hi_done, 1)

            def weights_hi(i, s):
                act.wait_ge(wT_done, TT * i + s + 1)
                q0 = (s % QG) * P
                act.activation(wT_hi[:, 0:s + 1, q0:q0 + P], wT[:, 0:s + 1, :],
                               ACT.Copy).then_inc(wT_hi_done, 1)

            def step(i, attend, proj):
                for s in range(TT):
                    if attend:
                        weights_hi(i, s)
                    for head, block_ in ahead(i, s, attend, proj):
                        sigmoids(head, block_)
                    if proj:
                        project_hi(i + 1, s)
                    if attend and s < HALVES:
                        values_hi(i, s)

            iterations(act, step)

        @block.vector
        def _(dve):
            def project_lo(j, v):
                u, half = PLAN[v]
                bank = pj[:, v % 2, :]
                if u == VAL:
                    dve.wait_ge(proj_done, PROJ * j + v + 1)
                    dve.tensor_copy(v_cols[:, half_cols(half)], bank).then_inc(proj_free, 1)
                    return
                order = sum(w != VAL for w, _ in PLAN[:v + 1])
                dve.wait_ge(proj_hi, HI_EVACS * j + order)
                if u == GATE:
                    cols = bass.ds((j % 2) * TOK + half * BANK, BANK)
                    dve.tensor_tensor(gate[:, cols], bank, gate[:, cols],
                                      ALU.mult).then_inc(proj_free, 1)
                elif u == KEY:
                    cols = bass.ds((j % 2) * TOK + half * BANK, BANK)
                    dve.tensor_tensor(k_lo[:, cols], bank, k_hi[:, cols].bitcast(F32),
                                      ALU.subtract).then_inc(proj_free, 1)
                else:
                    cols = half_cols(half)
                    dve.scalar_tensor_tensor(q_lo[:, cols], bank, STICK_SCALE,
                                             q_hi[:, cols].bitcast(F32), ALU.mult,
                                             ALU.subtract).then_inc(proj_free, 1)

            def weights(i, s):
                n_keys = (s + 1) * P
                dve.wait_ge(skip_done, TT * i + s + 1)
                from_last = skip[:, s % 2, 0:n_keys][:, ::-1]
                dve.tensor_tensor_scan(from_last, from_last, zero[:].broadcast_to([P, n_keys]),
                                       1.0, ALU.mult, ALU.add).then_inc(scan_done, 1)
                dve.wait_ge(scan_done, TT * i + s + 1)
                dve.wait_ge(take_done, TT * i + s + 1)
                dve.tensor_tensor(take[:, s % 2, 0:n_keys - 1], take[:, s % 2, 0:n_keys - 1],
                                  skip[:, s % 2, 1:n_keys], ALU.mult).then_inc(w_done, 1)

            def values_lo(i, half):
                tiles = slice(half * QG, (half + 1) * QG)
                dve.wait_ge(vT_hi_done, HALVES * i + half + 1)
                dve.tensor_tensor(v_lo[:, tiles, :], vT[:], v_hi[:, tiles, :].bitcast(F32),
                                  ALU.subtract).then_inc(vT_lo_done, 1)

            def weights_lo(i, s):
                q0 = (s % QG) * P
                dve.wait_ge(wT_hi_done, TT * i + s + 1)
                dve.tensor_tensor(wT_lo[:, 0:s + 1, q0:q0 + P], wT[:, 0:s + 1, :],
                                  wT_hi[:, 0:s + 1, q0:q0 + P].bitcast(F32),
                                  ALU.subtract).then_inc(wT_lo_done, 1)

            def gated(i, group):
                dve.wait_ge(pv_done, HALVES * i + group + 1)
                at_least(dve, og_out[group], 16 * i)
                dve.tensor_tensor(og[:, group, :], pv[:],
                                  gate[:, bass.ds((i % 2) * TOK + group * BANK, BANK)],
                                  ALU.mult).then_inc(og_done, 1)

            def step(i, attend, proj):
                for s in range(TT):
                    if attend:
                        if s == 0 and not (isinstance(i, int) and i == 0):
                            gated(i - 1, 1)
                        if s == QG:
                            gated(i, 0)
                        weights_lo(i, s)
                    for head, block_ in ahead(i, s, attend, proj):
                        weights(head, block_)
                    if proj:
                        project_lo(i + 1, s)
                    if attend and s < HALVES:
                        values_lo(i, s)

            dve.memset(zero[:], 0.0).then_inc(zeroed, 1)
            dve.wait_ge(zeroed, 1)
            iterations(dve, step)
            gated(HEADS - 1, 1)


def build_out(nc, c, w_out, og_dram, x_dram, x_sb, x_save, final_gain, out_dram):
    w_raw = c.sb("w_raw", [P, 2, D])
    w_hi, w_lo = c.sb("w_hi", [P, 2, D], F32R), c.sb("w_lo", [P, 2, D], F32R)
    og_raw = c.sb("og_raw", [P, 2, BANK])
    og_hi, og_lo = c.sb("og_hi", [P, 2, BANK], F32R), c.sb("og_lo", [P, 2, BANK], F32R)
    y = c.psum("y", [P, QG, 2, BANK])
    raw_in = [c.sem(f"raw_in{s}") for s in range(2)]
    x_in, hi_done, og_lo_done, w_lo_done, mm_done, added, saved = (
        c.sem(n) for n in ("x_in", "hi_done", "og_lo_done", "w_lo_done", "mm_done", "added",
                           "saved"))
    final = final_gain is not None
    if final:
        gain = c.sb("gain", [P, D])
        junk = c.sb("junk", [P, D])
        sq_sum, var, rstd, tmp = (c.sb(n, [P, TT]) for n in ("sq_sum", "var", "rstd", "tmp"))
        gain_in, squared, var_done, root_done, linked = (
            c.sem(n) for n in ("gain_in", "squared", "var_done", "root_done", "linked"))
    normed = c.sem("normed")

    def pairs(eng, half, work):
        for k in range(2):
            work(half * HEADS + k, k, k == 0, False)
        with eng.Fori(1, HEADS // 2 - 1) as pair:
            for k in range(2):
                work(pair * 2 + (half * HEADS + k), k, False, False)
        for k in range(2):
            work(half * HEADS + HEADS - 2 + k, k, False, k == 1)

    with nc.Block() as block:

        @block.sync
        def _(sp):
            def load(half):
                def work(n, slot, first, last):
                    h = settled(sp, n - half * HEADS)
                    at_least(sp, og_lo_done, n - 1)
                    at_least(sp, w_lo_done, n - 1)
                    sp.dma_start(og_raw[:, slot, :],
                                 og_dram[bass.ds(h, 1), :, half * BANK:(half + 1) * BANK]
                                 .rearrange("h p n -> (h p) n")).then_inc(raw_in[slot], 16)
                    sp.dma_start(w_raw[:, slot, :],
                                 w_out[bass.ds(h * HD, HD), :]).then_inc(raw_in[slot], 16)
                return work

            for half in range(HALVES):
                pairs(sp, half, load(half))

        @block.gpsimd
        def _(pool):
            def work(n, slot, first, last):
                pool.wait_ge(hi_done, 2 * n + 2)
                at_least(pool, mm_done, n - 1)
                pool.tensor_tensor(w_lo[:, slot, :], w_raw[:, slot, :],
                                   w_hi[:, slot, :].bitcast(F32), ALU.subtract).then_inc(w_lo_done, 1)

            for t in range(TT):
                pool.dma_start(x_sb[:, t, :], x_dram[t * P:(t + 1) * P, :]).then_inc(x_in, 16)
            if final:
                pool.dma_start(gain[:], final_gain.rearrange("(a n) -> a n", a=1)
                               .broadcast_to([P, D])).then_inc(gain_in, 16)
            for half in range(HALVES):
                pairs(pool, half, work)

        @block.scalar
        def _(act):
            def work(n, slot, first, last):
                act.wait_ge(raw_in[slot], n * 16 + (32 - slot * 16))
                at_least(act, mm_done, n - 1)
                act.activation(og_hi[:, slot, :], og_raw[:, slot, :], ACT.Copy).then_inc(hi_done, 1)
                act.activation(w_hi[:, slot, :], w_raw[:, slot, :], ACT.Copy).then_inc(hi_done, 1)

            for half in range(HALVES):
                pairs(act, half, work)
            if final:
                for half in range(HALVES):
                    for t in range(half * QG, (half + 1) * QG):
                        act.wait_ge(added, 2 * t + 2)
                        if t:
                            act.wait_ge(squared, t)
                        act.activation(junk[:], x_sb[:, t, :], ACT.Square,
                                       accum_out=sq_sum[:, t:t + 1]).then_inc(squared, 1)
                    act.wait_ge(var_done, half + 1)
                    act.activation(rstd[:, half * QG:(half + 1) * QG],
                                   var[:, half * QG:(half + 1) * QG],
                                   ACT.Sqrt).then_inc(root_done, 1)
            else:
                for t in range(TT):
                    act.wait_ge(added, 2 * t + 2)
                    act.dma_start(x_save[t * P:(t + 1) * P, :], x_sb[:, t, :]).then_inc(saved, 16)
                act.wait_ge(saved, 16 * TT)

        @block.vector
        def _(dve):
            count = [0]

            def chain(ins):
                count[0] += 1
                ins.then_inc(linked, 1)
                dve.wait_ge(linked, count[0])

            def work(n, slot, first, last):
                dve.wait_ge(hi_done, 2 * n + 1)
                at_least(dve, mm_done, n - 1)
                dve.tensor_tensor(og_lo[:, slot, :], og_raw[:, slot, :],
                                  og_hi[:, slot, :].bitcast(F32), ALU.subtract).then_inc(og_lo_done, 1)

            for half in range(HALVES):
                pairs(dve, half, work)
                dve.wait_ge(mm_done, HEADS * (half + 1))
                if half == 0:
                    dve.wait_ge(x_in, 16 * TT)
                for b in range(QG):
                    for n in range(2):
                        cols = slice(n * BANK, (n + 1) * BANK)
                        t = half * QG + b
                        dve.tensor_tensor(x_sb[:, t, cols], y[:, b, n, :], x_sb[:, t, cols],
                                          ALU.add).then_inc(added, 1)
            if final:
                dve.wait_ge(gain_in, 16)
                for half in range(HALVES):
                    cols = slice(half * QG, (half + 1) * QG)
                    dve.wait_ge(squared, (half + 1) * QG)
                    rstd_steps(dve, chain, sq_sum[:, cols], D, var[:, cols], rstd[:, cols],
                               tmp[:, cols], var_done, root_done, half + 1)
                    for t in range(half * QG, (half + 1) * QG):
                        dve.scalar_tensor_tensor(x_sb[:, t, :], x_sb[:, t, :], rstd[:, t:t + 1],
                                                 gain[:], ALU.mult, ALU.mult).then_inc(normed, 1)
                for t in range(TT):
                    dve.wait_ge(normed, t + 1)

        @block.tensor
        def _(pe):
            def work(n, slot, first, last):
                pe.wait_ge(og_lo_done, n + 1)
                pe.wait_ge(w_lo_done, n + 1)
                for b in range(QG):
                    for col in range(2):
                        if first and not (isinstance(n, int) and n == 0):
                            pe.wait_ge(added, 2 * b + col + 1)
                        for k, (o, w) in enumerate(products(og_hi, og_lo, w_hi, w_lo)):
                            mm = pe.matmul(y[:, b, col, :], o[:, slot, b * P:(b + 1) * P],
                                           w[:, slot, col * BANK:(col + 1) * BANK],
                                           start=(first and k == 0), stop=(last and k == 2))
                mm.then_inc(mm_done, 1)

            for half in range(HALVES):
                pairs(pe, half, work)

    if final:
        stored = c.sem("stored")
        with nc.Block() as block:

            @block.sync
            def _(sp):
                for t in range(TT):
                    sp.dma_start(out_dram[t * P:(t + 1) * P, :], x_sb[:, t, :]).then_inc(stored, 16)
                sp.wait_ge(stored, 16 * TT)


def build_latents(nc, c, w_in, positions, inv_freq, q_norm, kv_norm, w_qb, ident, hT_hi, hT_lo,
                  qn_hi, qn_lo, kvn_hi, kvn_lo, kr_hi, kr_lo, qr_dram):
    GROUPS = 2
    GH = HEADS // GROUPS
    LAT_T = QKT + 1

    wl_raw = c.sb("wl_raw", [P, KT, LAT])
    wl_hi, wl_lo = c.sb("wl_hi", [P, KT, LAT], F32R), c.sb("wl_lo", [P, KT, LAT], F32R)
    wr_raw = c.sb("wr_raw", [P, QKT, HEADS, ROPE])
    wr_hi = c.sb("wr_hi", [P, QKT, HEADS, ROPE], F32R)
    wr_lo = c.sb("wr_lo", [P, QKT, HEADS, ROPE], F32R)
    lat = c.sb("lat", [P, TT, LAT])
    junk = c.sb("junk", [P, Q_RANK])
    sq_sum, var, rstd, tmp = (c.sb(n, [P, 2 * TT]) for n in ("sq_sum", "var", "rstd", "tmp"))
    gain = c.sb("gain", [P, LAT_T])
    pos_i = c.sb("pos_i", [P, TT], I32)
    pos = c.sb("pos", [P, TT])
    freq = c.sb("freq", [P, HALF_ROPE])
    ang, turns, part = (c.sb(n, [P, TT, HALF_ROPE]) for n in ("ang", "turns", "part"))
    t_hi, t_lo = (c.sb(n, [P, TT, HALF_ROPE], F32R) for n in ("t_hi", "t_lo"))
    cos2, sin2 = (c.sb(n, [P, TT, 2, HALF_ROPE]) for n in ("cos2", "sin2"))
    qx = c.sb("qx", [P, 2, GH, 2, HALF_ROPE])
    qc, qs = (c.sb(n, [P, 2, GH, 2, HALF_ROPE]) for n in ("qc", "qs"))
    qr = c.sb("qr", [P, 2, GH, 2, HALF_ROPE])
    kc, ks = qc[:, 0, :, :, :], qs[:, 0, :, :, :]
    kr = qr[:].rearrange("p s h a r -> p (s h a r)").rearrange("p (t a r) -> p t a r", t=TT, a=2)
    assert GH == TT
    banks = c.psum("banks", [P, 8, BANK])

    (in_w, in_wr, in_small, in_gain, wl_hi_done, wl_lo_done, wr_done, mm_done, lat_done, squared,
     var_done, root_done, linked, scaled, angles, trig, turned, hi_done, lo_done, rotated_k,
     q_mm, q_x, q_mul, q_rot, q_out0, q_out1, pooled) = (c.sem(n) for n in (
         "in_w", "in_wr", "in_small", "in_gain", "wl_hi_done", "wl_lo_done", "wr_done", "mm_done",
         "lat_done", "squared", "var_done", "root_done", "linked", "scaled", "angles", "trig",
         "turned", "hi_done", "lo_done", "rotated_k", "q_mm", "q_x", "q_mul", "q_rot", "q_out0",
         "q_out1", "pooled"))
    q_out = [q_out0, q_out1]

    import math
    two_pi = 2.0 * math.pi
    c1 = math.floor(two_pi * 2 ** 9) / 2 ** 9
    c2 = math.floor((two_pi - c1) * 2 ** 21) / 2 ** 21
    c3 = two_pi - c1 - c2
    ROUND = 1.5 * 2 ** 23

    turns_of = [(u, half) for u in range(LAT_T + 1) for half in range(HALVES)]
    units = [(t, g) for t in range(TT) for g in range(GROUPS)]
    KEY_BANKS = 4

    with nc.Block() as block:

        @block.sync
        def _(sp):
            sp.dma_start(wl_raw[:], w_in.rearrange("(k p) n -> p k n", p=P)[:, :, 0:LAT])\
                .then_inc(in_w, 16)
            sp.dma_start(pos_i[:], positions.rearrange("b (t p) -> p (b t)", p=P),
                         allow_slow_non_contiguous=True)\
                .then_inc(in_small, 16)
            sp.dma_start(freq[:], inv_freq.broadcast_to([P, HALF_ROPE])).then_inc(in_small, 16)
            sp.dma_start(gain[:, 0:QKT], q_norm.rearrange("(k p) -> p k", p=P),
                         allow_slow_non_contiguous=True).then_inc(in_gain, 16)
            sp.dma_start(gain[:, QKT:LAT_T], kv_norm.rearrange("(k p) -> p k", p=P),
                         allow_slow_non_contiguous=True)\
                .then_inc(in_gain, 16)
            for k in range(QKT):
                src = w_qb[k * P:(k + 1) * P, :].rearrange("p (h n) -> p h n", h=HEADS)
                sp.dma_start(wr_raw[:, k, :, :], src[:, :, NOPE:NOPE + ROPE]).then_inc(in_wr, 16)
            for n, (t, g) in enumerate(units):
                sp.wait_ge(q_rot, 2 * (n + 1))
                sp.dma_start(qr_dram[t * P:(t + 1) * P, g * GH * ROPE:(g + 1) * GH * ROPE],
                             qr[:, n % 2, :, :, :].rearrange("p h a r -> p (h a r)"))\
                    .then_inc(q_out[n % 2], 16)
            for s in range(2):
                sp.wait_ge(q_out[s], 16 * len(units) // 2)

        @block.gpsimd
        def _(pool):
            for kt in range(KT):
                pool.wait_ge(wl_hi_done, kt + 1)
                pool.tensor_tensor(wl_lo[:, kt, :], wl_raw[:, kt, :], wl_hi[:, kt, :].bitcast(F32),
                                   ALU.subtract).then_inc(wl_lo_done, 1)
            for k in range(QKT):
                pool.wait_ge(wr_done, k + 1)
                pool.tensor_tensor(wr_lo[:, k, :, :], wr_raw[:, k, :, :],
                                   wr_hi[:, k, :, :].bitcast(F32), ALU.subtract).then_inc(pooled, 1)
            for n in range(len(units)):
                pool.wait_ge(q_mul, 2 * (n + 1))
                if n >= 2:
                    pool.wait_ge(q_out[n % 2], 16 * (n // 2))
                s = n % 2
                pool.tensor_tensor(qr[:, s, :, 0, :], qc[:, s, :, 0, :], qs[:, s, :, 1, :],
                                   ALU.subtract).then_inc(q_rot, 1)
                pool.tensor_tensor(qr[:, s, :, 1, :], qs[:, s, :, 0, :], qc[:, s, :, 1, :],
                                   ALU.add).then_inc(q_rot, 1)

        @block.tensor
        def _(pe):
            for t in range(TT):
                at_least(pe, squared, 2 * (t - KEY_BANKS + 1))
                for kt in range(KT):
                    if t == 0:
                        pe.wait_ge(wl_lo_done, kt + 1)
                    for n, (h, w) in enumerate(products(hT_hi, hT_lo, wl_hi, wl_lo)):
                        mm = pe.matmul(banks[:, t % KEY_BANKS, 0:LAT], h[:, kt, t * P:(t + 1) * P],
                                       w[:, kt, :], start=(kt == 0 and n == 0),
                                       stop=(kt == KT - 1 and n == 2))
                mm.then_inc(mm_done, 1)
            pe.wait_ge(squared, 2 * TT)
            for n, (u, half) in enumerate(turns_of):
                if u == 0 and half == 0:
                    pe.wait_ge(scaled, 2 * TT)
                if u == LAT_T and half == 0:
                    pe.wait_ge(rotated_k, 4)
                at_least(pe, lo_done, n - KEY_BANKS + 1)
                for b in range(QG):
                    t = half * QG + b
                    src = lat[:, t, u * P:(u + 1) * P] if u < LAT_T else \
                        kr[:, t, :, :].rearrange("p a r -> p (a r)")
                    mm = pe.transpose(banks[:, n % KEY_BANKS, b * P:(b + 1) * P], src, ident[:])
                mm.then_inc(turned, 1)
            pe.wait_ge(lo_done, QKT * HALVES)
            pe.wait_ge(pooled, QKT)
            for n, (t, g) in enumerate(units):
                at_least(pe, q_x, n - 3)
                for k in range(QKT):
                    for m, (h, w) in enumerate(products(qn_hi, qn_lo, wr_hi, wr_lo)):
                        mm = pe.matmul(banks[:, KEY_BANKS + n % 4, :], h[:, k, t * P:(t + 1) * P],
                                       w[:, k, g * GH:(g + 1) * GH, :]
                                       .rearrange("p h r -> p (h r)"),
                                       start=(k == 0 and m == 0), stop=(k == QKT - 1 and m == 2))
                mm.then_inc(q_mm, 1)

        @block.scalar
        def _(act):
            for t in range(TT):
                act.wait_ge(mm_done, t + 1)
                bank = banks[:, t % KEY_BANKS, :]
                act.activation(lat[:, t, :], bank[:, 0:LAT], ACT.Copy).then_inc(lat_done, 1)
                if t:
                    act.wait_ge(squared, 2 * t)
                act.activation(junk[:], bank[:, 0:Q_RANK], ACT.Square,
                               accum_out=sq_sum[:, t:t + 1]).then_inc(squared, 1)
                act.wait_ge(squared, 2 * t + 1)
                act.activation(junk[:, 0:KV_RANK], bank[:, Q_RANK:Q_RANK + KV_RANK], ACT.Square,
                               accum_out=sq_sum[:, TT + t:TT + t + 1]).then_inc(squared, 1)
            act.wait_ge(var_done, 2)
            act.activation(rstd[:], var[:], ACT.Sqrt).then_inc(root_done, 1)
            act.wait_ge(angles, 2)
            for a in range(2):
                act.activation(sin2[:, :, a, :], ang[:], ACT.Sin).then_inc(trig, 1)
                act.activation(cos2[:, :, a, :], part[:], ACT.Sin).then_inc(trig, 1)
            act.wait_ge(in_gain, 32)
            for n, (u, half) in enumerate(turns_of):
                act.wait_ge(turned, n + 1)
                cols = slice(half * BANK, (half + 1) * BANK)
                bank = banks[:, n % KEY_BANKS, :]
                if u < QKT:
                    ins = act.activation(qn_hi[:, u, cols], bank, ACT.Copy, scale=gain[:, u:u + 1])
                elif u < LAT_T:
                    ins = act.activation(kvn_hi[:, cols], bank, ACT.Copy, scale=gain[:, u:u + 1])
                else:
                    ins = act.activation(kr_hi[:, cols], bank, ACT.Copy)
                ins.then_inc(hi_done, 1)
            for n in range(len(units)):
                act.wait_ge(q_mm, n + 1)
                at_least(act, q_mul, 2 * (n - 1))
                act.activation(qx[:, n % 2, :, :, :].rearrange("p h a r -> p (h a r)"),
                               banks[:, KEY_BANKS + n % 4, :], ACT.Copy).then_inc(q_x, 1)

        @block.vector
        def _(dve):
            count = [0]

            def chain(ins):
                count[0] += 1
                ins.then_inc(linked, 1)
                dve.wait_ge(linked, count[0])

            def reduce_angle():
                chain(dve.tensor_scalar(turns[:], ang[:], 1.0 / two_pi, ROUND, ALU.mult, ALU.add))
                chain(dve.tensor_scalar(turns[:], turns[:], -ROUND, None, ALU.add))
                chain(dve.tensor_copy(t_hi[:], turns[:]))
                chain(dve.tensor_tensor(t_lo[:], turns[:], t_hi[:].bitcast(F32), ALU.subtract))
                for const in (c1, c2, c3):
                    for t in (t_hi, t_lo):
                        chain(dve.scalar_tensor_tensor(ang[:], t[:].bitcast(F32), -const, ang[:],
                                                       ALU.mult, ALU.add))

            dve.wait_ge(in_w, 16)
            for kt in range(KT):
                dve.tensor_copy(wl_hi[:, kt, :], wl_raw[:, kt, :]).then_inc(wl_hi_done, 1)
            dve.wait_ge(in_wr, 16 * QKT)
            for k in range(QKT):
                dve.tensor_copy(wr_hi[:, k, :, :], wr_raw[:, k, :, :]).then_inc(wr_done, 1)
            dve.wait_ge(in_small, 32)
            chain(dve.tensor_copy(pos[:], pos_i[:]))
            chain(dve.tensor_tensor(ang[:], pos[:].unsqueeze(2).broadcast_to([P, TT, HALF_ROPE]),
                                    freq[:].unsqueeze(1).broadcast_to([P, TT, HALF_ROPE]),
                                    ALU.mult))
            reduce_angle()
            reduce_angle()
            chain(dve.tensor_scalar(part[:], ang[:], math.pi / 2, None, ALU.add))
            chain(dve.tensor_scalar(turns[:], part[:], math.pi, -two_pi, ALU.is_gt, ALU.mult))
            chain(dve.tensor_tensor(part[:], part[:], turns[:], ALU.add))
            PI_BELOW = 3.1415925
            dve.tensor_scalar(part[:], part[:], PI_BELOW, -PI_BELOW, ALU.min, ALU.max)\
                .then_inc(angles, 1)
            dve.tensor_scalar(ang[:], ang[:], PI_BELOW, -PI_BELOW, ALU.min, ALU.max)\
                .then_inc(angles, 1)

            dve.wait_ge(squared, 2 * TT)
            dve.tensor_scalar(var[:, 0:TT], sq_sum[:, 0:TT], 1.0 / Q_RANK, EPS, ALU.mult,
                              ALU.add).then_inc(var_done, 1)
            dve.tensor_scalar(var[:, TT:], sq_sum[:, TT:], 1.0 / KV_RANK, EPS, ALU.mult,
                              ALU.add).then_inc(var_done, 1)
            dve.wait_ge(root_done, 1)
            chain(dve.reciprocal(rstd[:], rstd[:]))
            chain(dve.tensor_tensor(tmp[:], rstd[:], rstd[:], ALU.mult))
            chain(dve.tensor_tensor(tmp[:], tmp[:], var[:], ALU.mult))
            chain(dve.tensor_scalar(tmp[:], tmp[:], -0.5, 1.5, ALU.mult, ALU.add))
            chain(dve.tensor_tensor(rstd[:], rstd[:], tmp[:], ALU.mult))
            dve.wait_ge(lat_done, TT)
            for t in range(TT):
                q, kv = lat[:, t, 0:Q_RANK], lat[:, t, Q_RANK:Q_RANK + KV_RANK]
                dve.tensor_scalar(q, q, rstd[:, t:t + 1], None, ALU.mult).then_inc(scaled, 1)
                dve.tensor_scalar(kv, kv, rstd[:, TT + t:TT + t + 1], None,
                                  ALU.mult).then_inc(scaled, 1)

            dve.wait_ge(trig, 4)
            k_x = lat[:, :, Q_RANK + KV_RANK:LAT].rearrange("p t (a r) -> p t a r", a=2)
            chain(dve.tensor_tensor(kc, k_x, cos2[:], ALU.mult))
            chain(dve.tensor_tensor(ks, k_x, sin2[:], ALU.mult))
            for a in range(2):
                dve.tensor_tensor(kr[:, :, a, 0:HALF_ROPE], kc[:, :, 0, :], ks[:, :, 1, :],
                                  ALU.subtract).then_inc(rotated_k, 1)
                dve.tensor_tensor(kr[:, :, a, HALF_ROPE:ROPE], ks[:, :, 0, :], kc[:, :, 1, :],
                                  ALU.add).then_inc(rotated_k, 1)

            dve.wait_ge(in_gain, 32)
            for n, (u, half) in enumerate(turns_of):
                dve.wait_ge(hi_done, n + 1)
                cols = slice(half * BANK, (half + 1) * BANK)
                bank = banks[:, n % KEY_BANKS, :]
                if u < QKT:
                    ins = dve.scalar_tensor_tensor(qn_lo[:, u, cols], bank, gain[:, u:u + 1],
                                                   qn_hi[:, u, cols].bitcast(F32), ALU.mult,
                                                   ALU.subtract)
                elif u < LAT_T:
                    ins = dve.scalar_tensor_tensor(kvn_lo[:, cols], bank, gain[:, u:u + 1],
                                                   kvn_hi[:, cols].bitcast(F32), ALU.mult,
                                                   ALU.subtract)
                else:
                    ins = dve.tensor_tensor(kr_lo[:, cols], bank, kr_hi[:, cols].bitcast(F32),
                                            ALU.subtract)
                ins.then_inc(lo_done, 1)
            dve.wait_ge(rotated_k, 4)
            for n, (t, g) in enumerate(units):
                s = n % 2
                dve.wait_ge(q_x, n + 1)
                at_least(dve, q_rot, 2 * (n - 1))
                x = qx[:, s, :, :, :].rearrange("p h a r -> p h (a r)")
                for out, trig2 in ((qc, cos2), (qs, sin2)):
                    angle = trig2[:, t, :, :].rearrange("p a r -> p (a r)").unsqueeze(1)
                    dve.tensor_tensor(out[:, s, :, :, :].rearrange("p h a r -> p h (a r)"), x,
                                      angle.broadcast_to([P, GH, ROPE]), ALU.mult)\
                       .then_inc(q_mul, 1)
            dve.wait_ge(lo_done, len(turns_of))


def build_mla_heads(nc, c, w_in, w_qb, w_kvb, ident, ident_r, chunk_r, hT_hi, hT_lo, qn_hi, qn_lo,
                    kvn_hi, kvn_lo, kr_hi, kr_lo, qr_dram, og_dram):
    CHUNKS = ((0, 3), (3, 3), (6, 2))
    G_PARTS = len(CHUNKS)
    GATE_PART = {1: (0, 0), 2: (0, 1), 3: (0, 2), 4: (1, 0), 5: (1, 1), 6: (1, 2)}
    AHEAD = 2
    ROPE_STACK = 2 * ROPE
    assert ROPE_STACK == P

    wg_raw = c.sb("wg_raw", [P, 3, P])
    wg_hi, wg_lo = c.sb("wg_hi", [P, KT, P], F32R), c.sb("wg_lo", [P, KT, P], F32R)
    ws_raw = c.sb("ws_raw", [P, QKT + 1, P])
    ws_hi, ws_lo = c.sb("ws_hi", [P, QKT + 1, P], F32R), c.sb("ws_lo", [P, QKT + 1, P], F32R)
    wv_raw = c.sb("wv_raw", [P, HD])
    wv_hi, wv_lo = c.sb("wv_hi", [P, HD], F32R), c.sb("wv_lo", [P, HD], F32R)
    qr_in = c.sb("qr_in", [P, TT, 2, ROPE])
    qr = c.sb("qr", [P, TOK], F32R)
    q_hi, q_lo = c.sb("q_hi", [P, TOK], F32R), c.sb("q_lo", [P, TOK], F32R)
    k_hi, k_lo = c.sb("k_hi", [P, 2 * TOK], F32R), c.sb("k_lo", [P, 2 * TOK], F32R)
    v_hi, v_lo = c.sb("v_hi", [P, TT, HD], F32R), c.sb("v_lo", [P, TT, HD], F32R)
    gate = c.sb("gate", [P, HALVES, BANK])
    prob = c.sb("prob", [P, 2, TOK])
    pT_hi, pT_lo = c.sb("pT_hi", [P, TT, BANK], F32R), c.sb("pT_lo", [P, TT, BANK], F32R)
    og = c.sb("og", [P, HALVES, BANK])
    top, neg_top, total, inverse = (c.sb(n, [P, TT]) for n in ("top", "neg_top", "total",
                                                               "inverse"))
    zero = c.sb("zero", [P, 1])

    z = c.psum("z", [P, TOK])
    pT = c.psum("pT", [P, TT, P])
    small = c.psum("small", [P, 2, BANK])
    pv = c.psum("pv", [P, BANK])
    g = c.psum("g", [P, BANK])

    (wg_in, ws_in, wv_in, qr_loaded, w_split, ws_split, wv_split, g_mm, g_tanh, g_done, small_mm, small_hi, small_free, z_done, top_done, neg_done, exp_done, inv_done,
     p_done, pT_done, pT_hi_done, pT_lo_done, pv_done, og_done, og_out0, og_out1, zeroed) = (
         c.sem(n) for n in (
             "wg_in", "ws_in", "wv_in", "qr_loaded", "w_split", "ws_split", "wv_split", "g_mm",
             "g_tanh", "g_done", "small_mm", "small_hi", "small_free",
             "z_done", "top_done", "neg_done", "exp_done", "inv_done", "p_done", "pT_done",
             "pT_hi_done", "pT_lo_done", "pv_done", "og_done", "og_out0", "og_out1", "zeroed"))
    og_out = [og_out0, og_out1]

    w_cols = w_in.rearrange("(k p) n -> p k n", p=P)
    qb_cols = w_qb.rearrange("(k p) n -> p k n", p=P)
    qr_rows = qr_dram.rearrange("(t p) n -> p t n", p=P)

    USES = V0, V1, Q0, K0, R0, K1, Q1, R1 = range(8)
    HALF = {V0: 0, V1: 1, Q0: 0, K0: 0, R0: 0, K1: 1, Q1: 1, R1: 1}
    BEFORE = {6: (K1,)}
    AFTER = {1: (V0,), 2: (V1,), 3: (Q0,), 4: (K0, R0), 7: (Q1, R1)}

    def small_uses(table, s, attend, proj):
        return [n for n in table.get(s, ()) if (attend if n in (V0, V1) else proj)]

    def use(i, n):
        return i * len(USES) + (len(USES) - 2 + n + 1)

    def ahead(i, s, attend, proj):
        if s + AHEAD < TT:
            return [(i, s + AHEAD)] if attend else []
        return [(i + 1, s + AHEAD - TT)] if proj else []

    def first_bank(s):
        return s % 2 if s < QG else 0

    def blocks_before(i, s):
        return TT * i + (max(s - 1, 0) if s < QG else s)

    def half_cols(half):
        return slice(half * BANK, (half + 1) * BANK)

    def iterations(eng, step):
        step(-1, False, True)
        step(0, True, True)
        with eng.Fori(1, HEADS - 1) as i:
            step(i, True, True)
        step(HEADS - 1, True, False)

    with nc.Block() as block:

        @block.sync
        def _(sp):
            def load_small(j):
                at_least(sp, ws_split, 2 * j)
                sp.dma_start(ws_raw[:, 0:QKT, :],
                             qb_cols[:, :, bass.ds(j * (NOPE + ROPE), NOPE)]).then_inc(ws_in, 16)
                sp.dma_start(ws_raw[:, QKT, :],
                             w_kvb[:, bass.ds(j * (NOPE + HD), NOPE)]).then_inc(ws_in, 16)

            def load_gate(j, n):
                k0, count = CHUNKS[n]
                at_least(sp, w_split, 2 * (G_PARTS * j + n))
                sp.dma_start(wg_raw[:, 0:count, :],
                             w_cols[:, k0:k0 + count, bass.ds(j * HD + LAT, HD)])\
                    .then_inc(wg_in, 16)

            def load_values(j):
                at_least(sp, wv_split, 2 * j)
                sp.dma_start(wv_raw[:], w_kvb[:, bass.ds(j * (NOPE + HD) + NOPE, HD)])\
                    .then_inc(wv_in, 16)

            def load_rotated(j):
                if not (isinstance(j, int) and j == 0):
                    sp.wait_ge(small_mm, use(j - 2, R1))
                src = qr_rows[:, :, bass.ds(j * ROPE, ROPE)]
                for a in range(2):
                    sp.dma_start(qr_in[:, :, a, :], src).then_inc(qr_loaded, 16)

            def store(i, group):
                i = settled(sp, i)
                sp.wait_ge(og_done, HALVES * i + group + 1)
                dst = og_dram[bass.ds(i, 1), :, half_cols(group)].rearrange("h p n -> (h p) n")
                sp.dma_start(dst, og[:, group, :]).then_inc(og_out[group], 16)

            def load(j, more):
                load_values(j)
                load_gate(j, 0)
                if not (isinstance(j, int) and j == 0):
                    store(j - 1, 0)
                load_gate(j, 1)
                load_gate(j, 2)
                if more:
                    load_small(j + 1)
                    load_rotated(j + 1)
                if not (isinstance(j, int) and j == 0):
                    store(j - 1, 1)

            load_small(0)
            load_rotated(0)
            load(0, True)
            with sp.Fori(1, HEADS - 1) as j:
                load(j, True)
            load(HEADS - 1, False)
            store(HEADS - 1, 0)
            store(HEADS - 1, 1)
            for group in range(HALVES):
                sp.wait_ge(og_out[group], 16 * HEADS)

        @block.gpsimd
        def _(pool):
            def split(raw, hi, lo, done, before):
                zeros = zero[:].broadcast_to([P, HD]) if len(raw.shape) == 2 else \
                    zero[:].unsqueeze(2).broadcast_to([P, raw.shape[1], P])
                pool.tensor_tensor(hi, raw, zeros, ALU.add).then_inc(done, 1)
                pool.wait_ge(done, before * 2 + 1)
                pool.tensor_tensor(lo, raw, hi.bitcast(F32), ALU.subtract).then_inc(done, 1)

            def split_small(j):
                pool.wait_ge(ws_in, 32 * j + 32)
                if not (isinstance(j, int) and j == 0):
                    pool.wait_ge(small_mm, use(j - 2, Q1))
                split(ws_raw[:], ws_hi[:], ws_lo[:], ws_split, j)

            def splits(j, more):
                pool.wait_ge(wv_in, 16 * j + 16)
                if not (isinstance(j, int) and j == 0):
                    pool.wait_ge(small_mm, use(j - 1, V1))
                split(wv_raw[:], wv_hi[:], wv_lo[:], wv_split, j)
                for n, (k0, count) in enumerate(CHUNKS):
                    m = G_PARTS * j + n
                    pool.wait_ge(wg_in, 16 * m + 16)
                    if not (isinstance(j, int) and j == 0):
                        pool.wait_ge(g_mm, HALVES * G_PARTS * (j - 1) + G_PARTS + n + 1)
                    split(wg_raw[:, 0:count, :], wg_hi[:, k0:k0 + count, :],
                          wg_lo[:, k0:k0 + count, :], w_split, m)
                if more:
                    split_small(j + 1)

            pool.wait_ge(zeroed, 1)
            split_small(0)
            splits(0, True)
            with pool.Fori(1, HEADS - 1) as j:
                splits(j, True)
            splits(HEADS - 1, False)

        @block.tensor
        def _(pe):
            def small_bank(i, n):
                at_least(pe, small_free, use(i, n) - 2)
                return small[:, n % 2, :]

            def keys(i, half):
                bank = small_bank(i, (K0, K1)[half])
                for m, (w, x) in enumerate(products(ws_hi, ws_lo, kvn_hi, kvn_lo)):
                    mm = pe.matmul(bank, w[:, QKT, :], x[:, half_cols(half)],
                                   start=(m == 0), stop=(m == 2))
                mm.then_inc(small_mm, 1)

            def queries(i, half):
                pe.wait_ge(ws_split, 2 * i + 4)
                bank = small_bank(i, (Q0, Q1)[half])
                for k in range(QKT):
                    for m, (w, x) in enumerate(products(ws_hi, ws_lo, qn_hi, qn_lo)):
                        mm = pe.matmul(bank, w[:, k, :], x[:, k, half_cols(half)],
                                       start=(k == 0 and m == 0), stop=(k == QKT - 1 and m == 2))
                mm.then_inc(small_mm, 1)

            def rotated(i, half):
                pe.wait_ge(qr_loaded, 32 * i + 64)
                bank = small_bank(i, (R0, R1)[half])
                for b in range(QG):
                    mm = pe.transpose(bank[:, b * P:(b + 1) * P],
                                      qr_in[:, half * QG + b, :, :].rearrange("p a r -> p (a r)"),
                                      ident[:])
                mm.then_inc(small_mm, 1)

            def values(i, half):
                pe.wait_ge(wv_split, 2 * i + 2)
                bank = small_bank(i, (V0, V1)[half])
                for b in range(QG):
                    rows = slice((half * QG + b) * P, (half * QG + b + 1) * P)
                    for m, (x, w) in enumerate(products(kvn_hi, kvn_lo, wv_hi, wv_lo)):
                        mm = pe.matmul(bank[:, b * P:(b + 1) * P], x[:, rows], w[:],
                                       start=(m == 0), stop=(m == 2))
                mm.then_inc(small_mm, 1)

            def gates(i, half, n):
                k0, count = CHUNKS[n]
                pe.wait_ge(w_split, 2 * (G_PARTS * i + n + 1))
                if n == 0:
                    at_least(pe, g_done, HALVES * i + half)
                for kt in range(k0, k0 + count):
                    for k, (w, h) in enumerate(products(wg_hi, wg_lo, hT_hi, hT_lo)):
                        mm = pe.matmul(g[:], w[:, kt, :], h[:, kt, half_cols(half)],
                                       start=(kt == 0 and k == 0), stop=(kt == KT - 1 and k == 2))
                mm.then_inc(g_mm, 1)

            def scores(i, s):
                pe.wait_ge(small_free, use(i - 1, (R0, R1)[s // QG]))
                at_least(pe, exp_done, blocks_before(i, s))
                n_keys = (s + 1) * P
                rows = slice(s * P, (s + 1) * P)
                z0 = first_bank(s) * BANK
                for c0 in range(0, n_keys, BANK):
                    width = min(BANK, n_keys - c0)
                    last = c0 + width == n_keys
                    out = z[:, z0 + c0:z0 + c0 + width]
                    pe.matmul(out, qr[:, rows], kr_lo[:, c0:c0 + width], start=True, stop=False)
                    for q, k in products(q_hi, q_lo, k_hi, k_lo):
                        pe.matmul(out, q[:, rows], k[:, bass.ds((i % 2) * TOK + c0, width)],
                                  start=False, stop=False)
                    mm = pe.matmul(out, qr[:, rows], kr_hi[:, c0:c0 + width], start=False,
                                   stop=not last)
                    if last:
                        mm = pe.matmul(z[:, z0 + s * P:z0 + (s + 1) * P], ident_r[:], chunk_r[:],
                                       start=False, stop=True)
                mm.then_inc(z_done, 1)

            def turn_probs(i, s):
                pe.wait_ge(p_done, TT * i + s + 1)
                at_least(pe, pT_lo_done, blocks_before(i, s))
                b0 = first_bank(s) * QG
                for kb in range(s + 1):
                    mm = pe.transpose(pT[:, b0 + kb, :], prob[:, s % 2, kb * P:(kb + 1) * P],
                                      ident[:])
                mm.then_inc(pT_done, 1)

            def mix(i, group):
                pe.wait_ge(pT_lo_done, TT * i + QG * (group + 1))
                pe.wait_ge(small_free, use(i, (V0, V1)[group]))
                at_least(pe, og_done, HALVES * i + group)
                blocks = QG * (group + 1)
                for kb in range(blocks):
                    q0 = max(kb - QG * group, 0) * P
                    for n, (v, w) in enumerate(products(v_hi, v_lo, pT_hi, pT_lo)):
                        mm = pe.matmul(pv[:, q0:BANK], v[:, kb, :], w[:, kb, q0:BANK],
                                       start=(kb == 0 and n == 0),
                                       stop=(kb == blocks - 1 and n == 2))
                mm.then_inc(pv_done, 1)

            PRODUCT = {V0: values, V1: values, Q0: queries, Q1: queries, K0: keys, K1: keys,
                       R0: rotated, R1: rotated}

            def step(i, attend, proj):
                for s in range(TT):
                    if attend:
                        if s == 0 and not (isinstance(i, int) and i == 0):
                            mix(i - 1, 1)
                        if s == QG:
                            mix(i, 0)
                        turn_probs(i, s)
                    for n in small_uses(BEFORE, s, attend, proj):
                        PRODUCT[n](i, HALF[n])
                    for head, block_ in ahead(i, s, attend, proj):
                        scores(head, block_)
                    for n in small_uses(AFTER, s, attend, proj):
                        PRODUCT[n](i, HALF[n])
                    if attend and s in GATE_PART:
                        gates(i, *GATE_PART[s])

            iterations(pe, step)
            mix(HEADS - 1, 1)

        @block.scalar
        def _(act):
            def evacuate(i, n):
                act.wait_ge(small_mm, use(i, n))
                half = HALF[n]
                if n in (K0, K1):
                    out = k_hi[:, bass.ds(((i + 1) % 2) * TOK + half * BANK, BANK)]
                elif n in (V0, V1):
                    out = v_hi[:, half * QG:(half + 1) * QG, :].rearrange("p t d -> p (t d)")
                elif n in (Q0, Q1):
                    out = q_hi[:, half_cols(half)]
                else:
                    out = qr[:, half_cols(half)]
                act.activation(out, small[:, n % 2, :], ACT.Copy).then_inc(small_hi, 1)

            def exps(i, s):
                n_keys = (s + 1) * P
                z0 = first_bank(s) * BANK
                act.wait_ge(neg_done, TT * i + s + 1)
                at_least(act, pT_done, TT * i + s - 1)
                act.activation(prob[:, s % 2, 0:n_keys], z[:, z0:z0 + n_keys], ACT.Exp,
                               bias=neg_top[:, s:s + 1], scale=MLA_SCALE,
                               accum_out=total[:, s:s + 1]).then_inc(exp_done, 1)

            def probs_hi(i, s):
                act.wait_ge(pT_done, TT * i + s + 1)
                q0 = (s % QG) * P
                b0 = first_bank(s) * QG
                act.activation(pT_hi[:, 0:s + 1, q0:q0 + P], pT[:, b0:b0 + s + 1, :],
                               ACT.Copy).then_inc(pT_hi_done, 1)

            def gate_tanh(i, half):
                act.wait_ge(g_mm, G_PARTS * (HALVES * i + half + 1))
                at_least(act, og_done, HALVES * (i - 1) + half + 1)
                act.activation(gate[:, half, :], g[:], ACT.Tanh, scale=0.5).then_inc(g_tanh, 1)

            def step(i, attend, proj):
                for s in range(TT):
                    if attend:
                        probs_hi(i, s)
                    for n in small_uses(BEFORE, s, attend, proj):
                        evacuate(i, n)
                    for head, block_ in ahead(i, s, attend, proj):
                        exps(head, block_)
                    for n in small_uses(AFTER, s, attend, proj):
                        evacuate(i, n)
                    if attend and s in GATE_PART and GATE_PART[s][1] == G_PARTS - 1:
                        gate_tanh(i, GATE_PART[s][0])

            iterations(act, step)

        @block.vector
        def _(dve):
            def evacuate(i, n):
                dve.wait_ge(small_hi, use(i, n))
                half = HALF[n]
                src = small[:, n % 2, :]
                if n in (K0, K1):
                    cols = bass.ds(((i + 1) % 2) * TOK + half * BANK, BANK)
                    hi, lo = k_hi[:, cols], k_lo[:, cols]
                elif n in (V0, V1):
                    tiles = slice(half * QG, (half + 1) * QG)
                    hi = v_hi[:, tiles, :].rearrange("p t d -> p (t d)")
                    lo = v_lo[:, tiles, :].rearrange("p t d -> p (t d)")
                elif n in (Q0, Q1):
                    hi, lo = q_hi[:, half_cols(half)], q_lo[:, half_cols(half)]
                else:
                    hi = lo = qr[ROPE:P, half_cols(half)]
                    src = small[ROPE:P, n % 2, :]
                dve.tensor_tensor(lo, src, hi.bitcast(F32), ALU.subtract).then_inc(small_free, 1)

            def maxima(i, s):
                n_keys = (s + 1) * P
                z0 = first_bank(s) * BANK
                dve.wait_ge(z_done, TT * i + s + 1)
                dve.tensor_reduce(top[:, s:s + 1], z[:, z0:z0 + n_keys], axis=AX_X,
                                  op=ALU.max).then_inc(top_done, 1)
                dve.wait_ge(top_done, TT * i + s + 1)
                dve.tensor_scalar(neg_top[:, s:s + 1], top[:, s:s + 1], -MLA_SCALE, None,
                                  ALU.mult).then_inc(neg_done, 1)

            def normalise(i, s):
                n_keys = (s + 1) * P
                dve.wait_ge(exp_done, TT * i + s + 1)
                dve.reciprocal(inverse[:, s:s + 1], total[:, s:s + 1]).then_inc(inv_done, 1)
                dve.wait_ge(inv_done, TT * i + s + 1)
                dve.tensor_scalar(prob[:, s % 2, 0:n_keys], prob[:, s % 2, 0:n_keys],
                                  inverse[:, s:s + 1], None, ALU.mult).then_inc(p_done, 1)

            def probs_lo(i, s):
                q0 = (s % QG) * P
                b0 = first_bank(s) * QG
                dve.wait_ge(pT_hi_done, TT * i + s + 1)
                dve.tensor_tensor(pT_lo[:, 0:s + 1, q0:q0 + P], pT[:, b0:b0 + s + 1, :],
                                  pT_hi[:, 0:s + 1, q0:q0 + P].bitcast(F32),
                                  ALU.subtract).then_inc(pT_lo_done, 1)

            def silu(i, half):
                dve.wait_ge(g_tanh, HALVES * i + half + 1)
                dve.scalar_tensor_tensor(gate[:, half, :], gate[:, half, :], 1.0, g[:], ALU.add,
                                         ALU.mult).then_inc(g_done, 1)

            def gated(i, group):
                dve.wait_ge(pv_done, HALVES * i + group + 1)
                at_least(dve, og_out[group], 16 * i)
                dve.wait_ge(g_done, HALVES * i + group + 1)
                dve.scalar_tensor_tensor(og[:, group, :], pv[:], 0.5, gate[:, group, :], ALU.mult,
                                         ALU.mult).then_inc(og_done, 1)

            def step(i, attend, proj):
                for s in range(TT):
                    before = not (isinstance(i, int) and i <= 0)
                    if attend:
                        if s + 1 < TT:
                            normalise(i, s + 1)
                        if s == QG:
                            silu(i, 0)
                        if s == TT - 1:
                            silu(i, 1)
                        if s == 1 and before:
                            gated(i - 1, 1)
                        probs_lo(i, s)
                    if proj and s == TT - 1:
                        normalise(i + 1, 0)
                    for n in small_uses(BEFORE, s, attend, proj):
                        evacuate(i, n)
                    for head, block_ in ahead(i, s, attend, proj):
                        maxima(head, block_)
                    for n in small_uses(AFTER, s, attend, proj):
                        evacuate(i, n)
                    if attend and s == QG + 1:
                        gated(i, 0)

            dve.memset(zero[:], 0.0).then_inc(zeroed, 1)
            iterations(dve, step)
            gated(HEADS - 1, 1)


def build(nc, x, positions, ln0, w_in0, w_out0, ln1, w_in1, q_norm1, w_qb1, kv_norm1, w_kvb1,
          w_out1, final_norm, inv_freq, out):
    og_dram = nc.dram_tensor("og_scratch", [HEADS, HD, TOK], F32, kind="Internal").ap()
    x1_dram = nc.dram_tensor("x1_scratch", [TOK, D], F32, kind="Internal").ap()
    qr_dram = nc.dram_tensor("qr_scratch", [TOK, HEADS * ROPE], F32, kind="Internal").ap()
    x_rows = x.rearrange("b t d -> (b t) d")
    out_rows = out.rearrange("b t d -> (b t) d")

    with ExitStack() as whole:
        shared = Chip(nc, whole, "all")
        with ExitStack() as ctx:
            ident, ident_r, strict_r, chunk_r = build_constants(nc, Chip(nc, ctx, "const"), shared)

        with ExitStack() as layer:
            h = Chip(nc, layer, "h0")
            hT_hi, hT_lo = h.sb("hT_hi", [P, KT, TOK], F32R), h.sb("hT_lo", [P, KT, TOK], F32R)
            with ExitStack() as ctx:
                c = Chip(nc, ctx, "norm0")
                build_norm(nc, c, c.sb("x", [P, TT, D]), x_rows, ln0, ident, hT_hi, hT_lo)
            with ExitStack() as ctx:
                build_stick_heads(nc, Chip(nc, ctx, "stick"), w_in0, ident, ident_r, strict_r,
                                  hT_hi, hT_lo, og_dram)

        with ExitStack() as layer:
            h = Chip(nc, layer, "h1")
            hT_hi, hT_lo = h.sb("hT_hi", [P, KT, TOK], F32R), h.sb("hT_lo", [P, KT, TOK], F32R)
            with ExitStack() as ctx:
                x_sb = Chip(nc, ctx, "x1").sb("x", [P, TT, D])
                with ExitStack() as inner:
                    build_out(nc, Chip(nc, inner, "out0"), w_out0, og_dram, x_rows, x_sb, x1_dram,
                              None, None)
                with ExitStack() as inner:
                    build_norm(nc, Chip(nc, inner, "norm1"), x_sb, None, ln1, ident, hT_hi, hT_lo)
            qn_hi, qn_lo = (h.sb(n, [P, QKT, TOK], F32R) for n in ("qn_hi", "qn_lo"))
            kvn_hi, kvn_lo = (h.sb(n, [P, TOK], F32R) for n in ("kvn_hi", "kvn_lo"))
            kr_hi, kr_lo = (h.sb(n, [P, TOK], F32R) for n in ("kr_hi", "kr_lo"))
            with ExitStack() as ctx:
                build_latents(nc, Chip(nc, ctx, "lat"), w_in1, positions, inv_freq, q_norm1,
                              kv_norm1, w_qb1, ident, hT_hi, hT_lo, qn_hi, qn_lo, kvn_hi, kvn_lo,
                              kr_hi, kr_lo, qr_dram)
            with ExitStack() as ctx:
                build_mla_heads(nc, Chip(nc, ctx, "mla"), w_in1, w_qb1, w_kvb1, ident, ident_r,
                                chunk_r, hT_hi, hT_lo, qn_hi, qn_lo, kvn_hi, kvn_lo, kr_hi, kr_lo,
                                qr_dram, og_dram)

        with ExitStack() as ctx:
            c = Chip(nc, ctx, "out1")
            build_out(nc, c, w_out1, og_dram, x1_dram, c.sb("x", [P, TT, D]), None, final_norm,
                      out_rows)


_INS = ["x", "positions", "ln0", "w_in0", "w_out0", "ln1", "w_in1", "q_norm1", "w_qb1",
        "kv_norm1", "w_kvb1", "w_out1", "final_norm"]


def kernel(**inputs):
    import numpy as _np
    import concourse.bacc as _bacc
    from concourse import mybir as _mybir
    from concourse.bass_utils import run_bass_kernel_spmd as _run

    nc = _bacc.Bacc("TRN2", target_bir_lowering=False, num_devices=1)
    arrays = {f"in_{n}_dram": _np.ascontiguousarray(inputs[n]) for n in _INS}
    freq = 10000.0 ** (-_np.arange(0, ROPE, 2, dtype=_np.float64) / ROPE)
    arrays["in_inv_freq_dram"] = freq.astype(_np.float32).reshape(1, HALF_ROPE)
    args = [nc.dram_tensor(n, a.shape, _mybir.dt.from_np(a.dtype), kind="ExternalInput").ap()
            for n, a in arrays.items()]
    out = nc.dram_tensor("out_0_dram", (1, TOK, D), F32, kind="ExternalOutput").ap()
    build(nc, *args, out)
    r = _run(nc, [arrays], core_ids=[0])
    return r.results[0]["out_0_dram"]
```

```python
from contextlib import ExitStack

import concourse.bass as bass
from concourse import mybir

F32 = mybir.dt.float32
F32R = mybir.dt.float32r
I32 = mybir.dt.int32
ALU = mybir.AluOpType
ACT = mybir.ActivationFunctionType
AX_X = mybir.AxisListType.X

P = 128
BANK = 512
D = 1024
TOK = 1024
KT = D // P
TT = TOK // P
HEADS = 16
HD = 128
D_INNER = HEADS * HD
HALVES = TOK // BANK
QG = BANK // P
CHUNK = 64
Q_RANK, KV_RANK, ROPE = 256, 128, 64
QKT = Q_RANK // P
HALF_ROPE = ROPE // 2
LAT = Q_RANK + KV_RANK + ROPE
NOPE = 128
EPS = 1e-6
NEG = -1e30
STICK_SCALE = HD ** -0.5
MLA_SCALE = (NOPE + ROPE) ** -0.5


def at_least(eng, sem, value):
    if isinstance(value, int) and value <= 0:
        return
    eng.wait_ge(sem, value)


def settled(eng, value):
    return value if isinstance(value, int) else eng.snap(value)


def products(w_hi, w_lo, x_hi, x_lo):
    return ((w_lo, x_hi), (w_hi, x_lo), (w_hi, x_hi))


class Chip:

    def __init__(self, nc, ctx, tag):
        self.nc, self.ctx, self.tag = nc, ctx, tag

    def sb(self, name, shape, dt=F32, side=None):
        return self.ctx.enter_context(self.nc.sbuf_tensor(f"{self.tag}_{name}", shape, dt,
                                                          side=side))

    def psum(self, name, shape):
        return self.ctx.enter_context(self.nc.psum_tensor(f"{self.tag}_{name}", shape, F32))

    def sem(self, name):
        return self.ctx.enter_context(self.nc.semaphore(f"{self.tag}_{name}"))


def build_constants(nc, c, outer):
    ident = outer.sb("ident", [P, P])
    strict = outer.sb("strict", [P, P])
    zero = outer.sb("zero", [P, 1])
    cleared, made, zeroed = c.sem("cleared"), c.sem("made"), c.sem("zeroed")
    with nc.Block() as block:

        @block.gpsimd
        def _(pool):
            pool.memset(ident[:], 0.0).then_inc(cleared, 1)
            pool.memset(strict[:], 0.0).then_inc(cleared, 1)
            pool.wait_ge(cleared, 2)
            pool.affine_select(out=ident[:], in_=ident[:], compare_op=ALU.not_equal, fill=1.0,
                               base=0, pattern=[[-1, P]], channel_multiplier=1).then_inc(made, 1)
            pool.affine_select(out=strict[:], in_=strict[:], compare_op=ALU.is_gt, fill=NEG,
                               base=0, pattern=[[-1, P]], channel_multiplier=1).then_inc(made, 1)
            pool.wait_ge(made, 2)

        @block.vector
        def _(dve):
            dve.memset(zero[:], 0.0).then_inc(zeroed, 1)
            dve.wait_ge(zeroed, 1)
    return ident, strict, zero


def split_on_pool(pool, raw, hi, lo, zero, done, before):
    zeros = zero[:].broadcast_to([P, raw.shape[1]]) if len(raw.shape) == 2 else \
        zero[:].unsqueeze(2).broadcast_to([P, raw.shape[1], raw.shape[2]])
    pool.tensor_tensor(hi, raw, zeros, ALU.add).then_inc(done, 1)
    pool.wait_ge(done, 2 * before + 1)
    pool.tensor_tensor(lo, raw, hi.bitcast(F32), ALU.subtract).then_inc(done, 1)


class StickWeights:
    UNITS = 4
    KEY, QRY, VAL, GATE = range(UNITS)
    PART = {QRY: 0, KEY: 1, VAL: 2, GATE: 3}
    SLOT = {KEY: 0, VAL: 1, QRY: 2, GATE: 2}

    def __init__(self, c, w_in):
        self.raw = c.sb("w_raw", [P, 2, KT, P])
        self.hi = c.sb("w_hi", [P, 3, KT, P], F32R)
        self.lo = c.sb("w_lo", [P, 3, KT, P], F32R)
        self.loaded = [c.sem(f"w_in{s}") for s in range(2)]
        self.split_done = c.sem("w_split")
        self.units = w_in.rearrange("(k p) (u h n) -> h u p k n", p=P, u=self.UNITS, n=HD)

    def load(self, sp, j):
        for u in range(self.UNITS):
            n = self.UNITS * j + u
            if u != self.QRY:
                at_least(sp, self.split_done, 2 * (n - 1 + (u == self.KEY)))
            src = self.units[bass.ds(j, 1), self.PART[u], :, :, :]
            sp.dma_start(self.raw[:, u % 2, :, :], src.rearrange("h p k n -> (h p) k n"))\
                .then_inc(self.loaded[u % 2], 16)

    def split(self, pool, j, u, zero):
        pool.wait_ge(self.loaded[u % 2], 16 * (2 * j + u // 2 + 1))
        split_on_pool(pool, self.raw[:, u % 2, :, :], self.hi[:, self.SLOT[u], :, :],
                      self.lo[:, self.SLOT[u], :, :], zero, self.split_done, self.UNITS * j + u)


class LatentWeights:
    CHUNK = 2
    COUNT = KT // CHUNK
    SLOTS = 2

    def __init__(self, hold, passing, w_in):
        self.hi, self.lo = (hold.sb(n, [P, KT, LAT], F32R, side="right")
                            for n in ("wl_hi", "wl_lo"))
        self.raw = passing.sb("wl_raw", [P, self.SLOTS, self.CHUNK, LAT])
        self.loaded = [hold.sem(f"wl_in{s}") for s in range(self.SLOTS)]
        self.split_done = hold.sem("wl_split")
        self.rows = w_in.rearrange("(k p) n -> p k n", p=P)

    def load(self, sp, n):
        at_least(sp, self.split_done, 2 * (n - self.SLOTS + 1))
        k0 = n * self.CHUNK
        sp.dma_start(self.raw[:, n % self.SLOTS, :, :], self.rows[:, k0:k0 + self.CHUNK, 0:LAT])\
            .then_inc(self.loaded[n % self.SLOTS], 16)

    def split(self, pool, n, zero):
        pool.wait_ge(self.loaded[n % self.SLOTS], 16 * (n // self.SLOTS + 1))
        tiles = slice(n * self.CHUNK, (n + 1) * self.CHUNK)
        split_on_pool(pool, self.raw[:, n % self.SLOTS, :, :], self.hi[:, tiles, :],
                      self.lo[:, tiles, :], zero, self.split_done, n)


class SmallWeights:

    def __init__(self, c, w_qb, w_kvb):
        self.raw = c.sb("ws_raw", [P, QKT + 1, P])
        self.hi, self.lo = (c.sb(n, [P, QKT + 1, P], F32R) for n in ("ws_hi", "ws_lo"))
        self.loaded, self.split_done = c.sem("ws_in"), c.sem("ws_split")
        self.qb_cols, self.w_kvb = w_qb.rearrange("(k p) n -> p k n", p=P), w_kvb

    def load(self, sp, j):
        at_least(sp, self.split_done, 2 * j)
        sp.dma_start(self.raw[:, 0:QKT, :],
                     self.qb_cols[:, :, bass.ds(j * (NOPE + ROPE), NOPE)])\
            .then_inc(self.loaded, 16)
        sp.dma_start(self.raw[:, QKT, :],
                     self.w_kvb[:, bass.ds(j * (NOPE + HD), NOPE)]).then_inc(self.loaded, 16)

    def split(self, pool, j, zero):
        pool.wait_ge(self.loaded, 32 * j + 32)
        split_on_pool(pool, self.raw[:], self.hi[:], self.lo[:], zero, self.split_done, j)


def rstd_steps(dve, chain, sq_sum, width, var, rstd, tmp, var_done, root_done, root_value):
    dve.tensor_scalar(var, sq_sum, 1.0 / width, EPS, ALU.mult, ALU.add).then_inc(var_done, 1)
    dve.wait_ge(root_done, root_value)
    chain(dve.reciprocal(rstd, rstd))
    chain(dve.tensor_tensor(tmp, rstd, rstd, ALU.mult))
    chain(dve.tensor_tensor(tmp, tmp, var, ALU.mult))
    chain(dve.tensor_scalar(tmp, tmp, -0.5, 1.5, ALU.mult, ALU.add))
    chain(dve.tensor_tensor(rstd, rstd, tmp, ALU.mult))


class OutOperands:

    def __init__(self, c, layer, first_slot, w_out, og_dram):
        self.w, self.og = ([tile] for tile in first_slot)
        self.loaded = [c.sem(f"raw_in{layer}_{s}") for s in range(2)]
        self.w_out, self.og_dram = w_out, og_dram

    def second_slot(self, c):
        self.w.append(c.sb("w_raw1", [P, D]))
        self.og.append(c.sb("og_raw1", [P, BANK]))

    def load(self, sp, h, half, slot):
        sp.dma_start(self.w[slot][:], self.w_out[bass.ds(h * HD, HD), :])\
            .then_inc(self.loaded[slot], 16)
        sp.dma_start(self.og[slot][:],
                     self.og_dram[bass.ds(h, 1), :, half * BANK:(half + 1) * BANK]
                     .rearrange("h p n -> (h p) n")).then_inc(self.loaded[slot], 16)


def build_norm(nc, c, x_dram, gain_dram, ident, zero, hT_hi, hT_lo, weights):
    x_sb = c.sb("x", [P, TT, D])
    gain = c.sb("gain", [P, KT])
    junk = c.sb("junk", [P, D])
    sq_sum, var, rstd, tmp = (c.sb(n, [P, TT]) for n in ("sq_sum", "var", "rstd", "tmp"))
    banks = c.psum("banks", [P, 4, BANK])
    x_in = [c.sem(f"x_in{t}") for t in range(TT)]
    gain_in, squared, var_done, root_done, linked, scaled, turned, hi_done, lo_done = (
        c.sem(n) for n in ("gain_in", "squared", "var_done", "root_done", "linked", "scaled",
                           "turned", "hi_done", "lo_done"))
    groups = [(half, kt) for half in range(HALVES) for kt in range(KT)]
    with nc.Block() as block:

        @block.sync
        def _(sp):
            for t in range(TT):
                sp.dma_start(x_sb[:, t, :], x_dram[t * P:(t + 1) * P, :]).then_inc(x_in[t], 16)
            sp.dma_start(gain[:], gain_dram.rearrange("(k p) -> p k", p=P),
                         allow_slow_non_contiguous=True).then_inc(gain_in, 16)
            weights.load(sp, 0)

        @block.gpsimd
        def _(pool):
            for u in (weights.KEY, weights.QRY, weights.VAL):
                weights.split(pool, 0, u, zero)
            pool.wait_ge(weights.split_done, 6)

        @block.scalar
        def _(act):
            for half in range(HALVES):
                for t in range(half * QG, (half + 1) * QG):
                    act.wait_ge(x_in[t], 16)
                    if t:
                        act.wait_ge(squared, t)
                    act.activation(junk[:], x_sb[:, t, :], ACT.Square,
                                   accum_out=sq_sum[:, t:t + 1]).then_inc(squared, 1)
                act.wait_ge(var_done, half + 1)
                act.activation(rstd[:, half * QG:(half + 1) * QG], var[:, half * QG:(half + 1) * QG],
                               ACT.Sqrt).then_inc(root_done, 1)
            act.wait_ge(gain_in, 16)
            for n, (half, kt) in enumerate(groups):
                act.wait_ge(turned, n + 1)
                act.activation(hT_hi[:, kt, half * BANK:(half + 1) * BANK], banks[:, n % 4, :],
                               ACT.Copy, scale=gain[:, kt:kt + 1]).then_inc(hi_done, 1)

        @block.vector
        def _(dve):
            count = [0]

            def chain(ins):
                count[0] += 1
                ins.then_inc(linked, 1)
                dve.wait_ge(linked, count[0])

            for half in range(HALVES):
                cols = slice(half * QG, (half + 1) * QG)
                dve.wait_ge(squared, (half + 1) * QG)
                rstd_steps(dve, chain, sq_sum[:, cols], D, var[:, cols], rstd[:, cols],
                           tmp[:, cols], var_done, root_done, half + 1)
                for t in range(half * QG, (half + 1) * QG):
                    dve.tensor_scalar(x_sb[:, t, :], x_sb[:, t, :], rstd[:, t:t + 1], None,
                                      ALU.mult).then_inc(scaled, 1)
            dve.wait_ge(gain_in, 16)
            for n, (half, kt) in enumerate(groups):
                dve.wait_ge(hi_done, n + 1)
                cols = slice(half * BANK, (half + 1) * BANK)
                dve.scalar_tensor_tensor(hT_lo[:, kt, cols], banks[:, n % 4, :], gain[:, kt:kt + 1],
                                         hT_hi[:, kt, cols].bitcast(F32), ALU.mult,
                                         ALU.subtract).then_inc(lo_done, 1)
            dve.wait_ge(lo_done, len(groups))

        @block.tensor
        def _(pe):
            for n, (half, kt) in enumerate(groups):
                if kt == 0:
                    pe.wait_ge(scaled, (half + 1) * QG)
                at_least(pe, lo_done, n - 3)
                for q in range(QG):
                    mm = pe.transpose(banks[:, n % 4, q * P:(q + 1) * P],
                                      x_sb[:, half * QG + q, kt * P:(kt + 1) * P], ident[:])
                mm.then_inc(turned, 1)


def build_stick_heads(nc, c, weights, ident, strict, zero, hT_hi, hT_lo, og,
                      og_out, og_dram, operands):
    KEY, VAL, QRY, GATE = weights.KEY, weights.VAL, weights.QRY, weights.GATE
    UNITS, SLOT = weights.UNITS, weights.SLOT
    w_hi, w_lo, w_split = weights.hi, weights.lo, weights.split_done
    PLAN = ((KEY, 0), (KEY, 1), (QRY, 0), (VAL, 0), (QRY, 1), (VAL, 1), (GATE, 0), (GATE, 1))
    STEP_OF = {what: v for v, what in enumerate(PLAN)}
    AHEAD = 2
    PROJ = UNITS * HALVES
    HI_EVACS = 6

    q_hi, q_lo = c.sb("q_hi", [P, TOK], F32R), c.sb("q_lo", [P, TOK], F32R)
    k_hi, k_lo = c.sb("k_hi", [P, 2 * TOK], F32R), c.sb("k_lo", [P, 2 * TOK], F32R)
    v_cols = c.sb("v_cols", [P, TOK])
    v_hi, v_lo = c.sb("v_hi", [P, TT, HD], F32R), c.sb("v_lo", [P, TT, HD], F32R)
    gate = c.sb("gate", [P, HALVES, BANK])
    skip = c.sb("skip", [P, 2, TOK])
    take = c.sb("take", [P, 2, TOK])
    wT_hi = c.sb("wT_hi", [P, TT, BANK], F32R)
    wT_lo = c.sb("wT_lo", [P, TT, BANK], F32R)

    pj = c.psum("pj", [P, 2, BANK])
    z = c.psum("z", [P, TOK])
    wT = c.psum("wT", [P, TT, P])
    vT = c.psum("vT", [P, QG, P])
    pv = c.psum("pv", [P, BANK])

    (proj_done, proj_hi, proj_free, z_done, masked, skip_done, take_done, scan_done, w_done,
     wT_done, wT_hi_done, wT_lo_done, vT_done, vT_hi_done, vT_lo_done, pv_done, og_done) = (
         c.sem(n) for n in ("proj_done", "proj_hi", "proj_free", "z_done", "masked", "skip_done",
                            "take_done", "scan_done", "w_done", "wT_done", "wT_hi_done",
                            "wT_lo_done", "vT_done", "vT_hi_done", "vT_lo_done", "pv_done",
                            "og_done"))

    def half_cols(half):
        return slice(half * BANK, (half + 1) * BANK)

    def ahead(i, s, attend, proj):
        if s + AHEAD < TT:
            return [(i, s + AHEAD)] if attend else []
        return [(i + 1, s + AHEAD - TT)] if proj else []

    def projected(i, s, attend, proj):
        if not proj:
            return [(i, {5: 6, 6: 7}[s])] if s in (5, 6) else []
        if s < HALVES:
            return [(i, STEP_OF[GATE, s])] if attend else []
        return [(i + 1, s - HALVES)]

    def iterations(eng, step):
        step(-1, False, True)
        step(0, True, True)
        with eng.Fori(1, HEADS - 1) as i:
            step(i, True, True)
        step(HEADS - 1, True, False)

    with nc.Block() as block:

        @block.sync
        def _(sp):
            def store(i, group):
                i = settled(sp, i)
                sp.wait_ge(og_done, HALVES * i + group + 1)
                dst = og_dram[bass.ds(i, 1), :, half_cols(group)].rearrange("h p n -> (h p) n")
                sp.dma_start(dst, og[:, group, :]).then_inc(og_out[group], 16)

            weights.load(sp, 1)
            store(0, 0)
            with sp.Fori(2, HEADS) as j:
                weights.load(sp, j)
                store(j - 2, 1)
                store(j - 1, 0)
            store(HEADS - 2, 1)
            sp.wait_ge(og_out[0], 16)
            operands.load(sp, 0, 0, 0)
            store(HEADS - 1, 0)
            store(HEADS - 1, 1)

        @block.gpsimd
        def _(pool):
            def split(j, u):
                before, j0 = {GATE: (QRY, j), QRY: (GATE, j - 1)}.get(u, (u, j - 1))
                at_least(pool, proj_done, PROJ * j0 + (STEP_OF[before, 1] + 1))
                weights.split(pool, j, u, zero)

            split(0, GATE)
            with pool.Fori(1, HEADS) as j:
                for u in range(UNITS):
                    split(j, u)

        @block.tensor
        def _(pe):
            def project(j, v):
                m = PROJ * j + v
                u, half = PLAN[v]
                if half == 0:
                    at_least(pe, w_split, 2 * (UNITS * j + u + 1))
                at_least(pe, proj_free, m - 1)
                for kt in range(KT):
                    for n, (w, h) in enumerate(products(w_hi, w_lo, hT_hi, hT_lo)):
                        mm = pe.matmul(pj[:, v % 2, :], w[:, SLOT[u], kt, :],
                                       h[:, kt, half_cols(half)], start=(kt == 0 and n == 0),
                                       stop=(kt == KT - 1 and n == 2))
                mm.then_inc(proj_done, 1)

            def scores(i, s):
                if s % QG == 0:
                    at_least(pe, proj_free, PROJ * i + STEP_OF[QRY, s // QG] + 1)
                at_least(pe, take_done, TT * i + s)
                n_keys = (s + 1) * P
                queries = slice(s * P, (s + 1) * P)
                for c0 in range(0, n_keys, BANK):
                    width = min(BANK, n_keys - c0)
                    for n, (q, k) in enumerate(products(q_hi, q_lo, k_hi, k_lo)):
                        mm = pe.matmul(z[:, c0:c0 + width], q[:, queries],
                                       k[:, bass.ds((i % 2) * TOK + c0, width)],
                                       start=(n == 0), stop=(n == 2))
                mm.then_inc(z_done, 1)

            def turn_weights(i, s):
                pe.wait_ge(w_done, TT * i + s + 1)
                at_least(pe, wT_lo_done, TT * i + s)
                for kb in range(s + 1):
                    mm = pe.transpose(wT[:, kb, :], take[:, s % 2, kb * P:(kb + 1) * P], ident[:])
                mm.then_inc(wT_done, 1)

            def turn_values(i, half):
                pe.wait_ge(proj_free, PROJ * i + (STEP_OF[VAL, half] + 1))
                at_least(pe, vT_lo_done, HALVES * i + half)
                for b in range(QG):
                    t = half * QG + b
                    mm = pe.transpose(vT[:, b, :], v_cols[:, t * P:(t + 1) * P], ident[:])
                mm.then_inc(vT_done, 1)

            def mix(i, group, first=0, last=QG):
                pe.wait_ge(wT_lo_done, TT * i + QG * group + last)
                pe.wait_ge(vT_lo_done, HALVES * i + group + 1)
                at_least(pe, og_done, HALVES * i + group)
                blocks = QG * group + last
                cols = last * P
                for kb in range(blocks):
                    q0 = max(kb - QG * group, first) * P
                    for n, (v, w) in enumerate(products(v_hi, v_lo, wT_hi, wT_lo)):
                        mm = pe.matmul(pv[:, q0:cols], v[:, kb, :], w[:, kb, q0:cols],
                                       start=(kb == 0 and n == 0),
                                       stop=(kb == blocks - 1 and n == 2))
                if last == QG:
                    mm.then_inc(pv_done, 1)

            def step(i, attend, proj):
                for s in range(TT):
                    if attend:
                        if s == 0 and not (isinstance(i, int) and i == 0):
                            mix(i - 1, 1)
                        if s == QG:
                            mix(i, 0)
                        turn_weights(i, s)
                    for head, block_ in ahead(i, s, attend, proj):
                        scores(head, block_)
                    for head, v in projected(i, s, attend, proj):
                        project(head, v)
                    if attend and s < HALVES:
                        turn_values(i, s)

            iterations(pe, step)
            mix(HEADS - 1, 1, 0, QG - 1)
            mix(HEADS - 1, 1, QG - 1, QG)

        @block.scalar
        def _(act):
            def project_hi(j, v):
                u, half = PLAN[v]
                if u == VAL:
                    return
                act.wait_ge(proj_done, PROJ * j + v + 1)
                bank = pj[:, v % 2, :]
                if u == GATE:
                    at_least(act, og_done, HALVES * (j - 1) + half + 1)
                    act.activation(gate[:, half, :], bank, ACT.Sigmoid).then_inc(proj_hi, 1)
                elif u == KEY:
                    act.activation(k_hi[:, bass.ds((j % 2) * TOK + half * BANK, BANK)], bank,
                                   ACT.Copy).then_inc(proj_hi, 1)
                else:
                    act.activation(q_hi[:, half_cols(half)], bank, ACT.Copy,
                                   scale=STICK_SCALE).then_inc(proj_hi, 1)

            def sigmoids(i, s):
                n_keys = (s + 1) * P
                act.wait_ge(masked, TT * i + s + 1)
                at_least(act, wT_done, TT * i + s - 1)
                act.activation(skip[:, s % 2, 0:n_keys], z[:, 0:n_keys], ACT.Sigmoid,
                               scale=-1.0).then_inc(skip_done, 1)
                act.activation(take[:, s % 2, 0:n_keys], z[:, 0:n_keys],
                               ACT.Sigmoid).then_inc(take_done, 1)

            def values_hi(i, half):
                act.wait_ge(vT_done, HALVES * i + half + 1)
                act.activation(v_hi[:, half * QG:(half + 1) * QG, :], vT[:],
                               ACT.Copy).then_inc(vT_hi_done, 1)

            def weights_hi(i, s):
                act.wait_ge(wT_done, TT * i + s + 1)
                q0 = (s % QG) * P
                act.activation(wT_hi[:, 0:s + 1, q0:q0 + P], wT[:, 0:s + 1, :],
                               ACT.Copy).then_inc(wT_hi_done, 1)

            def step(i, attend, proj):
                for s in range(TT):
                    if attend:
                        weights_hi(i, s)
                    for head, block_ in ahead(i, s, attend, proj):
                        sigmoids(head, block_)
                    for head, v in projected(i, s, attend, proj):
                        project_hi(head, v)
                    if attend and s < HALVES:
                        values_hi(i, s)

            iterations(act, step)

        @block.vector
        def _(dve):
            def project_lo(j, v):
                u, half = PLAN[v]
                bank = pj[:, v % 2, :]
                if u == VAL:
                    dve.wait_ge(proj_done, PROJ * j + v + 1)
                    dve.tensor_copy(v_cols[:, half_cols(half)], bank).then_inc(proj_free, 1)
                    return
                order = sum(w != VAL for w, _ in PLAN[:v + 1])
                dve.wait_ge(proj_hi, HI_EVACS * j + order)
                if u == GATE:
                    dve.tensor_tensor(gate[:, half, :], bank, gate[:, half, :],
                                      ALU.mult).then_inc(proj_free, 1)
                elif u == KEY:
                    cols = bass.ds((j % 2) * TOK + half * BANK, BANK)
                    dve.tensor_tensor(k_lo[:, cols], bank, k_hi[:, cols].bitcast(F32),
                                      ALU.subtract).then_inc(proj_free, 1)
                else:
                    cols = half_cols(half)
                    dve.scalar_tensor_tensor(q_lo[:, cols], bank, STICK_SCALE,
                                             q_hi[:, cols].bitcast(F32), ALU.mult,
                                             ALU.subtract).then_inc(proj_free, 1)

            def weights(i, s):
                n_keys = (s + 1) * P
                diagonal = z[:, s * P:n_keys]
                dve.wait_ge(z_done, TT * i + s + 1)
                dve.tensor_tensor(diagonal, diagonal, strict[:], ALU.add).then_inc(masked, 1)
                dve.wait_ge(skip_done, TT * i + s + 1)
                from_last = skip[:, s % 2, 0:n_keys][:, ::-1]
                dve.tensor_tensor_scan(from_last, from_last, zero[:].broadcast_to([P, n_keys]),
                                       1.0, ALU.mult, ALU.add).then_inc(scan_done, 1)
                dve.wait_ge(scan_done, TT * i + s + 1)
                dve.wait_ge(take_done, TT * i + s + 1)
                dve.tensor_tensor(take[:, s % 2, 0:n_keys - 1], take[:, s % 2, 0:n_keys - 1],
                                  skip[:, s % 2, 1:n_keys], ALU.mult).then_inc(w_done, 1)

            def values_lo(i, half):
                tiles = slice(half * QG, (half + 1) * QG)
                dve.wait_ge(vT_hi_done, HALVES * i + half + 1)
                dve.tensor_tensor(v_lo[:, tiles, :], vT[:], v_hi[:, tiles, :].bitcast(F32),
                                  ALU.subtract).then_inc(vT_lo_done, 1)

            def weights_lo(i, s):
                q0 = (s % QG) * P
                dve.wait_ge(wT_hi_done, TT * i + s + 1)
                dve.tensor_tensor(wT_lo[:, 0:s + 1, q0:q0 + P], wT[:, 0:s + 1, :],
                                  wT_hi[:, 0:s + 1, q0:q0 + P].bitcast(F32),
                                  ALU.subtract).then_inc(wT_lo_done, 1)

            def gated(i, group):
                dve.wait_ge(pv_done, HALVES * i + group + 1)
                at_least(dve, og_out[group], 16 * i)
                at_least(dve, proj_free, PROJ * i + (STEP_OF[GATE, group] + 1))
                dve.tensor_tensor(og[:, group, :], pv[:], gate[:, group, :],
                                  ALU.mult).then_inc(og_done, 1)

            def step(i, attend, proj):
                for s in range(TT):
                    if attend:
                        if s == 0 and not (isinstance(i, int) and i == 0):
                            gated(i - 1, 1)
                        if s == (QG if proj else QG + 2):
                            gated(i, 0)
                        weights_lo(i, s)
                    for head, block_ in ahead(i, s, attend, proj):
                        weights(head, block_)
                    for head, v in projected(i, s, attend, proj):
                        project_lo(head, v)
                    if attend and s < HALVES:
                        values_lo(i, s)

            iterations(dve, step)
            gated(HEADS - 1, 1)


def build_out(nc, c, operands, og_out, x_dram, gain_dram, x_save=None, ident=None,
              zero=None, hT_hi=None, hT_lo=None, latent=None, out_dram=None):
    final = out_dram is not None
    x_sb = c.sb("x", [P, TT, D])
    if final:
        gain = c.sb("gain", [P, D])
        junk_of = c.sb("junk", [P, 1, D])
    else:
        gain = c.sb("gain", [P, KT])
        xn = c.sb("xn", [P, TT, D])
        turned, hT_hi_done, hT_lo_done = (c.sem(n) for n in ("turned", "hT_hi_done",
                                                             "hT_lo_done"))
    operands.second_slot(c)
    w_raw, og_raw, raw_in = operands.w, operands.og, operands.loaded
    w_hi, w_lo = c.sb("w_hi", [P, 2, D], F32R), c.sb("w_lo", [P, 2, D], F32R)
    og_hi, og_lo = c.sb("og_hi", [P, 2, BANK], F32R), c.sb("og_lo", [P, 2, BANK], F32R)
    sq_sum, var, rstd, tmp = (c.sb(n, [P, TT]) for n in ("sq_sum", "var", "rstd", "tmp"))
    y = c.psum("y", [P, QG * 2, BANK])
    (x_in, hi_done, og_lo_done, w_lo_done, mm_done, added, saved, gain_in, squared, var_done,
     root_done, linked, normed) = (
        c.sem(n) for n in ("x_in", "hi_done", "og_lo_done", "w_lo_done", "mm_done", "added",
                           "saved", "gain_in", "squared", "var_done", "root_done", "linked",
                           "normed"))
    BANKS = 2 * QG
    LINKS = 5
    ROW_TILES = ((QG, QG + 2), (QG + 2, TT))

    GROUPS = [(half, kt) for half in range(HALVES) for kt in range(KT)]

    def slot_free(eng, n, half):
        at_least(eng, mm_done, n - 1 + (BANKS - 1 if half and not
                                        (isinstance(n, int) and n == HEADS) else 0))

    def heads(eng, half, work, under=None):
        def pair_of(pair, tile):
            for k in range(2):
                work(pair * 2 + (half * HEADS + k), k, half)
                if tile is not None:
                    under(tile, k)

        if under is None:
            with eng.Fori(1, HEADS // 2 - 1) as pair:
                pair_of(pair, None)
        else:
            with eng.Fori(1, QG + 1) as pair:
                pair_of(pair, pair - 1)
            with eng.Fori(QG + 1, HEADS // 2 - 1) as pair:
                pair_of(pair, None)

    def ends(work, half, last):
        n = half * HEADS + (HEADS - 2 if last else 0)
        for k in range(2):
            work(n + k, k, half)

    with nc.Block() as block:

        @block.sync
        def _(sp):
            def work(n, slot, half):
                h = settled(sp, n - half * HEADS)
                at_least(sp, og_lo_done, n - 1)
                at_least(sp, w_lo_done, n - 1)
                operands.load(sp, h, half, slot)

            def load_x(t):
                sp.dma_start(x_sb[:, bass.ds(t, 1), :].rearrange("p a n -> p (a n)"),
                             x_dram[bass.ds(t * P, P), :]).then_inc(x_in, 16)

            work(1, 1, 0)
            if final:
                sp.dma_start(gain[:], gain_dram.rearrange("(a n) -> a n", a=1)
                             .broadcast_to([P, D])).then_inc(gain_in, 16)
            else:
                sp.dma_start(gain[:], gain_dram.rearrange("(k p) -> p k", p=P),
                             allow_slow_non_contiguous=True).then_inc(gain_in, 16)
            with sp.Fori(1, HEADS // 2 - 1) as pair:
                for k in range(2):
                    work(pair * 2 + k, k, 0)
                load_x(pair - 1)
            for t in range(HEADS // 2 - 2, TT):
                load_x(t)
            for group in range(HALVES):
                sp.wait_ge(og_out[group], 16 * HEADS)
            ends(work, 0, True)
            ends(work, 1, False)
            heads(sp, 1, work)
            ends(work, 1, True)
            if not final:
                for n in range(latent.SLOTS):
                    latent.load(sp, n)
            for t in range(TT):
                if final:
                    sp.wait_ge(normed, t + 1)
                    sp.dma_start(out_dram[t * P:(t + 1) * P, :], x_sb[:, t, :]).then_inc(saved, 16)
                else:
                    sp.wait_ge(added, 2 * t + 2)
                    sp.dma_start(x_save[t * P:(t + 1) * P, :], x_sb[:, t, :]).then_inc(saved, 16)
            if not final:
                for n in range(latent.SLOTS, latent.COUNT):
                    latent.load(sp, n)
            sp.wait_ge(saved, 16 * TT)

        @block.gpsimd
        def _(pool):
            def work(n, slot, half):
                pool.wait_ge(hi_done, 2 * n + 1)
                slot_free(pool, n, half)
                pool.tensor_tensor(w_lo[:, slot, :], w_raw[slot][:],
                                   w_hi[:, slot, :].bitcast(F32), ALU.subtract).then_inc(w_lo_done, 1)

            for half in range(HALVES):
                if half == 0:
                    pool.wait_ge(w_lo_done, 1)
                    work(1, 1, 0)
                else:
                    ends(work, half, False)
                heads(pool, half, work)
                ends(work, half, True)
            if not final:
                for n in range(latent.COUNT):
                    latent.split(pool, n, zero)
                pool.wait_ge(latent.split_done, 2 * latent.COUNT)

        @block.scalar
        def _(act):
            def work(n, slot, half):
                act.wait_ge(raw_in[slot], n * 16 + (32 - slot * 16))
                slot_free(act, n, half)
                act.activation(w_hi[:, slot, :], w_raw[slot][:], ACT.Copy).then_inc(hi_done, 1)
                act.activation(og_hi[:, slot, :], og_raw[slot][:], ACT.Copy).then_inc(hi_done, 1)

            def squares(t):
                return (junk_of[:] if final else xn[:, bass.ds(t, 1), :])\
                    .rearrange("p a n -> p (a n)")

            def square(t):
                act.wait_ge(added, 2 * t + 2)
                if final:
                    act.wait_ge(squared, t)
                act.activation(squares(t), x_sb[:, t, :], ACT.Square,
                               accum_out=sq_sum[:, t:t + 1]).then_inc(squared, 1)

            def under(t, k):
                if k == 0:
                    t = settled(act, t)
                    act.wait_ge(added, BANKS)
                    act.activation(squares(t), x_sb[:, bass.ds(t, 1), :]
                                   .rearrange("p a n -> p (a n)"), ACT.Square,
                                   accum_out=sq_sum[:, bass.ds(t, 1)]).then_inc(squared, 1)
                else:
                    act.wait_ge(var_done, t + 1)
                    act.activation(rstd[:, bass.ds(t, 1)], var[:, bass.ds(t, 1)],
                                   ACT.Sqrt).then_inc(root_done, 1)

            ends(work, 0, False)
            heads(act, 0, work)
            ends(work, 0, True)
            ends(work, 1, False)
            heads(act, 1, work, under)
            ends(work, 1, True)
            for m, (t0, t1) in enumerate(ROW_TILES):
                for t in range(t0, t1):
                    square(t)
                act.wait_ge(var_done, QG + m + 1)
                act.activation(rstd[:, t0:t1], var[:, t0:t1], ACT.Sqrt).then_inc(root_done, 1)
            if not final:
                act.wait_ge(gain_in, 16)
                for n, (half, kt) in enumerate(GROUPS):
                    act.wait_ge(turned, n + 1)
                    act.activation(hT_hi[:, kt, half * BANK:(half + 1) * BANK],
                                   y[:, n % BANKS, :], ACT.Copy,
                                   scale=gain[:, kt:kt + 1]).then_inc(hT_hi_done, 1)

        @block.vector
        def _(dve):
            def work(n, slot, half):
                dve.wait_ge(hi_done, 2 * n + 2)
                slot_free(dve, n, half)
                dve.tensor_tensor(og_lo[:, slot, :], og_raw[slot][:],
                                  og_hi[:, slot, :].bitcast(F32), ALU.subtract).then_inc(og_lo_done, 1)

            def add(half, b):
                for col in range(2):
                    dve.wait_ge(mm_done, (half + 1) * (HEADS - 1) + half * BANKS + 2 * b + col + 1)
                    cols = slice(col * BANK, (col + 1) * BANK)
                    dve.tensor_tensor(x_sb[:, half * QG + b, cols], y[:, 2 * b + col, :],
                                      x_sb[:, half * QG + b, cols], ALU.add).then_inc(added, 1)

            def root(m, cols):
                links = m * LINKS

                def chain(ins, n):
                    ins.then_inc(linked, 1)
                    dve.wait_ge(linked, links + n)

                dve.wait_ge(root_done, m + 1)
                r, w = rstd[:, cols], tmp[:, cols]
                chain(dve.reciprocal(r, r), 1)
                chain(dve.tensor_tensor(w, r, r, ALU.mult), 2)
                chain(dve.tensor_tensor(w, w, var[:, cols], ALU.mult), 3)
                chain(dve.tensor_scalar(w, w, -0.5, 1.5, ALU.mult, ALU.add), 4)
                chain(dve.tensor_tensor(r, r, w, ALU.mult), 5)

            def mean_square(cols):
                dve.tensor_scalar(var[:, cols], sq_sum[:, cols], 1.0 / D, EPS, ALU.mult,
                                  ALU.add).then_inc(var_done, 1)

            def under(t, k):
                t = settled(dve, t)
                if k == 0:
                    dve.wait_ge(squared, t + 1)
                    mean_square(bass.ds(t, 1))
                else:
                    root(t, bass.ds(t, 1))
                    scale(t)

            def scale(t):
                rows = x_sb[:, bass.ds(t, 1), :].rearrange("p a n -> p (a n)")
                if final:
                    dve.scalar_tensor_tensor(rows, rows, rstd[:, bass.ds(t, 1)], gain[:],
                                             ALU.mult, ALU.mult).then_inc(normed, 1)
                else:
                    dve.tensor_scalar(xn[:, bass.ds(t, 1), :].rearrange("p a n -> p (a n)"), rows,
                                      rstd[:, bass.ds(t, 1)], None, ALU.mult).then_inc(normed, 1)

            dve.wait_ge(hi_done, 1)
            dve.tensor_tensor(w_lo[:, 0, :], w_raw[0][:], w_hi[:, 0, :].bitcast(F32),
                              ALU.subtract).then_inc(w_lo_done, 1)
            ends(work, 0, False)
            heads(dve, 0, work)
            ends(work, 0, True)
            work(HEADS, 0, 1)
            dve.wait_ge(x_in, 16 * TT)
            for b in range(QG):
                add(0, b)
            work(HEADS + 1, 1, 1)
            dve.wait_ge(gain_in, 16)
            heads(dve, 1, work, under)
            ends(work, 1, True)
            for m, (t0, t1) in enumerate(ROW_TILES):
                for t in range(t0, t1):
                    add(1, t - QG)
            for m, (t0, t1) in enumerate(ROW_TILES):
                dve.wait_ge(squared, t1)
                mean_square(slice(t0, t1))
                root(QG + m, slice(t0, t1))
                for t in range(t0, t1):
                    scale(t)
            if not final:
                for n, (half, kt) in enumerate(GROUPS):
                    dve.wait_ge(hT_hi_done, n + 1)
                    cols = slice(half * BANK, (half + 1) * BANK)
                    dve.scalar_tensor_tensor(hT_lo[:, kt, cols], y[:, n % BANKS, :],
                                             gain[:, kt:kt + 1], hT_hi[:, kt, cols].bitcast(F32),
                                             ALU.mult, ALU.subtract).then_inc(hT_lo_done, 1)
                dve.wait_ge(hT_lo_done, len(GROUPS))
            dve.wait_ge(normed, TT)

        @block.tensor
        def _(pe):
            def work(n, slot, half):
                pe.wait_ge(og_lo_done, n + 1)
                pe.wait_ge(w_lo_done, n + 1)
                first = isinstance(n, int) and n % HEADS == 0
                last = isinstance(n, int) and n % HEADS == HEADS - 1
                for b in range(QG):
                    for col in range(2):
                        if first and half:
                            pe.wait_ge(added, 2 * b + col + 1)
                        for k, (o, w) in enumerate(products(og_hi, og_lo, w_hi, w_lo)):
                            mm = pe.matmul(y[:, 2 * b + col, :], o[:, slot, b * P:(b + 1) * P],
                                           w[:, slot, col * BANK:(col + 1) * BANK],
                                           start=(first and k == 0), stop=(last and k == 2))
                        if last:
                            mm.then_inc(mm_done, 1)
                if not last:
                    mm.then_inc(mm_done, 1)

            for half in range(HALVES):
                ends(work, half, False)
                heads(pe, half, work)
                ends(work, half, True)
            if not final:
                for n, (half, kt) in enumerate(GROUPS):
                    if half == 0:
                        pe.wait_ge(added, BANKS + n + 1)
                    else:
                        pe.wait_ge(hT_lo_done, n - BANKS + 1)
                    if kt == 0:
                        pe.wait_ge(normed, (half + 1) * QG)
                    for q in range(QG):
                        mm = pe.transpose(y[:, n % BANKS, q * P:(q + 1) * P],
                                          xn[:, half * QG + q, kt * P:(kt + 1) * P], ident[:])
                    mm.then_inc(turned, 1)


def build_latents(nc, c, latent, small, zero, positions, inv_freq, q_norm, kv_norm, w_qb, ident,
                  hT_hi, hT_lo, qn_hi, qn_lo, kvn_hi, kvn_lo, kr_hi, kr_lo, qr_dram):
    GROUPS = 2
    GH = HEADS // GROUPS
    LAT_T = QKT + 1

    wl_hi, wl_lo = latent.hi, latent.lo
    wr_raw = c.sb("wr_raw", [P, HEADS, ROPE])
    wr_hi = c.sb("wr_hi", [P, QKT, HEADS, ROPE], F32R)
    wr_lo = c.sb("wr_lo", [P, QKT, HEADS, ROPE], F32R)
    lat = c.sb("lat", [P, TT, LAT])
    sq_sum, var, rstd, tmp = (c.sb(n, [P, 2 * TT]) for n in ("sq_sum", "var", "rstd", "tmp"))
    gain = c.sb("gain", [P, LAT_T])
    pos_i = c.sb("pos_i", [P, TT], I32)
    pos = c.sb("pos", [P, TT])
    freq = c.sb("freq", [P, HALF_ROPE])
    ang, turns, part = (c.sb(n, [P, TT, HALF_ROPE]) for n in ("ang", "turns", "part"))
    t_hi, t_lo = (c.sb(n, [P, TT, HALF_ROPE], F32R) for n in ("t_hi", "t_lo"))
    cos2, sin2 = (c.sb(n, [P, TT, 2, HALF_ROPE]) for n in ("cos2", "sin2"))
    SLOTS = 3
    qc, qs = (c.sb(n, [P, SLOTS, GH, 2, HALF_ROPE]) for n in ("qc", "qs"))
    OUT_SLOTS = 4
    qr = c.sb("qr", [P, OUT_SLOTS, GH, 2, HALF_ROPE])
    kc, ks = qc[:, 0, :, :, :], qs[:, 0, :, :, :]
    kr = qr[:, 0:2, :, :, :].rearrange("p s h a r -> p (s h a r)")\
        .rearrange("p (t a r) -> p t a r", t=TT, a=2)
    junk = qs[:, 1, :, :, :].rearrange("p h a r -> p (h a r)")
    assert GH == TT
    banks = c.psum("banks", [P, 8, BANK])

    (in_wr, in_small, in_gain, wr_done, mm_done, lat_done, squared,
     var_done, root_done, linked, scaled, angles, trig, turned, hi_done, lo_done, rotated_k,
     q_mm, q_mul, q_rot, pooled) = (c.sem(n) for n in (
         "in_wr", "in_small", "in_gain", "wr_done", "mm_done",
         "lat_done", "squared", "var_done", "root_done", "linked", "scaled", "angles", "trig",
         "turned", "hi_done", "lo_done", "rotated_k", "q_mm", "q_mul", "q_rot", "pooled"))
    q_out = [c.sem(f"q_out{s}") for s in range(OUT_SLOTS)]

    import math
    two_pi = 2.0 * math.pi
    c1 = math.floor(two_pi * 2 ** 9) / 2 ** 9
    c2 = math.floor((two_pi - c1) * 2 ** 21) / 2 ** 21
    c3 = two_pi - c1 - c2
    ROUND = 1.5 * 2 ** 23

    TURNS = [(0, 0), (1, 0), (2, 0), (3, 0), (3, 1), (0, 1), (1, 1), (2, 1)]
    K_TURNS = 5
    UNITS = [(t, g) for t in range(TT) for g in range(GROUPS)]
    ORDER = ([(False, n) for n in range(4)] + [(True, n) for n in range(2)] + [(False, 4)] +
             [(True, n) for n in range(2, 8)] + [(False, n) for n in range(5, 8)] +
             [(True, n) for n in range(8, 16)])
    KEY_BANKS = 4

    def stat(half, kind, b=None):
        c0 = (half * 2 + kind) * QG
        return slice(c0, c0 + QG) if b is None else slice(c0 + b, c0 + b + 1)

    with nc.Block() as block:

        @block.sync
        def _(sp):
            sp.dma_start(pos_i[:], positions.rearrange("b (t p) -> p (b t)", p=P),
                         allow_slow_non_contiguous=True)\
                .then_inc(in_small, 16)
            sp.dma_start(freq[:], inv_freq.broadcast_to([P, HALF_ROPE])).then_inc(in_small, 16)
            sp.dma_start(gain[:, 0:QKT], q_norm.rearrange("(k p) -> p k", p=P),
                         allow_slow_non_contiguous=True).then_inc(in_gain, 16)
            sp.dma_start(gain[:, QKT:LAT_T], kv_norm.rearrange("(k p) -> p k", p=P),
                         allow_slow_non_contiguous=True)\
                .then_inc(in_gain, 16)
            for k in range(QKT):
                at_least(sp, pooled, k)
                src = w_qb[k * P:(k + 1) * P, :].rearrange("p (h n) -> p h n", h=HEADS)
                sp.dma_start(wr_raw[:], src[:, :, NOPE:NOPE + ROPE]).then_inc(in_wr, 16)
            small.load(sp, 0)
            for n, (t, g) in enumerate(UNITS):
                sp.wait_ge(q_rot, 2 * (n + 1))
                sp.dma_start(qr_dram[t * P:(t + 1) * P, g * GH * ROPE:(g + 1) * GH * ROPE],
                             qr[:, n % OUT_SLOTS, :, :, :].rearrange("p h a r -> p (h a r)"))\
                    .then_inc(q_out[n % OUT_SLOTS], 16)
            for s in range(OUT_SLOTS):
                sp.wait_ge(q_out[s], 16 * len(UNITS) // OUT_SLOTS)

        @block.gpsimd
        def _(pool):
            for k in range(QKT):
                pool.wait_ge(wr_done, k + 1)
                pool.tensor_tensor(wr_lo[:, k, :, :], wr_raw[:],
                                   wr_hi[:, k, :, :].bitcast(F32), ALU.subtract).then_inc(pooled, 1)
            small.split(pool, 0, zero)
            pool.wait_ge(turned, K_TURNS)
            for n in range(len(UNITS)):
                pool.wait_ge(q_mul, 2 * (n + 1))
                out, s = n % OUT_SLOTS, n % SLOTS
                if n >= OUT_SLOTS:
                    pool.wait_ge(q_out[out], 16 * (n // OUT_SLOTS))
                pool.tensor_tensor(qr[:, out, :, 0, :], qc[:, s, :, 0, :], qs[:, s, :, 1, :],
                                   ALU.subtract).then_inc(q_rot, 1)
                pool.tensor_tensor(qr[:, out, :, 1, :], qs[:, s, :, 0, :], qc[:, s, :, 1, :],
                                   ALU.add).then_inc(q_rot, 1)

        @block.tensor
        def _(pe):
            for t in range(TT):
                at_least(pe, squared, 2 * (t - KEY_BANKS + 1))
                for kt in range(KT):
                    for n, (h, w) in enumerate(products(hT_hi, hT_lo, wl_hi, wl_lo)):
                        mm = pe.matmul(banks[:, t % KEY_BANKS, 0:LAT], h[:, kt, t * P:(t + 1) * P],
                                       w[:, kt, :], start=(kt == 0 and n == 0),
                                       stop=(kt == KT - 1 and n == 2))
                mm.then_inc(mm_done, 1)

            def turn(n):
                u, half = TURNS[n]
                if n < KEY_BANKS:
                    pe.wait_ge(squared, 2 * (KEY_BANKS + n + 1))
                else:
                    pe.wait_ge(lo_done, n - KEY_BANKS + 1)
                if u < LAT_T:
                    pe.wait_ge(scaled, 2 * QG * (half + 1))
                else:
                    pe.wait_ge(rotated_k, 4 * (half + 1))
                for b in range(QG):
                    t = half * QG + b
                    src = lat[:, t, u * P:(u + 1) * P] if u < LAT_T else \
                        kr[:, t, :, :].rearrange("p a r -> p (a r)")
                    mm = pe.transpose(banks[:, n % KEY_BANKS, b * P:(b + 1) * P], src, ident[:])
                mm.then_inc(turned, 1)

            def unit(n):
                t, g = UNITS[n]
                if n == 0:
                    pe.wait_ge(pooled, QKT)
                pe.wait_ge(lo_done, TURNS.index((QKT - 1, t // QG)) + 1)
                at_least(pe, q_mul, 2 * (n - 3))
                for k in range(QKT):
                    for m, (h, w) in enumerate(products(qn_hi, qn_lo, wr_hi, wr_lo)):
                        mm = pe.matmul(banks[:, KEY_BANKS + n % 4, :], h[:, k, t * P:(t + 1) * P],
                                       w[:, k, g * GH:(g + 1) * GH, :]
                                       .rearrange("p h r -> p (h r)"),
                                       start=(k == 0 and m == 0), stop=(k == QKT - 1 and m == 2))
                mm.then_inc(q_mm, 1)

            for is_unit, n in ORDER:
                (unit if is_unit else turn)(n)

        @block.scalar
        def _(act):
            def roots(half):
                act.wait_ge(var_done, 2 * half + 2)
                cols = slice(half * 2 * QG, (half + 1) * 2 * QG)
                act.activation(rstd[:, cols], var[:, cols], ACT.Sqrt).then_inc(root_done, 1)

            for half in range(HALVES):
                for b in range(QG):
                    t = half * QG + b
                    act.wait_ge(mm_done, t + 1)
                    bank = banks[:, t % KEY_BANKS, :]
                    act.activation(lat[:, t, :], bank[:, 0:LAT], ACT.Copy).then_inc(lat_done, 1)
                    if t:
                        act.wait_ge(squared, 2 * t)
                    act.activation(junk[:, 0:Q_RANK], bank[:, 0:Q_RANK], ACT.Square,
                                   accum_out=sq_sum[:, stat(half, 0, b)]).then_inc(squared, 1)
                    act.wait_ge(squared, 2 * t + 1)
                    act.activation(junk[:, 0:KV_RANK], bank[:, Q_RANK:Q_RANK + KV_RANK],
                                   ACT.Square,
                                   accum_out=sq_sum[:, stat(half, 1, b)]).then_inc(squared, 1)
                if half == 0:
                    act.wait_ge(angles, 2)
                    for a in range(2):
                        act.activation(sin2[:, :, a, :], ang[:], ACT.Sin).then_inc(trig, 1)
                        act.activation(cos2[:, :, a, :], part[:], ACT.Sin).then_inc(trig, 1)
                    roots(0)
            act.wait_ge(in_gain, 32)
            for n, (u, half) in enumerate(TURNS):
                if n == QKT:
                    roots(1)
                act.wait_ge(turned, n + 1)
                cols = slice(half * BANK, (half + 1) * BANK)
                bank = banks[:, n % KEY_BANKS, :]
                if u < QKT:
                    ins = act.activation(qn_hi[:, u, cols], bank, ACT.Copy, scale=gain[:, u:u + 1])
                elif u < LAT_T:
                    ins = act.activation(kvn_hi[:, cols], bank, ACT.Copy, scale=gain[:, u:u + 1])
                else:
                    ins = act.activation(kr_hi[:, cols], bank, ACT.Copy)
                ins.then_inc(hi_done, 1)

        @block.vector
        def _(dve):
            count = [0]

            def chain(ins):
                count[0] += 1
                ins.then_inc(linked, 1)
                dve.wait_ge(linked, count[0])

            def reduce_angle():
                chain(dve.tensor_scalar(turns[:], ang[:], 1.0 / two_pi, ROUND, ALU.mult, ALU.add))
                chain(dve.tensor_scalar(turns[:], turns[:], -ROUND, None, ALU.add))
                chain(dve.tensor_copy(t_hi[:], turns[:]))
                chain(dve.tensor_tensor(t_lo[:], turns[:], t_hi[:].bitcast(F32), ALU.subtract))
                for const in (c1, c2, c3):
                    for t in (t_hi, t_lo):
                        chain(dve.scalar_tensor_tensor(ang[:], t[:].bitcast(F32), -const, ang[:],
                                                       ALU.mult, ALU.add))

            for k in range(QKT):
                dve.wait_ge(in_wr, 16 * (k + 1))
                dve.tensor_copy(wr_hi[:, k, :, :], wr_raw[:]).then_inc(wr_done, 1)
            dve.wait_ge(in_small, 32)
            chain(dve.tensor_copy(pos[:], pos_i[:]))
            chain(dve.tensor_tensor(ang[:], pos[:].unsqueeze(2).broadcast_to([P, TT, HALF_ROPE]),
                                    freq[:].unsqueeze(1).broadcast_to([P, TT, HALF_ROPE]),
                                    ALU.mult))
            reduce_angle()
            reduce_angle()
            chain(dve.tensor_scalar(part[:], ang[:], math.pi / 2, None, ALU.add))
            chain(dve.tensor_scalar(turns[:], part[:], math.pi, -two_pi, ALU.is_gt, ALU.mult))
            chain(dve.tensor_tensor(part[:], part[:], turns[:], ALU.add))
            PI_BELOW = 3.1415925
            dve.tensor_scalar(part[:], part[:], PI_BELOW, -PI_BELOW, ALU.min, ALU.max)\
                .then_inc(angles, 1)
            dve.tensor_scalar(ang[:], ang[:], PI_BELOW, -PI_BELOW, ALU.min, ALU.max)\
                .then_inc(angles, 1)

            def norm(half):
                dve.wait_ge(squared, 2 * QG * (half + 1))
                for kind, rank in enumerate((Q_RANK, KV_RANK)):
                    cols = stat(half, kind)
                    dve.tensor_scalar(var[:, cols], sq_sum[:, cols], 1.0 / rank, EPS, ALU.mult,
                                      ALU.add).then_inc(var_done, 1)
                dve.wait_ge(root_done, half + 1)
                cols = slice(half * 2 * QG, (half + 1) * 2 * QG)
                r, w = rstd[:, cols], tmp[:, cols]
                chain(dve.reciprocal(r, r))
                chain(dve.tensor_tensor(w, r, r, ALU.mult))
                chain(dve.tensor_tensor(w, w, var[:, cols], ALU.mult))
                chain(dve.tensor_scalar(w, w, -0.5, 1.5, ALU.mult, ALU.add))
                chain(dve.tensor_tensor(r, r, w, ALU.mult))
                dve.wait_ge(lat_done, QG * (half + 1))
                for b in range(QG):
                    t = half * QG + b
                    q, kv = lat[:, t, 0:Q_RANK], lat[:, t, Q_RANK:Q_RANK + KV_RANK]
                    dve.tensor_scalar(q, q, rstd[:, stat(half, 0, b)], None,
                                      ALU.mult).then_inc(scaled, 1)
                    dve.tensor_scalar(kv, kv, rstd[:, stat(half, 1, b)], None,
                                      ALU.mult).then_inc(scaled, 1)

            def rotate_key(half):
                ts = slice(half * QG, (half + 1) * QG)
                if half == 0:
                    dve.wait_ge(trig, 4)
                k_x = lat[:, ts, Q_RANK + KV_RANK:LAT].rearrange("p t (a r) -> p t a r", a=2)
                chain(dve.tensor_tensor(kc[:, ts], k_x, cos2[:, ts], ALU.mult))
                chain(dve.tensor_tensor(ks[:, ts], k_x, sin2[:, ts], ALU.mult))
                for a in range(2):
                    dve.tensor_tensor(kr[:, ts, a, 0:HALF_ROPE], kc[:, ts, 0, :], ks[:, ts, 1, :],
                                      ALU.subtract).then_inc(rotated_k, 1)
                    dve.tensor_tensor(kr[:, ts, a, HALF_ROPE:ROPE], ks[:, ts, 0, :],
                                      kc[:, ts, 1, :], ALU.add).then_inc(rotated_k, 1)

            def turn(n):
                u, half = TURNS[n]
                dve.wait_ge(hi_done, n + 1)
                cols = slice(half * BANK, (half + 1) * BANK)
                bank = banks[:, n % KEY_BANKS, :]
                if u < QKT:
                    ins = dve.scalar_tensor_tensor(qn_lo[:, u, cols], bank, gain[:, u:u + 1],
                                                   qn_hi[:, u, cols].bitcast(F32), ALU.mult,
                                                   ALU.subtract)
                elif u < LAT_T:
                    ins = dve.scalar_tensor_tensor(kvn_lo[:, cols], bank, gain[:, u:u + 1],
                                                   kvn_hi[:, cols].bitcast(F32), ALU.mult,
                                                   ALU.subtract)
                else:
                    ins = dve.tensor_tensor(kr_lo[:, cols], bank, kr_hi[:, cols].bitcast(F32),
                                            ALU.subtract)
                ins.then_inc(lo_done, 1)

            def unit(n):
                t, g = UNITS[n]
                s = n % SLOTS
                if n == 0:
                    dve.wait_ge(rotated_k, 8)
                dve.wait_ge(q_mm, n + 1)
                at_least(dve, q_rot, 2 * (n - SLOTS + 1))
                x = banks[:, KEY_BANKS + n % 4, :].rearrange("p (h r) -> p h r", h=GH)
                for out, trig2 in ((qc, cos2), (qs, sin2)):
                    angle = trig2[:, t, :, :].rearrange("p a r -> p (a r)").unsqueeze(1)
                    dve.tensor_tensor(out[:, s, :, :, :].rearrange("p h a r -> p h (a r)"), x,
                                      angle.broadcast_to([P, GH, ROPE]), ALU.mult)\
                       .then_inc(q_mul, 1)

            norm(0)
            rotate_key(0)
            dve.wait_ge(in_gain, 32)
            for is_unit, n in ORDER:
                if not is_unit and n == QKT:
                    norm(1)
                    rotate_key(1)
                (unit if is_unit else turn)(n)
            dve.wait_ge(lo_done, len(TURNS))


def build_mla_heads(nc, c, w_in, ws, w_kvb, ident, zero, hT_hi, hT_lo, qn_hi, qn_lo,
                    kvn_hi, kvn_lo, kr_hi, kr_lo, qr_dram, og, og_out, og_dram, operands):
    CHUNKS = ((0, 3), (3, 3), (6, 2))
    G_PARTS = len(CHUNKS)
    GATE_PART = {1: (0, 0), 2: (0, 1), 3: (0, 2), 4: (1, 0), 5: (1, 1), 6: (1, 2)}
    AHEAD = 2
    ROPE_STACK = 2 * ROPE
    assert ROPE_STACK == P

    wg_raw = c.sb("wg_raw", [P, 3, P])
    wg_hi, wg_lo = c.sb("wg_hi", [P, KT, P], F32R), c.sb("wg_lo", [P, KT, P], F32R)
    ws_hi, ws_lo = ws.hi, ws.lo
    wv_raw = c.sb("wv_raw", [P, HD])
    wv_hi, wv_lo = c.sb("wv_hi", [P, HD], F32R), c.sb("wv_lo", [P, HD], F32R)
    qr_in = c.sb("qr_in", [P, TT, 2, ROPE])
    qr = c.sb("qr", [P, TOK], F32R)
    q_hi, q_lo = c.sb("q_hi", [P, TOK], F32R), c.sb("q_lo", [P, TOK], F32R)
    k_hi, k_lo = c.sb("k_hi", [P, TOK], F32R), c.sb("k_lo", [P, TOK], F32R)
    lt_hi, lt_lo = c.sb("lt_hi", [P, TT, KV_RANK], F32R), c.sb("lt_lo", [P, TT, KV_RANK], F32R)
    u_hi, u_lo = c.sb("u_hi", [P, BANK], F32R), c.sb("u_lo", [P, BANK], F32R)
    gate = c.sb("gate", [P, HALVES, BANK])
    prob = c.sb("prob", [P, 2, TOK])
    pT_hi, pT_lo = c.sb("pT_hi", [P, TT, BANK], F32R), c.sb("pT_lo", [P, TT, BANK], F32R)
    top, neg_top, total, inverse = (c.sb(n, [P, TT]) for n in ("top", "neg_top", "total",
                                                               "inverse"))

    z = c.psum("z", [P, TOK])
    pT = c.psum("pT", [P, TT, P])
    small = c.psum("small", [P, 2, BANK])
    pv = c.psum("pv", [P, BANK])
    g = c.psum("g", [P, BANK])

    (wg_in, wv_in, qr_loaded, w_split, wv_split, g_mm, g_tanh, g_done, small_mm, small_hi,
     small_free, z_done, masked, top_done, neg_done, exp_done, inv_done, p_done, pT_done, pT_hi_done,
     pT_lo_done, mixed, u_hi_done, u_lo_done, pv_done, og_done, lt_turned, lt_hi_done,
     lt_lo_done) = (c.sem(n) for n in (
         "wg_in", "wv_in", "qr_loaded", "w_split", "wv_split", "g_mm", "g_tanh", "g_done",
         "small_mm", "small_hi", "small_free", "z_done", "masked", "top_done", "neg_done", "exp_done",
         "inv_done", "p_done", "pT_done", "pT_hi_done", "pT_lo_done", "mixed",
         "u_hi_done", "u_lo_done", "pv_done", "og_done", "lt_turned", "lt_hi_done",
         "lt_lo_done"))

    w_cols = w_in.rearrange("(k p) n -> p k n", p=P)
    qr_rows = qr_dram.rearrange("(t p) n -> p t n", p=P)

    USES = Q0, R0, K0, K1, Q1, R1 = range(6)
    HALF = {Q0: 0, K0: 0, R0: 0, K1: 1, Q1: 1, R1: 1}
    BEFORE = {6: (K1,)}
    AFTER = {3: (Q0,), 4: (R0,), 5: (K0,), 7: (Q1, R1)}

    def use(i, n):
        return (i + 1) * len(USES) + n + 1

    def ahead(i, s, attend, proj):
        if s + AHEAD < TT:
            return [(i, s + AHEAD)] if attend else []
        return [(i + 1, s + AHEAD - TT)] if proj else []

    def first_bank(s):
        return s % 2 if s < QG else 0

    def blocks_before(i, s):
        return TT * i + (max(s - 1, 0) if s < QG else s)

    def prob_cols(s):
        c0 = BANK if 2 <= s < QG else 0
        return slice(c0, c0 + (s + 1) * P)

    def half_cols(half):
        return slice(half * BANK, (half + 1) * BANK)

    def iterations(eng, step):
        step(-1, False, True)
        step(0, True, True)
        with eng.Fori(1, HEADS - 1) as i:
            step(i, True, True)
        step(HEADS - 1, True, False)

    with nc.Block() as block:

        @block.sync
        def _(sp):
            def load_gate(j, n):
                k0, count = CHUNKS[n]
                at_least(sp, w_split, 2 * (G_PARTS * j + n))
                sp.dma_start(wg_raw[:, 0:count, :],
                             w_cols[:, k0:k0 + count, bass.ds(j * HD + LAT, HD)])\
                    .then_inc(wg_in, 16)

            def load_values(j):
                at_least(sp, wv_split, 2 * j)
                sp.dma_start(wv_raw[:], w_kvb[:, bass.ds(j * (NOPE + HD) + NOPE, HD)])\
                    .then_inc(wv_in, 16)

            def load_rotated(j):
                if not (isinstance(j, int) and j == 0):
                    sp.wait_ge(small_mm, use(j - 2, R1))
                src = qr_rows[:, :, bass.ds(j * ROPE, ROPE)]
                for a in range(2):
                    sp.dma_start(qr_in[:, :, a, :], src).then_inc(qr_loaded, 16)

            def store(i, group):
                i = settled(sp, i)
                sp.wait_ge(og_done, HALVES * i + group + 1)
                dst = og_dram[bass.ds(i, 1), :, half_cols(group)].rearrange("h p n -> (h p) n")
                sp.dma_start(dst, og[:, group, :]).then_inc(og_out[group], 16)

            def load(j, more):
                load_gate(j, 0)
                if not (isinstance(j, int) and j == 0):
                    store(j - 1, 0)
                load_gate(j, 1)
                load_gate(j, 2)
                if more:
                    ws.load(sp, j + 1)
                    load_rotated(j + 1)
                load_values(j)
                if not (isinstance(j, int) and j == 0):
                    store(j - 1, 1)

            load_rotated(0)
            load(0, True)
            with sp.Fori(1, HEADS - 1) as j:
                load(j, True)
            load(HEADS - 1, False)
            sp.wait_ge(og_out[0], 16)
            operands.load(sp, 0, 0, 0)
            store(HEADS - 1, 0)
            store(HEADS - 1, 1)

        @block.gpsimd
        def _(pool):
            def split_small(j):
                pool.wait_ge(small_mm, use(j - 2, Q1))
                ws.split(pool, j, zero)

            def splits(j, more):
                for n, (k0, count) in enumerate(CHUNKS):
                    m = G_PARTS * j + n
                    pool.wait_ge(wg_in, 16 * m + 16)
                    if not (isinstance(j, int) and j == 0):
                        pool.wait_ge(g_mm, HALVES * G_PARTS * (j - 1) + G_PARTS + n + 1)
                    split_on_pool(pool, wg_raw[:, 0:count, :], wg_hi[:, k0:k0 + count, :],
                                  wg_lo[:, k0:k0 + count, :], zero, w_split, m)
                if more:
                    split_small(j + 1)
                pool.wait_ge(wv_in, 16 * j + 16)
                at_least(pool, pv_done, HALVES * j)
                split_on_pool(pool, wv_raw[:], wv_hi[:], wv_lo[:], zero, wv_split, j)

            splits(0, True)
            with pool.Fori(1, HEADS - 1) as j:
                splits(j, True)
            splits(HEADS - 1, False)

        @block.tensor
        def _(pe):
            def small_bank(i, n):
                at_least(pe, small_free, use(i, n) - 2)
                return small[:, n % 2, :]

            def keys(i, half):
                bank = small_bank(i, (K0, K1)[half])
                for m, (w, x) in enumerate(products(ws_hi, ws_lo, kvn_hi, kvn_lo)):
                    mm = pe.matmul(bank, w[:, QKT, :], x[:, half_cols(half)],
                                   start=(m == 0), stop=(m == 2))
                mm.then_inc(small_mm, 1)

            def queries(i, half):
                if half == 0:
                    pe.wait_ge(ws.split_done, 2 * i + 4)
                bank = small_bank(i, (Q0, Q1)[half])
                for k in range(QKT):
                    for m, (w, x) in enumerate(products(ws_hi, ws_lo, qn_hi, qn_lo)):
                        mm = pe.matmul(bank, w[:, k, :], x[:, k, half_cols(half)],
                                       start=(k == 0 and m == 0), stop=(k == QKT - 1 and m == 2))
                mm.then_inc(small_mm, 1)

            def rotated(i, half):
                if half == 0:
                    pe.wait_ge(qr_loaded, 32 * i + 64)
                bank = small_bank(i, (R0, R1)[half])
                for b in range(QG):
                    mm = pe.transpose(bank[:, b * P:(b + 1) * P],
                                      qr_in[:, half * QG + b, :, :].rearrange("p a r -> p (a r)"),
                                      ident[:])
                mm.then_inc(small_mm, 1)

            def gates(i, half, n):
                k0, count = CHUNKS[n]
                if half == 0:
                    pe.wait_ge(w_split, 2 * (G_PARTS * i + n + 1))
                if n == 0:
                    at_least(pe, g_done, HALVES * i + half)
                for kt in range(k0, k0 + count):
                    for k, (w, h) in enumerate(products(wg_hi, wg_lo, hT_hi, hT_lo)):
                        mm = pe.matmul(g[:], w[:, kt, :], h[:, kt, half_cols(half)],
                                       start=(kt == 0 and k == 0), stop=(kt == KT - 1 and k == 2))
                mm.then_inc(g_mm, 1)

            def scores(i, s):
                if isinstance(i, int) and i == 0 and s == 0:
                    pe.wait_ge(lt_lo_done, 1)
                if s % QG == 0:
                    pe.wait_ge(small_free, use(i - 1, (K0, R1)[s // QG]))
                at_least(pe, exp_done, blocks_before(i, s))
                n_keys = (s + 1) * P
                rows = slice(s * P, (s + 1) * P)
                z0 = first_bank(s) * BANK
                for c0 in range(0, n_keys, BANK):
                    width = min(BANK, n_keys - c0)
                    out = z[:, z0 + c0:z0 + c0 + width]
                    pe.matmul(out, qr[:, rows], kr_lo[:, c0:c0 + width], start=True, stop=False)
                    for q, k in products(q_hi, q_lo, k_hi, k_lo):
                        pe.matmul(out, q[:, rows], k[:, c0:c0 + width],
                                  start=False, stop=False)
                    mm = pe.matmul(out, qr[:, rows], kr_hi[:, c0:c0 + width], start=False,
                                   stop=True)
                mm.then_inc(z_done, 1)

            def turn_probs(i, s):
                if isinstance(i, int) and i == 0 and s == 0:
                    pe.wait_ge(lt_hi_done, 1)
                pe.wait_ge(p_done, TT * i + s + 1)
                at_least(pe, pT_lo_done, blocks_before(i, s))
                b0 = first_bank(s) * QG
                c0 = prob_cols(s).start
                for kb in range(s + 1):
                    mm = pe.transpose(pT[:, b0 + kb, :],
                                      prob[:, s % 2, c0 + kb * P:c0 + (kb + 1) * P], ident[:])
                mm.then_inc(pT_done, 1)

            def mix(i, group, first=0, last=QG):
                pe.wait_ge(pT_lo_done, TT * i + QG * group + last)
                at_least(pe, og_done, HALVES * i + group)
                blocks = QG * group + last
                cols = last * P
                for kb in range(blocks):
                    q0 = max(kb - QG * group, first) * P
                    for n, (v, w) in enumerate(products(lt_hi, lt_lo, pT_hi, pT_lo)):
                        mm = pe.matmul(pv[:, q0:cols], v[:, kb, :], w[:, kb, q0:cols],
                                       start=(kb == 0 and n == 0),
                                       stop=(kb == blocks - 1 and n == 2))
                if last == QG:
                    mm.then_inc(mixed, 1)

            def output(i, group):
                if group == 0:
                    pe.wait_ge(wv_split, 2 * i + 2)
                pe.wait_ge(u_lo_done, HALVES * i + group + 1)
                for n, (w, u) in enumerate(products(wv_hi, wv_lo, u_hi, u_lo)):
                    mm = pe.matmul(pv[:], w[:], u[:], start=(n == 0), stop=(n == 2))
                mm.then_inc(pv_done, 1)

            PRODUCT = {Q0: queries, Q1: queries, K0: keys, K1: keys, R0: rotated, R1: rotated}

            def step(i, attend, proj):
                for s in range(TT):
                    first = attend and s == 0
                    if first:
                        scores(i, AHEAD)
                        if not (isinstance(i, int) and i == 0):
                            mix(i - 1, 1)
                    if attend:
                        if s == QG:
                            mix(i, 0)
                        turn_probs(i, s)
                    for n in BEFORE.get(s, ()) if proj else ():
                        PRODUCT[n](i, HALF[n])
                    for head, block_ in ahead(i, s, attend, proj) if not first else ():
                        scores(head, block_)
                    for n in AFTER.get(s, ()) if proj else ():
                        PRODUCT[n](i, HALF[n])
                    if s == QG + 1 and attend:
                        output(i, 0)
                    if attend and s in GATE_PART:
                        gates(i, *GATE_PART[s])
                    if s == 1 and attend and not (isinstance(i, int) and i == 0):
                        output(i - 1, 1)

            for t in range(TT):
                mm = pe.transpose(pT[:, t, :], kvn_hi[:, t * P:(t + 1) * P].bitcast(F32), ident[:])
            mm.then_inc(lt_turned, 1)
            for t in range(TT):
                mm = pe.transpose(z[:, t * P:(t + 1) * P],
                                  kvn_lo[:, t * P:(t + 1) * P].bitcast(F32), ident[:])
            mm.then_inc(lt_turned, 1)
            iterations(pe, step)
            mix(HEADS - 1, 1, 0, QG - 1)
            mix(HEADS - 1, 1, QG - 1, QG)
            output(HEADS - 1, 1)

        @block.scalar
        def _(act):
            def evacuate(i, n):
                act.wait_ge(small_mm, use(i, n))
                half = HALF[n]
                if n in (K0, K1):
                    out = k_hi[:, half_cols(half)]
                elif n in (Q0, Q1):
                    out = q_hi[:, half_cols(half)]
                else:
                    out = qr[:, half_cols(half)]
                act.activation(out, small[:, n % 2, :], ACT.Copy).then_inc(small_hi, 1)

            def exps(i, s):
                n_keys = (s + 1) * P
                z0 = first_bank(s) * BANK
                act.wait_ge(neg_done, TT * i + s + 1)
                at_least(act, pT_done, TT * i + (min(s - 1, 0) if s < QG else s - 1))
                act.activation(prob[:, s % 2, prob_cols(s)], z[:, z0:z0 + n_keys], ACT.Exp,
                               bias=neg_top[:, s:s + 1], scale=MLA_SCALE,
                               accum_out=total[:, s:s + 1]).then_inc(exp_done, 1)

            def probs_hi(i, s):
                act.wait_ge(pT_done, TT * i + s + 1)
                q0 = (s % QG) * P
                b0 = first_bank(s) * QG
                act.activation(pT_hi[:, 0:s + 1, q0:q0 + P], pT[:, b0:b0 + s + 1, :],
                               ACT.Copy).then_inc(pT_hi_done, 1)

            def mixed_hi(i, group):
                act.wait_ge(mixed, HALVES * i + group + 1)
                at_least(act, pv_done, HALVES * i + group)
                act.activation(u_hi[:], pv[:], ACT.Copy).then_inc(u_hi_done, 1)

            def gate_tanh(i, half):
                act.wait_ge(g_mm, G_PARTS * (HALVES * i + half + 1))
                at_least(act, og_done, HALVES * (i - 1) + half + 1)
                act.activation(gate[:, half, :], g[:], ACT.Tanh, scale=0.5).then_inc(g_tanh, 1)

            def step(i, attend, proj):
                for s in range(TT):
                    if attend and s == 0:
                        exps(i, AHEAD)
                        if not (isinstance(i, int) and i == 0):
                            mixed_hi(i - 1, 1)
                    if attend and s == QG:
                        mixed_hi(i, 0)
                    if attend:
                        probs_hi(i, s)
                    if attend and s == TT - 1:
                        gate_tanh(i, 1)
                    for n in BEFORE.get(s, ()) if proj else ():
                        evacuate(i, n)
                    early = s in (QG + 1, TT - 1)
                    for n in AFTER.get(s, ()) if proj and early else ():
                        evacuate(i, n)
                    for head, block_ in ahead(i, s, attend, proj) if s else ():
                        exps(head, block_)
                    for n in AFTER.get(s, ()) if proj and not early else ():
                        evacuate(i, n)
                    if attend and s == QG - 1:
                        gate_tanh(i, 0)

            act.wait_ge(lt_turned, 1)
            act.activation(lt_hi[:], pT[:], ACT.Copy).then_inc(lt_hi_done, 1)
            iterations(act, step)
            mixed_hi(HEADS - 1, 1)

        @block.vector
        def _(dve):
            def evacuate(i, n):
                dve.wait_ge(small_hi, use(i, n))
                half = HALF[n]
                src = small[:, n % 2, :]
                if n in (K0, K1):
                    hi, lo = k_hi[:, half_cols(half)], k_lo[:, half_cols(half)]
                elif n in (Q0, Q1):
                    hi, lo = q_hi[:, half_cols(half)], q_lo[:, half_cols(half)]
                else:
                    hi = lo = qr[ROPE:P, half_cols(half)]
                    src = small[ROPE:P, n % 2, :]
                dve.tensor_tensor(lo, src, hi.bitcast(F32), ALU.subtract).then_inc(small_free, 1)

            def maxima(i, s):
                n_keys = (s + 1) * P
                z0 = first_bank(s) * BANK
                dve.wait_ge(z_done, TT * i + s + 1)
                dve.memset(z[0:CHUNK, z0 + n_keys - CHUNK:z0 + n_keys], NEG).then_inc(masked, 1)
                dve.wait_ge(masked, TT * i + s + 1)
                dve.tensor_reduce(top[:, s:s + 1], z[:, z0:z0 + n_keys], axis=AX_X,
                                  op=ALU.max).then_inc(top_done, 1)
                dve.wait_ge(top_done, TT * i + s + 1)
                dve.tensor_scalar(neg_top[:, s:s + 1], top[:, s:s + 1], -MLA_SCALE, None,
                                  ALU.mult).then_inc(neg_done, 1)

            def normalise(i, s):
                p = prob[:, s % 2, prob_cols(s)]
                dve.wait_ge(exp_done, TT * i + s + 1)
                dve.reciprocal(inverse[:, s:s + 1], total[:, s:s + 1]).then_inc(inv_done, 1)
                dve.wait_ge(inv_done, TT * i + s + 1)
                dve.tensor_scalar(p, p, inverse[:, s:s + 1], None, ALU.mult).then_inc(p_done, 1)

            def probs_lo(i, s):
                q0 = (s % QG) * P
                b0 = first_bank(s) * QG
                dve.wait_ge(pT_hi_done, TT * i + s + 1)
                dve.tensor_tensor(pT_lo[:, 0:s + 1, q0:q0 + P], pT[:, b0:b0 + s + 1, :],
                                  pT_hi[:, 0:s + 1, q0:q0 + P].bitcast(F32),
                                  ALU.subtract).then_inc(pT_lo_done, 1)

            def silu(i, half):
                dve.wait_ge(g_tanh, HALVES * i + half + 1)
                dve.scalar_tensor_tensor(gate[:, half, :], gate[:, half, :], 1.0, g[:], ALU.add,
                                         ALU.mult).then_inc(g_done, 1)

            def mixed_lo(i, group):
                dve.wait_ge(u_hi_done, HALVES * i + group + 1)
                dve.tensor_tensor(u_lo[:], pv[:], u_hi[:].bitcast(F32),
                                  ALU.subtract).then_inc(u_lo_done, 1)

            def gated(i, group):
                dve.wait_ge(pv_done, HALVES * i + group + 1)
                at_least(dve, og_out[group], 16 * i)
                dve.wait_ge(g_done, HALVES * i + group + 1)
                dve.scalar_tensor_tensor(og[:, group, :], pv[:], 0.5, gate[:, group, :], ALU.mult,
                                         ALU.mult).then_inc(og_done, 1)

            def step(i, attend, proj):
                for s in range(TT):
                    before = not (isinstance(i, int) and i <= 0)
                    if attend:
                        if s + 1 < TT:
                            normalise(i, s + 1)
                        if s == QG:
                            silu(i, 0)
                        if s == 0:
                            maxima(i, AHEAD)
                            if before:
                                silu(i - 1, 1)
                                mixed_lo(i - 1, 1)
                        if s == QG:
                            mixed_lo(i, 0)
                        probs_lo(i, s)
                    if proj and s == TT - 1:
                        normalise(i + 1, 0)
                    for n in BEFORE.get(s, ()) if proj else ():
                        evacuate(i, n)
                    for head, block_ in ahead(i, s, attend, proj) if s else ():
                        maxima(head, block_)
                    for n in AFTER.get(s, ()) if proj else ():
                        evacuate(i, n)
                    if attend and s == 1 and before:
                        gated(i - 1, 1)
                    if attend and s == QG + 1:
                        gated(i, 0)

            dve.wait_ge(lt_turned, 2)
            dve.tensor_copy(lt_lo[:].rearrange("p t r -> p (t r)"), z[:]).then_inc(lt_lo_done, 1)
            iterations(dve, step)
            silu(HEADS - 1, 1)
            mixed_lo(HEADS - 1, 1)
            gated(HEADS - 1, 1)


def build(nc, x, positions, ln0, w_in0, w_out0, ln1, w_in1, q_norm1, w_qb1, kv_norm1, w_kvb1,
          w_out1, final_norm, inv_freq, out):
    og_dram = nc.dram_tensor("og_scratch", [HEADS, HD, TOK], F32, kind="Internal").ap()
    x1_dram = nc.dram_tensor("x1_scratch", [TOK, D], F32, kind="Internal").ap()
    qr_dram = nc.dram_tensor("qr_scratch", [TOK, HEADS * ROPE], F32, kind="Internal").ap()
    x_rows = x.rearrange("b t d -> (b t) d")
    out_rows = out.rearrange("b t d -> (b t) d")

    with ExitStack() as whole:
        shared = Chip(nc, whole, "all")
        with ExitStack() as ctx:
            ident, strict, zero = build_constants(nc, Chip(nc, ctx, "const"), shared)

        og = shared.sb("og", [P, HALVES, BANK])
        og_out = [[shared.sem(f"og_out{n}_{half}") for half in range(HALVES)] for n in range(2)]
        slot = (shared.sb("w_raw0", [P, D]), shared.sb("og_raw0", [P, BANK]))
        operands = [OutOperands(shared, n, slot, w, og_dram)
                    for n, w in enumerate((w_out0, w_out1))]

        with ExitStack() as layer:
            h = Chip(nc, layer, "h0")
            hT_hi, hT_lo = h.sb("hT_hi", [P, KT, TOK], F32R), h.sb("hT_lo", [P, KT, TOK], F32R)
            weights = StickWeights(h, w_in0)
            with ExitStack() as ctx:
                build_norm(nc, Chip(nc, ctx, "norm0"), x_rows, ln0, ident, zero, hT_hi, hT_lo,
                           weights)
            with ExitStack() as ctx:
                build_stick_heads(nc, Chip(nc, ctx, "stick"), weights, ident, strict, zero,
                                  hT_hi, hT_lo, og, og_out[0], og_dram, operands[0])

        with ExitStack() as layer:
            h = Chip(nc, layer, "h1")
            hT_hi, hT_lo = h.sb("hT_hi", [P, KT, TOK], F32R), h.sb("hT_lo", [P, KT, TOK], F32R)
            with ExitStack() as until_latents:
                hold = Chip(nc, until_latents, "lat_w")
                with ExitStack() as ctx:
                    c = Chip(nc, ctx, "out0")
                    latent = LatentWeights(hold, c, w_in1)
                    build_out(nc, c, operands[0], og_out[0], x_rows, ln1, x_save=x1_dram,
                              ident=ident, zero=zero, hT_hi=hT_hi, hT_lo=hT_lo, latent=latent)
                qn_hi, qn_lo = (h.sb(n, [P, QKT, TOK], F32R) for n in ("qn_hi", "qn_lo"))
                kvn_hi, kvn_lo = (h.sb(n, [P, TOK], F32R) for n in ("kvn_hi", "kvn_lo"))
                kr_hi, kr_lo = (h.sb(n, [P, TOK], F32R) for n in ("kr_hi", "kr_lo"))
                ws = SmallWeights(h, w_qb1, w_kvb1)
                with ExitStack() as ctx:
                    build_latents(nc, Chip(nc, ctx, "lat"), latent, ws, zero, positions, inv_freq,
                                  q_norm1, kv_norm1, w_qb1, ident, hT_hi, hT_lo, qn_hi, qn_lo,
                                  kvn_hi, kvn_lo, kr_hi, kr_lo, qr_dram)
            with ExitStack() as ctx:
                build_mla_heads(nc, Chip(nc, ctx, "mla"), w_in1, ws, w_kvb1, ident, zero,
                                hT_hi, hT_lo, qn_hi, qn_lo, kvn_hi, kvn_lo, kr_hi,
                                kr_lo, qr_dram, og, og_out[1], og_dram, operands[1])

        with ExitStack() as ctx:
            build_out(nc, Chip(nc, ctx, "out1"), operands[1], og_out[1], x1_dram, final_norm,
                      out_dram=out_rows)


_INS = ["x", "positions", "ln0", "w_in0", "w_out0", "ln1", "w_in1", "q_norm1", "w_qb1",
        "kv_norm1", "w_kvb1", "w_out1", "final_norm"]


def kernel(**inputs):
    import numpy as _np
    import concourse.bacc as _bacc
    from concourse import mybir as _mybir
    from concourse.bass_utils import run_bass_kernel_spmd as _run

    nc = _bacc.Bacc("TRN2", target_bir_lowering=False, num_devices=1)
    arrays = {f"in_{n}_dram": _np.ascontiguousarray(inputs[n]) for n in _INS}
    freq = 10000.0 ** (-_np.arange(0, ROPE, 2, dtype=_np.float64) / ROPE)
    arrays["in_inv_freq_dram"] = freq.astype(_np.float32).reshape(1, HALF_ROPE)
    args = [nc.dram_tensor(n, a.shape, _mybir.dt.from_np(a.dtype), kind="ExternalInput").ap()
            for n, a in arrays.items()]
    out = nc.dram_tensor("out_0_dram", (1, TOK, D), F32, kind="ExternalOutput").ap()
    build(nc, *args, out)
    r = _run(nc, [arrays], core_ids=[0])
    return r.results[0]["out_0_dram"]
```
